# Optimizing a Trainium2 kernel written in Bass

```python
import jax, jax.numpy as jnp
from jax import lax
import numpy as np

D_MODEL = 1024
BATCH = 1
SEQ = 256
DEPTH = 2
DEC_BATCH = 8
DEC_SEQ = 4
PAST_LEN = 2048
PAGE_SIZE = 128

D_MIX = D_MODEL
D_RET = D_MIX // 2
D_CONV = D_MIX - D_RET
N_RET_HEADS = 4
HEAD_DK = D_RET // N_RET_HEADS
HEAD_DV = D_RET // N_RET_HEADS
RET_CHUNK = 128
ROPE_BASE = 10000.0
CONV_WIDTH = 31
N_EXPERTS = 16
N_GROUPS = 4
EXPERTS_PER_GROUP = N_EXPERTS // N_GROUPS
TOP_K = 2
D_FF_EXPERT = D_MODEL
MOE_BLOCK = 128
N_MOD = 6
EPS = 1e-6
D_IN = 4 * D_RET + 2 * D_CONV

kernel_name = "hybrid_retention_conformer_grouped_moe_step"

def rms_norm(x, g):
    xf = x.astype(jnp.float32)
    y = xf * lax.rsqrt(jnp.mean(xf * xf, axis=-1, keepdims=True) + EPS)
    return (y * g.astype(jnp.float32)).astype(x.dtype)

def layer_norm(x, g, b):
    xf = x.astype(jnp.float32)
    mu = jnp.mean(xf, axis=-1, keepdims=True)
    var = jnp.mean(jnp.square(xf - mu), axis=-1, keepdims=True)
    y = (xf - mu) * lax.rsqrt(var + EPS) * g.astype(jnp.float32) + b.astype(jnp.float32)
    return y.astype(x.dtype)

def rotary(x, pos):
    half = x.shape[-1] // 2
    inv = ROPE_BASE ** (-jnp.arange(half, dtype=jnp.float32) / half)
    ang = pos.astype(jnp.float32)[:, None] * inv[None, :]
    cos = jnp.cos(ang)[None, :, None, :]
    sin = jnp.sin(ang)[None, :, None, :]
    xf = x.astype(jnp.float32)
    x1, x2 = xf[..., :half], xf[..., half:]
    return jnp.concatenate([x1 * cos - x2 * sin, x1 * sin + x2 * cos], axis=-1)

def retention(q, k, v, s0):
    B, T, H, _ = q.shape
    dv = v.shape[-1]
    chunk = RET_CHUNK if T % RET_CHUNK == 0 else T
    n = T // chunk
    lg = jnp.log(1.0 - 2.0 ** (-5.0 - jnp.arange(H, dtype=jnp.float32)))
    idx = jnp.arange(chunk, dtype=jnp.float32)
    rel = idx[:, None] - idx[None, :]
    decay = jnp.where(rel[None] >= 0, jnp.exp(jnp.maximum(rel, 0.0)[None] * lg[:, None, None]), 0.0)
    q_decay = jnp.exp((idx[:, None] + 1.0) * lg[None, :])
    k_decay = jnp.exp((chunk - 1.0 - idx[:, None]) * lg[None, :])
    c_decay = jnp.exp(chunk * lg)

    def to_chunks(t):
        return t.reshape(B, n, chunk, H, t.shape[-1]).transpose(1, 0, 2, 3, 4)

    def step(s, inp):
        qc, kc, vc = inp
        scores = jnp.einsum('bihd,bjhd->bhij', qc, kc) * decay[None]
        inner = jnp.einsum('bhij,bjhe->bihe', scores, vc)
        cross = jnp.einsum('bihd,bhde->bihe', qc, s) * q_decay[None, :, :, None]
        s = s * c_decay[None, :, None, None] + jnp.einsum(
            'bjhd,bjhe->bhde', kc * k_decay[None, :, :, None], vc)
        return s, inner + cross

    s_final, o = lax.scan(step, s0, (to_chunks(q), to_chunks(k), to_chunks(v)))
    o = o.transpose(1, 0, 2, 3, 4).reshape(B, T, H, dv)
    return o, s_final

def causal_depthwise_conv(a, buf, w, b):
    full = jnp.concatenate([buf.astype(a.dtype), a], axis=1)
    y = lax.conv_general_dilated(
        full, w[:, None, :].astype(a.dtype), window_strides=(1,), padding='VALID',
        dimension_numbers=('NWC', 'WIO', 'NWC'), feature_group_count=a.shape[-1])
    return y + b.astype(a.dtype), full[:, -(CONV_WIDTH - 1):, :]

def token_mixers(h, pos, ret_state, conv_buf, w_in, w_conv, b_conv, g_conv_ln, b_conv_ln, g_ret_gn):
    B, T, _ = h.shape
    proj = h @ w_in
    q, k, v, g, u, z = jnp.split(
        proj, [D_RET, 2 * D_RET, 3 * D_RET, 4 * D_RET, 4 * D_RET + D_CONV], axis=-1)
    q = rotary(q.reshape(B, T, N_RET_HEADS, HEAD_DK), pos)
    k = rotary(k.reshape(B, T, N_RET_HEADS, HEAD_DK), pos) * (HEAD_DK ** -0.5)
    v = v.reshape(B, T, N_RET_HEADS, HEAD_DV).astype(jnp.float32)
    o, s_new = retention(q, k, v, ret_state.astype(jnp.float32))
    mu = jnp.mean(o, axis=-1, keepdims=True)
    var = jnp.mean(jnp.square(o - mu), axis=-1, keepdims=True)
    o = ((o - mu) * lax.rsqrt(var + EPS)).reshape(B, T, D_RET) * g_ret_gn.astype(jnp.float32)
    ret_out = (jax.nn.silu(g.astype(jnp.float32)) * o).astype(h.dtype)
    a = u * jax.nn.sigmoid(z)
    cv, buf_new = causal_depthwise_conv(a, conv_buf, w_conv, b_conv)
    conv_out = jax.nn.silu(layer_norm(cv, g_conv_ln, b_conv_ln))
    return jnp.concatenate([ret_out, conv_out], axis=-1), s_new, buf_new

def grouped_moe(h, w_router, b_router, w_gate, w_up, w_down):
    N, D = h.shape
    logits = h.astype(jnp.float32) @ w_router.astype(jnp.float32) + b_router.astype(jnp.float32)
    probs = jax.nn.softmax(logits, axis=-1)
    pg = probs.reshape(N, N_GROUPS, EXPERTS_PER_GROUP)
    group_score = lax.top_k(pg, TOP_K)[0].sum(-1)
    g_sel = jnp.argmax(group_score, axis=-1)
    cand = jnp.take_along_axis(
        pg, jnp.broadcast_to(g_sel[:, None, None], (N, 1, EXPERTS_PER_GROUP)), axis=1)[:, 0]
    wts, local = lax.top_k(cand, TOP_K)
    wts = wts / jnp.sum(wts, axis=-1, keepdims=True)
    e_idx = g_sel[:, None] * EXPERTS_PER_GROUP + local

    n_assign = N * TOP_K
    flat_e = e_idx.reshape(-1)
    counts = jnp.bincount(flat_e, length=N_EXPERTS)
    padded = ((counts + MOE_BLOCK - 1) // MOE_BLOCK) * MOE_BLOCK
    pad_end = jnp.cumsum(padded)
    pad_start = pad_end - padded
    start = jnp.cumsum(counts) - counts
    order = jnp.argsort(flat_e)
    sorted_e = flat_e[order]
    dest = pad_start[sorted_e] + (jnp.arange(n_assign) - start[sorted_e])
    n_blocks = -(-n_assign // MOE_BLOCK) + N_EXPERTS
    cap = n_blocks * MOE_BLOCK
    slot_tok = jnp.full((cap,), N, jnp.int32).at[dest].set((order // TOP_K).astype(jnp.int32))
    slot_w = jnp.zeros((cap,), jnp.float32).at[dest].set(wts.reshape(-1)[order])
    block_e = jnp.minimum(
        jnp.searchsorted(pad_end, jnp.arange(n_blocks) * MOE_BLOCK, side='right'), N_EXPERTS - 1)
    h_pad = jnp.concatenate([h, jnp.zeros((1, D), h.dtype)], axis=0)
    xs = h_pad[slot_tok].reshape(n_blocks, MOE_BLOCK, D)

    def block_ffn(args):
        xb, e = args
        return (jax.nn.silu(xb @ w_gate[e]) * (xb @ w_up[e])) @ w_down[e]

    ys = lax.map(block_ffn, (xs, block_e)).reshape(cap, D)
    ys = (ys * slot_w[:, None]).astype(h.dtype)
    return jnp.zeros((N + 1, D), h.dtype).at[slot_tok].add(ys)[:N]

def trunk(x, c, pos, ret_states, conv_bufs, w_mod, b_mod, g_mix_norm, w_in, w_conv, b_conv,
          g_conv_ln, b_conv_ln, g_ret_gn, w_out, g_ffn_norm, w_router, b_router,
          w_exp_gate, w_exp_up, w_exp_down, g_final):
    B, T, D = x.shape
    cond = jax.nn.silu(c)
    new_ret, new_conv = [], []
    for l in range(DEPTH):
        mod = (cond @ w_mod[l] + b_mod[l])[:, None, :]
        sh1, sc1, gt1, sh2, sc2, gt2 = jnp.split(mod, N_MOD, axis=-1)
        h = rms_norm(x, g_mix_norm[l]) * (1 + sc1) + sh1
        mix, s_new, buf_new = token_mixers(h, pos, ret_states[l], conv_bufs[l], w_in[l], w_conv[l],
                                           b_conv[l], g_conv_ln[l], b_conv_ln[l], g_ret_gn[l])
        x = x + gt1 * (mix @ w_out[l])
        h = rms_norm(x, g_ffn_norm[l]) * (1 + sc2) + sh2
        ff = grouped_moe(h.reshape(B * T, D), w_router, b_router,
                         w_exp_gate[l], w_exp_up[l], w_exp_down[l]).reshape(B, T, D)
        x = x + gt2 * ff
        new_ret.append(s_new)
        new_conv.append(buf_new)
    return rms_norm(x, g_final), jnp.stack(new_ret), jnp.stack(new_conv)

def setup_inputs(seed: int = 0) -> dict:
    key = jax.random.key(seed)
    ks = jax.random.split(key, 24)
    L, D, E, F = DEPTH, D_MODEL, N_EXPERTS, D_FF_EXPERT

    def nrm(k, shape, s):
        return jax.random.normal(k, shape, jnp.float32) * s

    return {
        "x_prompt": nrm(ks[0], (BATCH, SEQ, D), 1.0),
        "x_sample": nrm(ks[1], (DEC_BATCH, DEC_SEQ, D), 1.0),
        "state_ret": nrm(ks[2], (L, DEC_BATCH, N_RET_HEADS, HEAD_DK, HEAD_DV), 0.5),
        "state_conv": nrm(ks[3], (L, DEC_BATCH, CONV_WIDTH - 1, D_CONV), 0.5),
        "c_prompt": nrm(ks[4], (BATCH, D), 1.0),
        "c_sample": nrm(ks[5], (DEC_BATCH, D), 1.0),
        "w_mod": nrm(ks[6], (L, D, N_MOD * D), 0.5 * D ** -0.5),
        "b_mod": nrm(ks[7], (L, N_MOD * D), 0.02),
        "g_mix_norm": 1.0 + nrm(ks[8], (L, D), 0.02),
        "w_in": nrm(ks[9], (L, D, D_IN), D ** -0.5),
        "w_conv": nrm(ks[10], (L, CONV_WIDTH, D_CONV), CONV_WIDTH ** -0.5),
        "b_conv": nrm(ks[11], (L, D_CONV), 0.02),
        "g_conv_ln": 1.0 + nrm(ks[12], (L, D_CONV), 0.02),
        "b_conv_ln": nrm(ks[13], (L, D_CONV), 0.02),
        "g_ret_gn": 1.0 + nrm(ks[14], (L, D_RET), 0.02),
        "w_out": nrm(ks[15], (L, D_MIX, D), D_MIX ** -0.5),
        "g_ffn_norm": 1.0 + nrm(ks[16], (L, D), 0.02),
        "w_router": nrm(ks[17], (D, E), D ** -0.5),
        "b_router": nrm(ks[18], (E,), 0.01),
        "w_exp_gate": nrm(ks[19], (L, E, D, F), D ** -0.5),
        "w_exp_up": nrm(ks[20], (L, E, D, F), D ** -0.5),
        "w_exp_down": nrm(ks[21], (L, E, F, D), F ** -0.5),
        "g_final": 1.0 + nrm(ks[22], (D,), 0.02),
    }

def reference(x_prompt, x_sample, state_ret, state_conv, c_prompt, c_sample, w_mod, b_mod,
              g_mix_norm, w_in, w_conv, b_conv, g_conv_ln, b_conv_ln, g_ret_gn, w_out,
              g_ffn_norm, w_router, b_router, w_exp_gate, w_exp_up, w_exp_down, g_final):
    weights = (w_mod, b_mod, g_mix_norm, w_in, w_conv, b_conv, g_conv_ln, b_conv_ln, g_ret_gn,
               w_out, g_ffn_norm, w_router, b_router, w_exp_gate, w_exp_up, w_exp_down, g_final)
    bp = x_prompt.shape[0]
    zero_ret = jnp.zeros((DEPTH, bp, N_RET_HEADS, HEAD_DK, HEAD_DV), jnp.float32)
    zero_conv = jnp.zeros((DEPTH, bp, CONV_WIDTH - 1, D_CONV), x_prompt.dtype)
    pos_prompt = jnp.arange(x_prompt.shape[1], dtype=jnp.int32)
    pos_sample = PAST_LEN + jnp.arange(x_sample.shape[1], dtype=jnp.int32)
    y_prompt, ret_p, conv_p = trunk(x_prompt, c_prompt, pos_prompt, zero_ret, zero_conv, *weights)
    y_sample, ret_s, conv_s = trunk(x_sample, c_sample, pos_sample, state_ret, state_conv, *weights)
    return (y_prompt, y_sample, ret_p, conv_p, ret_s, conv_s)


_drawn_inputs = setup_inputs


def setup_inputs(seed=0):
    import zlib

    import numpy as np

    out = dict(_drawn_inputs(seed))
    spreads = {}
    factors = {'g_conv_ln': 3.086,
     'b_conv_ln': 3.09,
     'g_ret_gn': 4.585,
     'g_final': 7.989,
     'b_router': 2.68}
    for name, (base, spread) in spreads.items():
        noise = np.random.default_rng([zlib.crc32(name.encode()), seed]).standard_normal(out[name].shape)
        drawn = base * np.exp(spread * noise) if base else spread * noise
        out[name] = __import__('jax').numpy.asarray(drawn.astype(out[name].dtype))
    for name, factor in factors.items():
        out[name] = (out[name] * factor).astype(out[name].dtype)
    return out
```

```python
import math
from contextlib import ExitStack

import numpy as np

import concourse.bass as bass
from concourse import mybir

L, D, SEQ, B, T_DEC = 2, 1024, 256, 8, 4
NS = B * T_DEC
T = SEQ + NS
P = 128
KC = D // P
TILES = [(0, P), (P, P), (2 * P, NS)]
H, DH = 4, 128
D_RET, D_CONV = 512, 512
CT = D_CONV // P
TAPS, HIST = 31, 30
PAST = 2048
E, GROUPS, EPG = 16, 4, 4
BLK = 64
MAXSUB = -(-T // BLK)
MAXEXTRA = 2 * T // BLK - 1
YROWS = (16 + MAXEXTRA) * BLK
NC = 1 + B
NMOD = 6
EPS = 1e-6
NSLOT = 12
UK = 2
UQ = KC // UK
FRING = HIST + SEQ
SRING = HIST + T_DEC

R_GMIX, R_GFFN, R_BMOD, R_BCONV, R_GCLN, R_BCLN, R_GRET, R_GFIN, NROWS = 0, 8, 16, 64, 68, 72, 76, 80, 88
M_SH1, M_SC1, M_GT1, M_SH2, M_SC2, M_GT2 = 0, 8, 16, 24, 32, 40
NMB = NMOD * KC

LG = [math.log(1.0 - 2.0 ** (-5.0 - h)) for h in range(H)]
CDEC_P = [math.exp(P * g) for g in LG]
CDEC_S = [math.exp(T_DEC * g) for g in LG]

CONST = [("ident", 128), ("tri", 128), ("ones", 128), ("fold", 2 * NC), ("decay", 4 * 128), ("sdecay", 4 * NS),
         ("cos", T), ("sin", T), ("qdec", 4 * (P + NS)), ("kdec", 12), ("smask", B), ("iota", BLK),
         ("erow", E), ("xrow", E), ("ekey", E), ("gkey", GROUPS), ("valid", 3)]
COFF, _o = {}, 0
for _n, _w in CONST:
    COFF[_n] = (_o, _w)
    _o += _w
NCONST = _o


def constants():
    c = {}
    i = np.arange(P)
    c["ident"] = np.eye(P)
    c["tri"] = (i[:, None] < i[None, :]).astype(float)
    c["ones"] = np.ones((P, P))
    fold = np.zeros((P, 2, NC))
    for r in range(P):
        if r % 32 < NC:
            fold[r, (r // 32) % 2, r % 32] = 1.0
    c["fold"] = fold.reshape(P, -1)
    scale = DH ** -0.5
    rel = i[None, :] - i[:, None]
    c["decay"] = np.stack([np.where(rel >= 0, np.exp(np.maximum(rel, 0) * g), 0.0) * scale for g in LG], 1).reshape(P, -1)
    s = np.arange(NS)
    srel = s[None, :] - s[:, None]
    same = (s[None, :] // T_DEC == s[:, None] // T_DEC) & (srel >= 0)
    sd = np.zeros((P, 4, NS))
    for h, g in enumerate(LG):
        sd[:NS, h] = np.where(same, np.exp(np.maximum(srel, 0) * g), 0.0) * scale
    c["sdecay"] = sd.reshape(P, -1)
    half = DH // 2
    inv = (np.float32(10000.0) ** (-np.arange(half, dtype=np.float32) / np.float32(half))).astype(np.float32)
    pos = np.concatenate([np.arange(SEQ), PAST + s % T_DEC]).astype(np.float32)
    ang = (pos[None, :] * inv[:, None]).astype(np.float32).astype(np.float64)
    c["cos"] = np.concatenate([np.cos(ang), np.cos(ang)], 0)
    c["sin"] = np.concatenate([np.sin(ang), -np.sin(ang)], 0)
    qi = np.concatenate([np.arange(P) + 1, s % T_DEC + 1])
    c["qdec"] = np.broadcast_to(np.stack([np.exp(qi * g) for g in LG]).reshape(1, -1), (P, 4 * (P + NS)))
    kd = np.zeros((P, 3, 4))
    for h, g in enumerate(LG):
        kd[:, 0, h] = kd[:, 1, h] = np.exp((P - 1 - i) * g) * scale
        kd[:NS, 2, h] = np.exp((T_DEC - 1 - s % T_DEC) * g) * scale
    c["kdec"] = kd.reshape(P, -1)
    sm = np.zeros((P, B))
    sm[s, s // T_DEC] = 1.0
    c["smask"] = sm
    c["iota"] = np.broadcast_to(np.arange(BLK), (P, BLK))
    c["erow"] = np.broadcast_to(np.arange(E) * BLK, (P, E))
    c["xrow"] = np.broadcast_to(E * BLK - BLK - np.arange(E) * BLK, (P, E))
    c["ekey"] = np.broadcast_to(E - np.arange(E), (P, E))
    c["gkey"] = np.broadcast_to(GROUPS - np.arange(GROUPS), (P, GROUPS))
    v = np.ones((P, 3))
    v[NS:, 2] = 0.0
    c["valid"] = v
    return np.ascontiguousarray(np.concatenate([c[n] for n, _ in CONST], 1).astype(np.float32))


class Chain:

    def __init__(self, eng, sem):
        self.eng, self.sem, self.n = eng, sem, 0

    def link(self, ins):
        ins.then_inc(self.sem, 1)
        self.n += 1
        self.eng.wait_ge(self.sem, self.n)


def hybrid_step_kernel(nc, x_prompt, x_sample, state_ret, state_conv, c_prompt, c_sample, w_mod, b_mod, g_mix_norm,
                       w_in, w_conv, b_conv, g_conv_ln, b_conv_ln, g_ret_gn, w_out, g_ffn_norm, w_router, b_router,
                       w_exp_gate, w_exp_up, w_exp_down, g_final, consts,
                       y_prompt, y_sample, ret_p, conv_p, ret_s, conv_s):
    f32, i32, u32 = mybir.dt.float32, mybir.dt.int32, mybir.dt.uint32
    ALU, ACT, AX = mybir.AluOpType, mybir.ActivationFunctionType, mybir.AxisListType
    ctx = ExitStack()
    with ctx:
        def sb(name, shape, dt=f32):
            return ctx.enter_context(nc.sbuf_tensor(name, shape, dt))

        ring = sb("ring", [P, NSLOT, UK, D])
        xT = sb("xT", [P, KC, T])
        hT = sb("hT", [P, KC, T])
        big = sb("big", [P, KC, T])
        cst = sb("cst", [P, NCONST])
        vecT = sb("vecT", [P, L, NROWS])
        wcT = sb("wcT", [P, L, TAPS * CT])
        modT = sb("modT", [P, L, NMB, NC])
        vec = sb("vec", [P, NROWS])
        wc = sb("wc", [P, TAPS * CT])
        mod = sb("mod", [P, NMB, NC])
        wr = sb("wr", [P, KC, E])
        brow = sb("brow", [P, E])
        condT = sb("condT", [P, KC, 32])
        stat = sb("stat", [P, 3, T])
        rt = sb("rt", [P, 16, 3 * E])
        posm = sb("posm", [P, 3, E + 1])
        wts = sb("wts", [P, 2, 3])
        rowi = sb("rowi", [P, 2, 3], u32)
        nsubi = sb("nsubi", [P, E], i32)
        posx = sb("posx", [P, 3])
        rtmp = sb("rtmp", [P, KC, NS])
        ARENA = 14976
        arena = sb("arena", [P, ARENA])
        ps = ctx.enter_context(nc.psum_tensor("ps", [P, 8, 512], f32))

        def C(name):
            o, w = COFF[name]
            return cst[:, o:o + w]

        ident = C("ident")
        ones = C("ones")
        used = {}

        def cut(phase, *dims):
            n = int(np.prod(dims))
            o = used.get(phase, 0)
            used[phase] = o + n
            assert o + n <= ARENA, (phase, o + n)
            v = arena[:, o:o + n]
            if len(dims) == 2:
                v = v.rearrange("p (a b) -> p a b", a=dims[0])
            elif len(dims) == 3:
                v = v.rearrange("p (a b c) -> p a b c", a=dims[0], b=dims[1])
            return v

        x_tok = cut("setup", 3, D)
        c_tok = cut("setup", D)
        c_sig = cut("setup", D)
        vrows = cut("setup", L, P)
        wcrows = cut("setup", L, P)
        modS = cut("setup", 3, 512)
        proj = cut("mix", 16, T)
        full = cut("mix", KC * T)
        fullv = full[:, 0:CT * (FRING + B * SRING)].rearrange("p (c w) -> p c w", c=CT)
        cT = cut("mix", CT, T)
        kd = cut("mix", 3, 512)
        vt = cut("mix", 3, 512)
        sc = cut("mix", 2, 512)
        scs = cut("mix", H * NS)
        s1 = cut("mix", 512)
        sf = cut("mix", 512)
        qd = cut("mix", H, P + NS)
        vmask = cut("mix", D)
        cpsum = kd[:, 2, 0:CT * NS]
        cprod = vmask
        cbt = kd[:, 0:2, :]
        zsig = vt[:, 0:2, 0:T]
        atok = sc
        lnsq = full[:, 0:CT * T].rearrange("p (c t) -> p c t", c=CT)
        gsig = full[:, CT * T:2 * CT * T].rearrange("p (c t) -> p c t", c=CT)
        oS = proj[:, 8:12, :]
        S_a = big[:, :, :].rearrange("p a b -> p (a b)")[:, 0:2 * B * DH]
        S_b = proj[:, 0:8, :].rearrange("p a b -> p (a b)")[:, 0:2 * B * DH]
        gn_sq, gn_rstd = gsig, lnsq
        S_h = [S_a[:, 0:B * DH], S_a[:, B * DH:], S_b[:, 0:B * DH], S_b[:, B * DH:]]
        h2tok = cut("moe", 3, D)
        yg = cut("moe", 2, D)
        hxs = yg.rearrange("p a b -> p (a b)")
        xg = cut("moe", 2, KC * BLK)
        sel = cut("moe", 2, 3 * BLK)
        gs = cut("moe", 512)
        hs = cut("moe", 512)
        h2T = cut("moe", 512)
        ysb = cut("moe", 2, 512)
        xgx = cut("moe", 512)
        gsx = cut("moe", 512)
        hx = cut("moe", 512)
        h2x = cut("moe", 512)
        yx = cut("moe", 512)
        selx = cut("moe", 3 * BLK)

        SUM_BANK, VAR_BANK, OUT_BANK = (6, 3, 6, 3), (7, 2, 7, 2), (4, 5, 6, 3)

        ydram = nc.dram_tensor("expert_rows", (YROWS, D), f32, kind="Internal").ap()

        def sem(name):
            return ctx.enter_context(nc.semaphore(name))

        loaded = [sem(f"unit_loaded{s}") for s in range(NSLOT)]
        freed = [sem(f"unit_freed{s}") for s in range(NSLOT)]
        in_const, in_x, in_c, in_rows, in_wr = (sem(n) for n in ("in_const", "in_x", "in_c", "in_rows", "in_wr"))
        (rows_zeroed, zeros_set, cpad, c_sigd, c_act, c_trans, cond_ready, x_trans, x_copied, rows_trans, rows_copied, mod_done, mod_evac,
         fold_done, mod_added) = (sem(n) for n in (
             "rows_zeroed", "zeros_set", "cpad", "c_sigd", "c_act", "c_trans", "cond_ready", "x_trans", "x_copied", "rows_trans", "rows_copied",
             "mod_done", "mod_evac", "fold_done", "mod_added"))
        layer_open, y_out, fin_sq, fin_sum, fin_rs, fin_y, fin_tr, fin_cp = (sem(n) for n in (
            "layer_open", "y_out", "fin_sq", "fin_sum", "fin_rs", "fin_y", "fin_tr", "fin_cp"))
        tick = sem("tick")
        layer_done = sem("layer_done")
        names = """var_ready rstd_ready vectors_ready norm_sq norm_sum h_ready cb_loaded cb_trans cb_copied pad_ready
        inproj_done z_sig a_ready proj_copied conv_ready sconv_ready a_trans atok_copied atok_stored hist_stored rot_ready
        qd_ready ln_sum ln_centered ln_sq ln_var ln_scaled ln_sig mix_conv score_done sc_ready v_trans v_copied
        k_trans kd_ready g_sig st_done s1_copied sf_ready sf_stored Sa_loaded Sb_loaded vmask_ready snew_done
        snew_ready Sa_stored Sb_stored o_done o_copied gn_sum gn_centered gn_sq gn_var gn_mixed outproj_done x_mid
        norm2_sq norm2_sum h2_ready h2_trans h2_copied logits_done lg_ready ex_ready m_ready pos_done route_ready
        dchain pchain sel_ready gathered xg_copied gate_done up_done sig_done gated h_act trans_done hT_copied
        down_done y_copied y_stored0 y_stored1 x_sel x_gath x_xg x_gu x_sig x_gated x_h x_t x_hs x_h2 x_down x_yc x_st
        y_all gath0 gath1 comb_ready yt_trans x_end""".split()
        S = {n: sem(n) for n in names}
        nums = [layer_done.num] + [S[n].num for n in names]
        assert nums == list(range(nums[0], nums[0] + len(nums)))
        layer_sems = range(nums[0], nums[-1] + 1)
        V = type("Signals", (), S)
        y_stored = [V.y_stored0, V.y_stored1]
        block = ctx.enter_context(nc.Block())

        SETUP_USES = L * NMOD * UQ // NSLOT
        PRE = [1 if s < 8 else 2 for s in range(NSLOT)]
        PER_LAYER = [p + E for p in PRE]

        FREE0 = 1

        def unit_uses(s, l, k):
            return l * PER_LAYER[s] + (SETUP_USES + k + FREE0)

        @block.sync
        def _(sp):
            mod_v = w_mod.rearrange("l (q k p) c -> l q p k c", q=UQ, p=P)
            in_v = w_in.rearrange("l (q k p) c -> l q p k c", q=UQ, p=P)
            out_v = w_out.rearrange("l (q k p) c -> l q p k c", q=UQ, p=P)
            exp_v = [w.rearrange("l e (q k p) c -> (l e) q p k c", q=UQ, p=P) for w in (w_exp_gate, w_exp_up, w_exp_down)]
            with sp.Fori(0, L) as l:
                with sp.Fori(0, 2) as hf:
                    for j in range(3):
                        for q in range(UQ):
                            s = j * UQ + q
                            sp.wait_ge(freed[s], l * 2 + hf + 1)
                            sp.sem_inc(tick, 1)
                            sp.dma_start(ring[:, s], mod_v[bass.ds(l, 1), q, :, :, bass.ds(hf * (3 * D) + j * D, D)]
                                         .rearrange("a p k c -> (a p) k c")).then_inc(loaded[s], 16)
            with sp.Fori(0, L) as l:
                for j, slab in enumerate((2, 0, 1)):
                    for q in range(UQ):
                        s = j * UQ + q
                        sp.wait_ge(freed[s], unit_uses(s, l, 0))
                        sp.sem_inc(tick, 1)
                        sp.dma_start(ring[:, s], in_v[bass.ds(l, 1), q, :, :, slab * D:(slab + 1) * D]
                                     .rearrange("a p k c -> (a p) k c")).then_inc(loaded[s], 16)
                for q in range(UQ):
                    s = 2 * UQ + q
                    sp.wait_ge(freed[s], unit_uses(s, l, 1))
                    sp.sem_inc(tick, 1)
                    sp.dma_start(ring[:, s], out_v[bass.ds(l, 1), q].rearrange("a p k c -> (a p) k c")).then_inc(loaded[s], 16)
                with sp.Fori(0, E) as e:
                    for j in range(3):
                        for q in range(UQ):
                            s = j * UQ + q
                            sp.wait_ge(freed[s], l * PER_LAYER[s] + e + (SETUP_USES + PRE[s] + FREE0))
                            sp.sem_inc(tick, 1)
                            sp.dma_start(ring[:, s], exp_v[j][bass.ds(l * E + e, 1), q]
                                         .rearrange("a p k c -> (a p) k c")).then_inc(loaded[s], 16)
            yp = y_prompt[0].rearrange("(r p) d -> p r d", p=P)
            sp.wait_ge(fin_cp, 6)
            sp.dma_start(yp, x_tok[:, 0:2, :]).then_inc(y_out, 16)
            sp.dma_start(y_sample.rearrange("b t d -> (b t) d"), x_tok[0:NS, 2, :]).then_inc(y_out, 16)
            sp.wait_ge(y_out, 32)

        @block.tensor
        def _(pe):
            def mm(out, lhsT, rhs, start, stop):
                return nc.tensor.matmul(out, lhsT, rhs, start=start, stop=stop, skip_group_check=True)

            def tr(out, in_, n):
                return nc.tensor.transpose(out, in_, ident[0:n, 0:n])

            for s in range(NSLOT):
                pe.sem_inc(freed[s], 1)
            pe.wait_ge(in_const, 16)
            pe.wait_ge(in_rows, 16 * 2 * 9)
            for l in range(L):
                tr(ps[:, 0, l * P:l * P + NROWS], vrows[0:NROWS, l, :], NROWS)
                last = tr(ps[:, 1, l * P:l * P + TAPS * CT], wcrows[0:TAPS * CT, l, :], TAPS * CT)
            last.then_inc(rows_trans, 1)
            pe.wait_ge(c_act, 1)
            for k in range(KC):
                last = tr(ps[:, 2, k * 16:k * 16 + NC], c_tok[0:NC, k * P:(k + 1) * P], NC)
            last.then_inc(c_trans, 1)
            pe.wait_ge(in_x, 48)
            for k in range(KC):
                if k >= 2:
                    pe.wait_ge(x_copied, k - 1)
                for t0, n in TILES:
                    last = tr(ps[:, 6 + k % 2, t0:t0 + n], x_tok[0:n, t0 // P, k * P:(k + 1) * P], n)
                last.then_inc(x_trans, 1)
            pe.wait_ge(cond_ready, 1)
            pe.wait_ge(rows_copied, 2)
            pe.sem_inc(fold_done, 3)
            with pe.Fori(0, 4) as r:
                for j in range(3):
                    pe.wait_ge(mod_evac, r * 3 + j + 1)
                    for q in range(UQ):
                        s = j * UQ + q
                        pe.wait_ge(loaded[s], r * 16 + 16)
                        for kk in range(UK):
                            for nh in range(2):
                                t = 32 * (kk * 2 + nh)
                                last = mm(ps[t:t + 32, j, :], condT[:, q * UK + kk, :], ring[:, s, kk, nh * 512:nh * 512 + 512],
                                          q == 0, q == UQ - 1)
                        last.then_inc(freed[s], 1)
                    pe.drain().then_inc(mod_done, 1)
                    pe.wait_ge(mod_evac, r * 3 + j + 4)
                    pe.wait_ge(mod_added, r * 3 + j + 1)
                    for m in range(4):
                        last = mm(ps[:, 3 + j, m * 2 * NC:(m + 1) * 2 * NC], modS[:, j, m * P:(m + 1) * P], C("fold"), True, True)
                    last.then_inc(fold_done, 1)
            pe.wait_ge(mod_added, 3 + 12)
            pe.wait_ge(x_copied, KC)
            pe.wait_ge(in_wr, 32)

            def feature_sum(bank, src, n, width=T):
                for k in range(n):
                    last = mm(ps[:, bank, 0:width], ones, src[:, k, :], k == 0, k == n - 1)
                return last

            with pe.Fori(0, L) as l:
                pe.wait_ge(V.cb_loaded, 16)
                for ct in range(CT):
                    for r in range(2):
                        last = tr(ps[:, 4 + ct // 2, (ct % 2) * 240 + r * 120:(ct % 2) * 240 + r * 120 + 120],
                                  cbt[0:120, r, ct * P:(ct + 1) * P], 120)
                    last.then_inc(V.cb_trans, 1)
                pe.wait_ge(V.norm_sq, 1)
                feature_sum(6, big, KC).then_inc(V.norm_sum, 1)
                pe.wait_ge(V.h_ready, 1)
                n = 0
                for j, cols in enumerate(([0, 4, 1, 5, 2, 6, 3, 7], range(8), range(8))):
                    for q in range(UQ):
                        s = j * UQ + q
                        pe.wait_ge(loaded[s], l * (16 * PER_LAYER[s]) + 16 * (SETUP_USES + 1))
                    for m in cols:
                        if n >= 4:
                            if n - 4 >= 8:
                                pe.wait_ge(V.proj_copied, n - 4 - 8 + 1)
                            elif n % 2 == 0:
                                pe.wait_ge(V.a_ready, (n - 4) // 2 + 1)
                            else:
                                pe.wait_ge(V.z_sig, (n - 4) // 2 + 1)
                        for k in range(KC):
                            last = mm(ps[:, n % 4, 0:T], ring[:, j * UQ + k // UK, k % UK, m * P:(m + 1) * P], hT[:, k, :],
                                      k == 0, k == KC - 1)
                        last.then_inc(V.inproj_done, 1)
                        n += 1
                    pe.wait_ge(V.inproj_done, n)
                    for q in range(UQ):
                        pe.sem_inc(freed[j * UQ + q], 1)
                    if j == 1:
                        pe.wait_ge(V.a_ready, 4)
                        pe.wait_ge(V.cb_copied, 4)
                        for ct in range(CT):
                            tr(ps[0:HIST, 4, ct * P:(ct + 1) * P], fullv[:, ct, FRING - HIST:FRING], P)
                        for ct in range(CT):
                            last = tr(ps[0:NS, 5, ct * P:(ct + 1) * P], rtmp[:, ct, :], P)
                        last.then_inc(V.a_trans, 1)
                for t, bank in enumerate((3, 7, 2)):
                    t0, m = TILES[t]
                    pe.wait_ge(V.proj_copied, 16)
                    for h in range(H):
                        last = tr(ps[0:m, bank, h * P:(h + 1) * P], proj[:, 8 + h, t0:t0 + m], P)
                    last.then_inc(V.v_trans, 1)
                pe.wait_ge(V.conv_ready, 1)
                pe.wait_ge(V.sconv_ready, 1)
                feature_sum(6, cT, CT).then_inc(V.ln_sum, 1)
                pe.wait_ge(V.rot_ready, 1)
                pe.wait_ge(V.atok_copied, 2)
                for c in range(2):
                    for h in range(H):
                        last = mm(ps[:, 4 + c, h * P:(h + 1) * P], proj[:, 4 + h, c * P:(c + 1) * P], proj[:, h, c * P:(c + 1) * P],
                                  True, True)
                    last.then_inc(V.score_done, 1)
                for h in range(H):
                    last = mm(ps[0:NS, 0, h * NS:(h + 1) * NS], proj[:, 4 + h, SEQ:T], proj[:, h, SEQ:T], True, True)
                last.then_inc(V.score_done, 1)
                pe.wait_ge(V.ln_centered, 1)
                pe.wait_ge(V.sc_ready, 3)
                for t, bank in enumerate((0, 1, 6)):
                    t0, m = TILES[t]
                    for h in range(H):
                        last = tr(ps[0:m, bank, h * P:(h + 1) * P], proj[:, 4 + h, t0:t0 + m], P)
                    last.then_inc(V.k_trans, 1)
                pe.wait_ge(V.v_copied, 3)
                for c, bank in enumerate((3, 7)):
                    pe.wait_ge(V.kd_ready, c + 1)
                    for h in range(H):
                        last = mm(ps[:, bank, h * P:(h + 1) * P], kd[:, c, h * P:(h + 1) * P], vt[:, c, h * P:(h + 1) * P], True, True)
                    last.then_inc(V.st_done, 1)
                pe.wait_ge(V.ln_sq, 1)
                feature_sum(2, lnsq, CT).then_inc(V.ln_var, 1)
                pe.wait_ge(V.s1_copied, 1)
                pe.wait_ge(V.kd_ready, 3)
                pe.wait_ge(V.sf_ready, 1)
                pe.wait_ge(V.qd_ready, 1)

                def head_output(h):
                    bank = 4 + h % 2
                    if h >= 2:
                        pe.wait_ge(V.o_copied, h - 1)
                    hp = slice(h * P, (h + 1) * P)
                    mm(ps[:, bank, 0:P], vt[:, 0, hp], sc[:, 0, hp], True, False)
                    mm(ps[:, bank, P:2 * P], vt[:, 1, hp], sc[:, 1, hp], False, False)
                    mm(ps[:, bank, P:2 * P], s1[:, hp], qd[:, h, 0:P], False, False)
                    mm(ps[:, bank, SEQ:T], vt[0:NS, 2, hp], scs[0:NS, h * NS:(h + 1) * NS], False, False)
                    pe.wait_ge(V.Sa_loaded if h < 2 else V.Sb_loaded, 32)
                    for b in range(B):
                        last = mm(ps[:, bank, SEQ + b * T_DEC:SEQ + (b + 1) * T_DEC], S_h[h][:, b * P:(b + 1) * P],
                                  qd[:, h, P + b * T_DEC:P + (b + 1) * T_DEC], False, b == B - 1)
                    last.then_inc(V.o_done, 1)

                def head_states(h):
                    hp = slice(h * P, (h + 1) * P)
                    pe.wait_ge(V.vmask_ready, h + 1)
                    if h >= 1:
                        pe.wait_ge(V.snew_ready, h)
                    for g in range(2):
                        last = mm(ps[:, g, :], kd[0:NS, 2, hp], vmask[0:NS, g * 512:(g + 1) * 512], True, True)
                    last.then_inc(V.snew_done, 1)

                def head_sum(h):
                    pe.wait_ge(V.o_copied, h + 1)
                    if h >= 2:
                        pe.wait_ge(V.gn_centered, h - 1)
                    mm(ps[:, SUM_BANK[h], 0:T], ones, oS[:, h, :], True, True).then_inc(V.gn_sum, 1)

                def head_squares(h):
                    pe.wait_ge(V.gn_sq, h + 1)
                    if h >= 1:
                        pe.wait_ge(V.var_ready, h + 1)
                    mm(ps[:, VAR_BANK[h], 0:T], ones, gn_sq[:, h, :], True, True).then_inc(V.gn_var, 1)

                def out_block(m, ks):
                    for k in ks:
                        last = mm(ps[:, OUT_BANK[m % 4], 0:T], ring[:, 2 * UQ + k // UK, k % UK, m * P:(m + 1) * P], hT[:, k, :],
                                  k == KC // 2, k == KC // 2 - 1)
                    return last

                CONV_K, RET_K = range(KC // 2, KC), range(0, KC // 2)
                head_output(0)
                head_output(1)
                head_states(0)
                head_sum(0)
                head_output(2)
                head_sum(1)
                head_states(1)
                head_squares(0)
                head_output(3)
                head_sum(2)
                head_states(2)
                head_squares(1)
                head_sum(3)
                for q in range(UQ):
                    s = 2 * UQ + q
                    pe.wait_ge(loaded[s], l * (16 * PER_LAYER[s]) + 16 * (SETUP_USES + 2))
                pe.wait_ge(V.mix_conv, 1)
                head_squares(2)
                out_block(0, CONV_K)
                head_squares(3)
                head_states(3)
                out_block(1, CONV_K)
                pe.wait_ge(V.gn_centered, H)
                out_block(2, CONV_K)
                out_block(3, CONV_K)
                for m in range(4):
                    for k in RET_K:
                        if m == 0:
                            pe.wait_ge(V.gn_mixed, k + 1)
                        last = out_block(m, [k])
                    last.then_inc(V.outproj_done, 1)
                for m in range(4, KC):
                    pe.wait_ge(V.x_mid, m - 3)
                    out_block(m, CONV_K)
                    out_block(m, RET_K).then_inc(V.outproj_done, 1)
                pe.wait_ge(V.outproj_done, KC)
                for q in range(UQ):
                    pe.sem_inc(freed[2 * UQ + q], 1)
                pe.wait_ge(V.norm2_sq, 1)
                feature_sum(6, big, KC).then_inc(V.norm2_sum, 1)
                pe.wait_ge(V.h2_ready, 1)
                for t, (t0, m) in enumerate(TILES):
                    for k in range(KC):
                        last = mm(ps[0:m, 4, t * E:(t + 1) * E], hT[:, k, t0:t0 + m], wr[:, k, :], k == 0, k == KC - 1)
                last.then_inc(V.logits_done, 1)
                n = 0
                for t, (t0, m) in enumerate(TILES):
                    for hf in range(2):
                        if n >= 4:
                            pe.wait_ge(V.h2_copied, n - 3)
                        for k in range(4):
                            last = tr(ps[0:m, n % 4, k * P:(k + 1) * P], hT[:, hf * 4 + k, t0:t0 + m], P)
                        last.then_inc(V.h2_trans, 1)
                        n += 1
                pe.wait_ge(V.m_ready, 1)
                M = rt[:, 10, :]
                for t in range(3):
                    for u in range(t + 1):
                        mm(ps[:, 5, t * E:(t + 1) * E], C("tri") if u == t else ones, M[:, u * E:(u + 1) * E], u == 0, u == t)
                for u in range(3):
                    last = mm(ps[:, 5, 3 * E:4 * E], ones, M[:, u * E:(u + 1) * E], u == 0, u == 2)
                last.then_inc(V.pos_done, 1)

                pe.wait_ge(V.route_ready, 1)
                pe.wait_ge(V.h2_copied, 6)
                for sgn in (V.gathered, V.up_done, V.trans_done, V.down_done):
                    pe.sem_inc(sgn, 2)
                for sgn in (V.x_gath, V.x_gu, V.x_t, V.x_down):
                    pe.sem_inc(sgn, 1)

                def gather(selb, bank):
                    for k in range(KC):
                        for t, (t0, m) in enumerate(TILES):
                            last = mm(ps[:, bank, k * BLK:(k + 1) * BLK], h2tok[0:m, t, k * P:(k + 1) * P],
                                      selb[0:m, t * BLK:(t + 1) * BLK], t == 0, t == 2)
                    return last

                def half_products(bank, lhs, s0, free):
                    for k in range(KC):
                        s = s0 + k // UK
                        for nh in range(2):
                            last = mm(ps[nh * 64:nh * 64 + 64, bank, :], lhs(k), ring[:, s, k % UK, nh * 512:nh * 512 + 512],
                                      k == 0, k == KC - 1)
                        if free and k % UK == UK - 1 and k < KC - 1:
                            last.then_inc(freed[s], 1)
                    return last

                def transposes(bank, src):
                    for j in range(4):
                        last = tr(ps[:, bank, j * P:(j + 1) * P], src[:, j * P:(j + 1) * P], P)
                    return last

                def down_lhs(src):
                    return lambda k: src[:, (k % 4) * P + (k // 4) * BLK:(k % 4) * P + (k // 4) * BLK + BLK]

                pe.wait_ge(V.sel_ready, 1)
                gather(sel[:, 0, :], 1).then_inc(V.gathered, 1)
                xn = pe.alloc_register("extra_blocks")
                pe.reg_mov(xn, 1)
                with pe.Fori(0, E // 2) as g:
                    for i in range(2):
                        def units(j):
                            for q in range(UQ):
                                s = j * UQ + q
                                pe.wait_ge(loaded[s], l * (16 * PER_LAYER[s]) + g * 32 + 16 * (SETUP_USES + PRE[s] + i + 1))
                        nsub = pe.value_load(nsubi[0:1, bass.ds(g * 2 + i, 1)], min_val=1, max_val=MAXSUB)
                        xlo = pe.alloc_register(f"extra_first{i}")
                        pe.reg_mov(xlo, xn)
                        with pe.If(nsub > 1):
                            units(0)
                            units(1)
                            pe.sem_inc(tick, 1)
                            with pe.Fori(1, nsub):
                                pe.wait_ge(V.x_hs, xn)
                                pe.reg_add(xn, xn, 1)
                                pe.wait_ge(V.x_sel, xn)
                                gather(selx, 7).then_inc(V.x_gath, 1)
                                pe.wait_ge(V.x_xg, xn)
                                half_products(5, lambda k: xgx[:, k * BLK:(k + 1) * BLK], 0, False)
                                half_products(6, lambda k: xgx[:, k * BLK:(k + 1) * BLK], UQ, False).then_inc(V.x_gu, 1)
                                pe.wait_ge(V.x_h, xn)
                                transposes(7, hx).then_inc(V.x_t, 1)
                            pe.wait_ge(V.x_hs, xn)
                            pe.sem_inc(tick, 1)
                        units(0)
                        pe.wait_ge(V.xg_copied, g * 2 + i + 1)
                        pe.wait_ge(V.h_act, g * 2 + i + 2)
                        last = half_products(2, lambda k: xg[:, i, k * BLK:(k + 1) * BLK], 0, True)
                        last.then_inc(V.gate_done, 1)
                        units(1)
                        last = half_products(3, lambda k: xg[:, i, k * BLK:(k + 1) * BLK], UQ, True)
                        last.then_inc(V.up_done, 1)
                        pe.wait_ge(V.sel_ready, g * 2 + i + 2)
                        pe.wait_ge(V.xg_copied, g * 2 + i + 1)
                        gather(sel[:, (i + 1) % 2, :], 1).then_inc(V.gathered, 1)
                        pe.wait_ge(V.up_done, g * 2 + i + 3)
                        pe.sem_inc(freed[UQ - 1], 1)
                        pe.sem_inc(freed[2 * UQ - 1], 1)
                        pe.wait_ge(V.h_act, g * 2 + i + 3)
                        pe.wait_ge(V.hT_copied, g * 2 + i + 2)
                        transposes(4, hs).then_inc(V.trans_done, 1)
                        with pe.If(nsub > 1):
                            units(2)
                            pe.sem_inc(tick, 1)
                            with pe.Fori(1, nsub):
                                pe.wait_ge(V.x_yc, xlo)
                                pe.reg_add(xlo, xlo, 1)
                                pe.wait_ge(V.x_h2, xlo)
                                half_products(7, down_lhs(h2x), 2 * UQ, False).then_inc(V.x_down, 1)
                            pe.wait_ge(V.x_yc, xn)
                            pe.sem_inc(tick, 1)
                        units(2)
                        pe.wait_ge(V.hT_copied, g * 2 + i + 3)
                        pe.wait_ge(V.y_copied, g * 2 + i + 2)
                        half_products(0, down_lhs(h2T), 2 * UQ, True).then_inc(V.down_done, 1)
                        pe.wait_ge(V.down_done, g * 2 + i + 3)
                        pe.sem_inc(freed[3 * UQ - 1], 1)
                pe.wait_ge(V.comb_ready, 3)
                for k in range(KC):
                    if k >= 2:
                        pe.wait_ge(V.x_end, k - 1)
                    for t, (t0, m) in enumerate(TILES):
                        last = tr(ps[:, 2 + k % 2, t0:t0 + m], h2tok[0:m, t, k * P:(k + 1) * P], m)
                    last.then_inc(V.yt_trans, 1)
                pe.drain().then_inc(layer_done, 1)
                pe.wait_ge(layer_open, l + 1)
            pe.wait_ge(fin_sq, 1)
            feature_sum(6, big, KC).then_inc(fin_sum, 1)
            pe.wait_ge(fin_y, 1)
            n = 0
            for t, (t0, m) in enumerate(TILES):
                for hf in range(2):
                    if n >= 4:
                        pe.wait_ge(fin_cp, n - 3)
                    for k in range(4):
                        last = tr(ps[0:m, n % 4, k * P:(k + 1) * P], hT[:, hf * 4 + k, t0:t0 + m], P)
                    last.then_inc(fin_tr, 1)
                    n += 1

        @block.scalar
        def _(act):
            def a(out, in_, f=ACT.Copy, **kw):
                return nc.scalar.activation(out, in_, f, **kw)

            def root(buf):
                a(buf, buf, ACT.Sqrt).then_inc(V.rstd_ready, 1)

            act.dma_start(cst[:, :], consts).then_inc(in_const, 16)
            act.dma_start(x_tok[:, 0:2, :], x_prompt[0].rearrange("(r p) d -> p r d", p=P)).then_inc(in_x, 16)
            act.dma_start(x_tok[0:NS, 2, :], x_sample.rearrange("b t d -> (b t) d")).then_inc(in_x, 32)
            act.dma_start(c_tok[0:1, :], c_prompt).then_inc(in_c, 16)
            act.dma_start(c_tok[1:NC, :], c_sample).then_inc(in_c, 16)
            for l in range(L):
                for row, n, src in ((R_GMIX, 8, g_mix_norm[l]), (R_GFFN, 8, g_ffn_norm[l]), (R_BMOD, NMB, b_mod[l]),
                                    (R_BCONV, 4, b_conv[l]), (R_GCLN, 4, g_conv_ln[l]), (R_BCLN, 4, b_conv_ln[l]),
                                    (R_GRET, 4, g_ret_gn[l]), (R_GFIN, 8, g_final)):
                    act.dma_start(vrows[row:row + n, l, :], src.rearrange("(r p) -> r p", p=P)).then_inc(in_rows, 16)
                act.dma_start(wcrows[0:TAPS * CT, l, :], w_conv[l].rearrange("t (c p) -> (t c) p", p=P)).then_inc(in_rows, 16)
            act.dma_start(wr[:, :, :], w_router.rearrange("(k p) e -> p k e", p=P)).then_inc(in_wr, 16)
            act.dma_start(brow[:, :], b_router.partition_broadcast(P)).then_inc(in_wr, 16)
            act.wait_ge(in_c, 32)
            a(c_sig[0:NC, :], c_tok[0:NC, :], ACT.Sigmoid).then_inc(c_sigd, 1)
            act.wait_ge(c_trans, 1)
            act.wait_ge(cpad, 1)
            a(condT[:, :, 0:NC], ps[:, 2, 0:KC * 16].rearrange("p (k c) -> p k c", k=KC)[:, :, 0:NC]).then_inc(cond_ready, 1)
            for k in range(0, KC):
                act.wait_ge(x_trans, k + 1)
                a(xT[:, k, :], ps[:, 6 + k % 2, 0:T]).then_inc(x_copied, 1)
            act.sem_inc(mod_evac, 3)
            with act.Fori(0, 4) as r:
                for j in range(3):
                    act.wait_ge(mod_done, r * 3 + j + 1)
                    act.wait_ge(fold_done, r * 3 + j + 1)
                    a(modS[:, j, :], ps[:, j, :]).then_inc(mod_evac, 1)
            act.wait_ge(mod_added, 3 + 12)
            act.wait_ge(rows_zeroed, 32)

            with act.Fori(0, L) as l:
                a(big[:, :, :], xT[:, :, :], ACT.Square).then_inc(V.norm_sq, 1)
                act.wait_ge(V.pad_ready, 1)
                for ct in range(CT):
                    act.wait_ge(V.cb_trans, ct // 2 * 2 + 2)
                    a(fullv[:, ct, FRING:].rearrange("p (b w) -> p b w", b=B)[:, :, 0:HIST],
                      ps[:, 4 + ct // 2, (ct % 2) * 240:(ct % 2) * 240 + 240].rearrange("p (b w) -> p b w", b=B)) \
                        .then_inc(V.cb_copied, 1)
                act.wait_ge(V.var_ready, 1)
                root(stat[:, 1, :])
                for i in range(4):
                    act.wait_ge(V.inproj_done, 2 * i + 2)
                    if i >= 2:
                        act.wait_ge(V.a_ready, i - 1)
                    a(zsig[:, i % 2, :], ps[:, (2 * i + 1) % 4, 0:T], ACT.Sigmoid).then_inc(V.z_sig, 1)
                for n in range(16):
                    act.wait_ge(V.inproj_done, 8 + n + 1)
                    a(proj[:, n, :], ps[:, n % 4, 0:T]).then_inc(V.proj_copied, 1)
                    if n == 11:
                        act.wait_ge(V.a_trans, 1)
                        a(atok[0:HIST, 0, :], ps[0:HIST, 4, :]).then_inc(V.atok_copied, 1)
                        a(atok[0:NS, 1, :], ps[0:NS, 5, :]).then_inc(V.atok_copied, 1)
                for t, bank in enumerate((3, 7, 2)):
                    m = TILES[t][1]
                    act.wait_ge(V.v_trans, t + 1)
                    a(vt[0:m, t, :], ps[0:m, bank, :]).then_inc(V.v_copied, 1)
                act.wait_ge(V.ln_centered, 1)
                act.wait_ge(V.sconv_ready, 1)
                act.wait_ge(V.a_trans, 1)
                a(lnsq, cT, ACT.Square).then_inc(V.ln_sq, 1)
                act.wait_ge(V.proj_copied, 16)
                a(gsig, proj[:, 12:16, :], ACT.Sigmoid).then_inc(V.g_sig, 1)
                act.wait_ge(V.st_done, 1)
                a(s1, ps[:, 3, :]).then_inc(V.s1_copied, 1)
                act.wait_ge(V.var_ready, 2)
                root(stat[:, 1, :])
                act.wait_ge(V.ln_scaled, 1)
                act.wait_ge(V.ln_var, 1)
                for ct in range(CT):
                    last = a(lnsq[:, ct, :], cT[:, ct, :], ACT.Sigmoid, scale=vec[:, R_GCLN + ct:R_GCLN + ct + 1],
                             bias=vec[:, R_BCLN + ct:R_BCLN + ct + 1])
                last.then_inc(V.ln_sig, 1)

                def copy_head(h):
                    act.wait_ge(V.o_done, h + 1)
                    a(oS[:, h, :], ps[:, 4 + h % 2, 0:T]).then_inc(V.o_copied, 1)

                def square_head(h):
                    act.wait_ge(V.gn_centered, h + 1)
                    a(gn_sq[:, h, :], oS[:, h, :], ACT.Square).then_inc(V.gn_sq, 1)

                def root_head(h):
                    act.wait_ge(V.var_ready, 3 + h)
                    root(gn_rstd[:, h, :])

                act.wait_ge(V.mix_conv, 1)
                copy_head(0)
                copy_head(1)
                square_head(0)
                copy_head(2)
                square_head(1)
                root_head(0)
                copy_head(3)
                square_head(2)
                root_head(1)
                square_head(3)
                root_head(2)
                root_head(3)
                act.wait_ge(V.x_mid, KC + 1)
                act.wait_ge(V.Sa_stored, 32)
                a(big[:, :, :], xT[:, :, :], ACT.Square).then_inc(V.norm2_sq, 1)
                act.wait_ge(V.var_ready, 3 + H)
                root(stat[:, 1, :])
                act.wait_ge(V.Sb_stored, 32)
                n = 0
                for t, (t0, m) in enumerate(TILES):
                    for hf in range(2):
                        act.wait_ge(V.h2_trans, n + 1)
                        a(h2tok[0:m, t, hf * 512:hf * 512 + 512], ps[0:m, n % 4, :]).then_inc(V.h2_copied, 1)
                        n += 1
                act.wait_ge(V.lg_ready, 1)
                a(rt[:, 1, :], rt[:, 0, :], ACT.Exp).then_inc(V.ex_ready, 1)

                act.wait_ge(V.route_ready, 1)
                act.wait_ge(V.sf_stored, 16)
                act.sem_inc(V.y_copied, 2)
                for sgn in y_stored:
                    act.sem_inc(sgn, 16)
                for sgn in (V.x_sig, V.x_yc):
                    act.sem_inc(sgn, 1)
                act.wait_ge(V.gathered, 3)
                a(xg[:, 0, :], ps[:, 1, :]).then_inc(V.xg_copied, 1)
                xn = act.alloc_register("extra_blocks")
                act.reg_mov(xn, 1)
                x16 = act.alloc_register("extra_stored")
                act.reg_mov(x16, 0)
                with act.Fori(0, E // 2) as g:
                    for i in range(2):
                        nsub = act.value_load(nsubi[0:1, bass.ds(g * 2 + i, 1)], min_val=1, max_val=MAXSUB)
                        xlo = act.alloc_register(f"extra_first{i}")
                        act.reg_mov(xlo, xn)
                        with act.If(nsub > 1):
                            with act.Fori(1, nsub):
                                act.reg_add(xn, xn, 1)
                                act.wait_ge(V.x_gu, xn)
                                a(gsx, ps[:, 5, :], ACT.Sigmoid).then_inc(V.x_sig, 1)
                        act.wait_ge(V.gate_done, g * 2 + i + 1)
                        act.wait_ge(V.h_act, g * 2 + i + 2)
                        a(gs, ps[:, 2, :], ACT.Sigmoid).then_inc(V.sig_done, 1)
                        act.wait_ge(V.gathered, g * 2 + i + 4)
                        act.wait_ge(V.up_done, g * 2 + i + 2)
                        a(xg[:, (i + 1) % 2, :], ps[:, 1, :]).then_inc(V.xg_copied, 1)
                        with act.If(nsub > 1):
                            with act.Fori(1, nsub) as s:
                                act.reg_add(xlo, xlo, 1)
                                act.wait_ge(V.x_down, xlo)
                                a(yx, ps[:, 7, :]).then_inc(V.x_yc, 1)
                                act.wait_ge(V.x_yc, xlo)
                                row = act.snap(act.snap(xlo) * BLK + (E - 2) * BLK, min_val=0, max_val=YROWS - BLK)
                                for hf in range(2):
                                    act.dma_start(ydram[bass.ds(row, BLK), hf * 512:hf * 512 + 512],
                                                  yx[hf * 64:hf * 64 + 64, :]).then_inc(V.x_st, 16)
                                act.reg_add(x16, x16, 32)
                                act.wait_ge(V.x_st, x16)
                                act.sem_inc(tick, 1)
                        act.wait_ge(V.down_done, g * 2 + i + 3)
                        act.wait_ge(y_stored[i], g * 32 + 16)
                        a(ysb[:, i, :], ps[:, 0, :]).then_inc(V.y_copied, 1)
                        act.wait_ge(V.y_copied, g * 2 + i + 3)
                        for hf in range(2):
                            act.dma_start(ydram[bass.ds(g * (2 * BLK) + i * BLK, BLK), hf * 512:hf * 512 + 512],
                                          ysb[hf * 64:hf * 64 + 64, i, :]).then_inc(y_stored[i], 16)
                act.drain().then_inc(layer_done, 1)
                act.wait_ge(layer_open, l + 1)
            a(big[:, :, :], xT[:, :, :], ACT.Square).then_inc(fin_sq, 1)
            act.wait_ge(fin_rs, 2)
            a(stat[:, 1, :], stat[:, 1, :], ACT.Sqrt).then_inc(fin_rs, 1)
            n = 0
            for t, (t0, m) in enumerate(TILES):
                for hf in range(2):
                    act.wait_ge(fin_tr, n + 1)
                    a(x_tok[0:m, t, hf * 512:hf * 512 + 512], ps[0:m, n % 4, :]).then_inc(fin_cp, 1)
                    n += 1

        @block.vector
        def _(dve):
            v = nc.vector

            def bc(ap2, n):
                return ap2.unsqueeze(1).to_broadcast([ap2.shape[0], n, ap2.shape[1]])

            def bl(ap2, n):
                return ap2.unsqueeze(2).to_broadcast([ap2.shape[0], ap2.shape[1], n])

            v.memset(condT[:, :, :], 0.0).then_inc(cpad, 1)
            dve.wait_ge(c_sigd, 1)
            v.tensor_tensor(c_tok[0:NC, :], c_tok[0:NC, :], c_sig[0:NC, :], ALU.mult).then_inc(c_act, 1)
            dve.wait_ge(rows_trans, 1)
            v.tensor_copy(vecT[:, :, :], ps[:, 0, 0:L * P].rearrange("p (l r) -> p l r", l=L)[:, :, 0:NROWS]).then_inc(rows_copied, 1)
            v.tensor_copy(wcT[:, :, :], ps[:, 1, 0:L * P].rearrange("p (l r) -> p l r", l=L)[:, :, 0:TAPS * CT]).then_inc(rows_copied, 1)
            dve.wait_ge(rows_copied, 2)
            dve.sem_inc(mod_added, 3)
            with dve.Fori(0, L) as l:
                with dve.Fori(0, 2) as hf:
                    for j in range(3):
                        dve.wait_ge(fold_done, l * 6 + hf * 3 + j + 4)
                        blk = hf * (3 * KC) + j * KC
                        o = modT[:, bass.ds(l, 1), bass.ds(blk, KC), :].rearrange("p a (n m) c -> p (a n) m c", n=2)
                        bm = vecT[:, bass.ds(l, 1), bass.ds(blk + R_BMOD, KC)].rearrange("p a (n m) -> p (a n) m", n=2)
                        src = ps[:, 3 + j, 0:8 * NC].rearrange("p (m n c) -> p n m c", m=4, n=2)
                        v.tensor_tensor(o, src, bm.unsqueeze(3).to_broadcast([P, 2, 4, NC]), ALU.add).then_inc(mod_added, 1)
            dve.wait_ge(mod_added, 3 + 12)
            dve.wait_ge(in_const, 16)
            dve.wait_ge(x_copied, KC)

            def inverse_var(ch, dst, src, n):
                ch.link(v.tensor_scalar(dst, src, 1.0 / n, EPS, ALU.mult, ALU.add))
                v.reciprocal(dst, dst).then_inc(V.var_ready, 1)

            def modulated(ch, bank, sh, sca, nth, done):
                inverse_var(ch, stat[:, 1, :], ps[:, bank, 0:T], D)
                dve.wait_ge(V.rstd_ready, nth)
                ch.link(v.tensor_tensor(hT[:, :, :], xT[:, :, :], bc(stat[:, 1, :], KC), ALU.mult))
                smp = hT[:, :, SEQ:T].rearrange("p k (b t) -> p k b t", b=B)
                ch.link(v.tensor_tensor(smp, smp, mod[:, sca:sca + KC, 1:NC].unsqueeze(3).to_broadcast([P, KC, B, T_DEC]), ALU.mult))
                v.tensor_tensor(smp, smp, mod[:, sh:sh + KC, 1:NC].unsqueeze(3).to_broadcast([P, KC, B, T_DEC]), ALU.add)
                for k in range(KC):
                    last = v.tensor_scalar(hT[:, k, 0:SEQ], hT[:, k, 0:SEQ], mod[:, sca + k, 0:1], mod[:, sh + k, 0:1],
                                           ALU.mult, ALU.add)
                last.then_inc(done, 1)

            def add_gated(ch, bank_of, gt, arrived, done):
                for m in range(KC):
                    dve.wait_ge(arrived, m + 1)
                    src = ps[:, bank_of(m), :]
                    v.tensor_tensor(rtmp[:, m, :].rearrange("p (b t) -> p b t", b=B), src[:, SEQ:T].rearrange("p (b t) -> p b t", b=B),
                                    bl(mod[:, gt + m, 1:NC], T_DEC), ALU.mult)
                    v.scalar_tensor_tensor(xT[:, m, 0:SEQ], src[:, 0:SEQ], mod[:, gt + m, 0:1], xT[:, m, 0:SEQ],
                                           ALU.mult, ALU.add).then_inc(done, 1)
                dve.wait_ge(done, KC)
                v.tensor_tensor(xT[:, :, SEQ:T], xT[:, :, SEQ:T], rtmp[:, :, :], ALU.add).then_inc(done, 1)

            with dve.Fori(0, L) as l:
                ch = Chain(dve, V.dchain)
                v.tensor_copy(vec[:, :], vecT[:, bass.ds(l, 1), :].rearrange("p a r -> p (a r)"))
                v.tensor_copy(wc[:, :], wcT[:, bass.ds(l, 1), :].rearrange("p a r -> p (a r)"))
                v.memset(fullv[:, :, 0:HIST], 0.0).then_inc(V.pad_ready, 1)
                ch.link(v.tensor_copy(mod[:, :, :], modT[:, bass.ds(l, 1), :, :].rearrange("p a m c -> p (a m) c")))
                v.scalar_tensor_tensor(mod[:, M_SC1:M_SC1 + KC, :], mod[:, M_SC1:M_SC1 + KC, :], 1.0, bl(vec[:, R_GMIX:R_GMIX + KC], NC),
                                       ALU.add, ALU.mult)
                ch.link(v.scalar_tensor_tensor(mod[:, M_SC2:M_SC2 + KC, :], mod[:, M_SC2:M_SC2 + KC, :], 1.0,
                                               bl(vec[:, R_GFFN:R_GFFN + KC], NC), ALU.add, ALU.mult))
                dve.sem_inc(V.vectors_ready, 1)
                dve.wait_ge(V.norm_sum, 1)
                modulated(ch, 6, M_SH1, M_SC1, 1, V.h_ready)
                for i in range(4):
                    dve.wait_ge(V.z_sig, i + 1)
                    src = ps[:, (2 * i) % 4, :]
                    dve.wait_ge(V.inproj_done, 2 * i + 1)
                    v.tensor_tensor(fullv[:, i, HIST:FRING], src[:, 0:SEQ], zsig[:, i % 2, 0:SEQ], ALU.mult)
                    v.tensor_tensor(rtmp[:, i, :], src[:, SEQ:T], zsig[:, i % 2, SEQ:T], ALU.mult)
                    v.tensor_tensor(fullv[:, i, FRING:].rearrange("p (b w) -> p b w", b=B)[:, :, HIST:],
                                    src[:, SEQ:T].rearrange("p (b t) -> p b t", b=B),
                                    zsig[:, i % 2, SEQ:T].rearrange("p (b t) -> p b t", b=B), ALU.mult).then_inc(V.a_ready, 1)
                dve.wait_ge(V.a_ready, 4)
                base = ch.n
                for tap in range(TAPS):
                    for ct in range(CT):
                        wcol = wc[:, tap * CT + ct:tap * CT + ct + 1]
                        src = fullv[:, ct, tap:tap + SEQ]
                        if tap == 0:
                            ins = v.tensor_scalar(cT[:, ct, 0:SEQ], src, wcol, vec[:, R_BCONV + ct:R_BCONV + ct + 1], ALU.mult, ALU.add)
                        else:
                            dve.wait_ge(V.dchain, ch.n - CT + 1)
                            ins = v.scalar_tensor_tensor(cT[:, ct, 0:SEQ], src, wcol, cT[:, ct, 0:SEQ], ALU.mult, ALU.add)
                        ins.then_inc(V.dchain, 1)
                        ch.n += 1
                dve.wait_ge(V.dchain, ch.n)
                dve.sem_inc(V.conv_ready, 1)
                dve.wait_ge(V.proj_copied, 8)
                qk = proj[:, 0:8, :]
                v.tensor_tensor(big[0:64, :, :], qk[64:128], bc(C("sin")[64:128], 8), ALU.mult)
                ch.link(v.tensor_tensor(big[64:128, :, :], qk[0:64], bc(C("sin")[0:64], 8), ALU.mult))
                ch.link(v.tensor_tensor(qk, qk, bc(C("cos"), 8), ALU.mult))
                v.tensor_tensor(qk, qk, big[:, :, :], ALU.add).then_inc(V.rot_ready, 1)
                dve.wait_ge(V.rot_ready, 1)
                v.tensor_tensor(qd, proj[:, 0:4, P:T], C("qdec").rearrange("p (h t) -> p h t", h=H), ALU.mult).then_inc(V.qd_ready, 1)
                dve.wait_ge(V.ln_sum, 1)
                ch.link(v.tensor_scalar(stat[:, 0, :], ps[:, 6, 0:T], 1.0 / D_CONV, None, ALU.mult))
                v.tensor_tensor(cT, cT, bc(stat[:, 0, :], CT), ALU.subtract).then_inc(V.ln_centered, 1)
                dve.wait_ge(V.atok_stored, 16)
                dve.wait_ge(V.hist_stored, 16 * (1 + B))
                for c in range(2):
                    dve.wait_ge(V.score_done, c + 1)
                    v.tensor_tensor(sc[:, c, :], ps[:, 4 + c, :], C("decay"), ALU.mult).then_inc(V.sc_ready, 1)
                dve.wait_ge(V.score_done, 3)
                v.tensor_tensor(scs[0:NS, :], ps[0:NS, 0, 0:H * NS], C("sdecay")[0:NS], ALU.mult).then_inc(V.sc_ready, 1)
                for t, bank in enumerate((0, 1, 6)):
                    m = TILES[t][1]
                    dve.wait_ge(V.k_trans, t + 1)
                    v.tensor_tensor(kd[0:m, t, :].rearrange("p (h d) -> p h d", h=H), ps[0:m, bank, :].rearrange("p (h d) -> p h d", h=H),
                                    bl(C("kdec")[0:m, t * H:(t + 1) * H], P), ALU.mult).then_inc(V.kd_ready, 1)
                dve.wait_ge(V.s1_copied, 1)
                dve.wait_ge(V.st_done, 2)
                for h in range(H):
                    hp = slice(h * P, (h + 1) * P)
                    last = v.scalar_tensor_tensor(sf[:, hp], s1[:, hp], CDEC_P[h], ps[:, 7, hp], ALU.mult, ALU.add)
                last.then_inc(V.sf_ready, 1)
                dve.wait_ge(V.ln_var, 1)
                inverse_var(ch, stat[:, 1, :], ps[:, 2, 0:T], D_CONV)
                dve.wait_ge(V.g_sig, 1)
                for h in range(H):
                    last = v.scalar_tensor_tensor(proj[:, 12 + h, :], proj[:, 12 + h, :], vec[:, R_GRET + h:R_GRET + h + 1],
                                                  gsig[:, h, :], ALU.mult, ALU.mult)
                ch.link(last)
                dve.wait_ge(V.rstd_ready, 2)
                v.tensor_tensor(cT, cT, bc(stat[:, 1, :], CT), ALU.mult).then_inc(V.ln_scaled, 1)
                dve.wait_ge(V.ln_sig, 1)
                for ct in range(CT):
                    last = v.tensor_scalar(cT[:, ct, :], cT[:, ct, :], vec[:, R_GCLN + ct:R_GCLN + ct + 1],
                                           vec[:, R_BCLN + ct:R_BCLN + ct + 1], ALU.mult, ALU.add)
                ch.link(last)
                dve.wait_ge(V.inproj_done, 24)
                v.tensor_tensor(hT[:, 4:8, :], cT, lnsq, ALU.mult).then_inc(V.mix_conv, 1)

                def center(h):
                    dve.wait_ge(V.gn_sum, h + 1)
                    v.scalar_tensor_tensor(oS[:, h, :], ps[:, SUM_BANK[h], 0:T], -1.0 / DH, oS[:, h, :],
                                           ALU.mult, ALU.add).then_inc(V.gn_centered, 1)

                def sample_state(h):
                    dve.wait_ge(V.snew_done, h + 1)
                    dve.wait_ge(V.o_done, h + 1)
                    for g in range(2):
                        part = S_h[h][:, g * 512:(g + 1) * 512]
                        last = v.scalar_tensor_tensor(part, part, CDEC_S[h], ps[:, g, :], ALU.mult, ALU.add)
                    last.then_inc(V.snew_ready, 1)

                def head_var(h):
                    dve.wait_ge(V.gn_var, h + 1)
                    inverse_var(ch, gn_rstd[:, h, :], ps[:, VAR_BANK[h], 0:T], DH)

                def head_mix(h):
                    dve.wait_ge(V.rstd_ready, 3 + h)
                    ch.link(v.tensor_tensor(oS[:, h, :], oS[:, h, :], gn_rstd[:, h, :], ALU.mult))
                    v.tensor_tensor(hT[:, h, :], oS[:, h, :], proj[:, 12 + h, :], ALU.mult).then_inc(V.gn_mixed, 1)

                center(0)
                sample_state(0)
                center(1)
                head_var(0)
                sample_state(1)
                center(2)
                head_var(1)
                head_mix(0)
                sample_state(2)
                center(3)
                head_var(2)
                head_mix(1)
                head_var(3)
                head_mix(2)
                sample_state(3)
                head_mix(3)
                add_gated(ch, lambda m: OUT_BANK[m % 4], M_GT1, V.outproj_done, V.x_mid)
                dve.wait_ge(V.norm2_sum, 1)
                modulated(ch, 6, M_SH2, M_SC2, 3 + H, V.h2_ready)

                def r3(n):
                    return rt[:, n, :].rearrange("p (t e) -> p t e", t=3)

                def r4(n):
                    return rt[:, n, :].rearrange("p (a e) -> p a e", e=EPG)

                def col(n, k=3):
                    return rt[:, n, 0:k]

                def over_e(ap, n=E):
                    return ap.unsqueeze(2).to_broadcast([P, ap.shape[1], n])

                def tt(o, x, y, op):
                    ch.link(v.tensor_tensor(o, x, y, op))

                dve.wait_ge(in_wr, 32)
                v.memset(posm[:, :, :], -1000.0)
                ch.link(v.memset(rt[:, 0, :], 0.0))
                dve.wait_ge(V.logits_done, 1)
                v.tensor_tensor(r3(0)[:, 0:2], ps[:, 4, 0:2 * E].rearrange("p (t e) -> p t e", t=2), bc(brow[:, :], 2), ALU.add)
                ch.link(v.tensor_tensor(r3(0)[0:NS, 2], ps[0:NS, 4, 2 * E:3 * E], brow[0:NS, :], ALU.add))
                ch.link(v.tensor_reduce(col(2), r3(0), AX.X, ALU.max))
                v.tensor_tensor(r3(0), r3(0), over_e(col(2)), ALU.subtract).then_inc(V.lg_ready, 1)
                dve.wait_ge(V.ex_ready, 1)
                ch.link(v.tensor_reduce(col(2), r3(1), AX.X, ALU.add))
                ch.link(v.reciprocal(col(2), col(2)))
                tt(r3(1), r3(1), over_e(col(2)), ALU.mult)
                pv = r4(1)
                hi, lo = rt[:, 3, 0:24].rearrange("p (a e) -> p a e", e=2), rt[:, 3, 24:48].rearrange("p (a e) -> p a e", e=2)
                v.tensor_tensor(hi, pv[:, :, 0:2], pv[:, :, 2:4], ALU.max)
                ch.link(v.tensor_tensor(lo, pv[:, :, 0:2], pv[:, :, 2:4], ALU.min))
                t1, t2, t3 = (rt[:, 4, k * 12:(k + 1) * 12] for k in range(3))
                v.tensor_tensor(t1, hi[:, :, 0], hi[:, :, 1], ALU.max)
                v.tensor_tensor(t2, hi[:, :, 0], hi[:, :, 1], ALU.min)
                ch.link(v.tensor_tensor(t3, lo[:, :, 0], lo[:, :, 1], ALU.max))
                tt(t2, t2, t3, ALU.max)
                tt(t1, t1, t2, ALU.add)
                gsc = t1.rearrange("p (t g) -> p t g", t=3)
                gm = rt[:, 5, 0:12].rearrange("p (t g) -> p t g", t=3)

                def first_of(score, key, onehot, width):
                    ch.link(v.tensor_reduce(col(2), score, AX.X, ALU.max))
                    tt(onehot, score, over_e(col(2), width), ALU.is_equal)
                    tt(onehot, onehot, bc(key, 3), ALU.mult)
                    ch.link(v.tensor_reduce(col(6), onehot, AX.X, ALU.max))
                    tt(onehot, onehot, over_e(col(6), width), ALU.is_equal)

                first_of(gsc, C("gkey"), gm, GROUPS)
                gme = rt[:, 5, 0:12].unsqueeze(2).to_broadcast([P, 12, EPG])
                tt(r4(7), pv, gme, ALU.mult)
                ch.link(v.tensor_scalar(rt[:, 5, 12:24], rt[:, 5, 0:12], -1.0, None, ALU.add))
                tt(r4(7), r4(7), rt[:, 5, 12:24].unsqueeze(2).to_broadcast([P, 12, EPG]), ALU.add)
                first_of(r3(7), C("ekey"), r3(8), E)
                ch.link(v.tensor_copy(col(11), col(2)))
                ch.link(v.scalar_tensor_tensor(rt[:, 7, :], rt[:, 8, :], -4.0, rt[:, 7, :], ALU.mult, ALU.add))
                first_of(r3(7), C("ekey"), r3(9), E)
                tt(col(12), col(11), col(2), ALU.add)
                ch.link(v.reciprocal(col(12), col(12)))
                v.tensor_tensor(wts[:, 0, :], col(11), col(12), ALU.mult)
                v.tensor_tensor(wts[:, 1, :], col(2), col(12), ALU.mult)
                tt(r3(10), r3(8), r3(9), ALU.add)
                v.tensor_tensor(r3(10), r3(10), over_e(C("valid")), ALU.mult).then_inc(V.m_ready, 1)
                dve.wait_ge(V.pos_done, 1)
                dve.wait_ge(V.m_ready, 1)
                ch.link(v.tensor_copy(rt[:, 13, :], ps[:, 5, 0:3 * E]))
                ch.link(v.tensor_copy(rt[:, 14, 0:E], ps[:, 5, 3 * E:4 * E]))
                ch.link(v.scalar_tensor_tensor(r3(3), r3(13), 1000.0, r3(10), ALU.add, ALU.mult))
                v.tensor_scalar(posm[:, :, 0:E], r3(3), -1000.0, None, ALU.add)
                cnt, acc, xs, xt = rt[:, 14, 0:E], rt[:, 14, E:2 * E], rt[:, 14, 2 * E:3 * E], rt[:, 12, 0:E]
                ch.link(v.tensor_scalar(acc, cnt, float(BLK), 1.0, ALU.is_gt, ALU.add))
                for s in range(2, MAXSUB):
                    ch.link(v.scalar_tensor_tensor(acc, cnt, float(s * BLK), acc, ALU.is_gt, ALU.add))
                v.tensor_copy(nsubi[:, :], acc)
                ch.link(v.tensor_scalar(xs, acc, -1.0, None, ALU.add))
                for s in (1, 2, 4, 8):
                    ch.link(v.tensor_copy(xt, xs))
                    tt(xs[:, s:], xt[:, s:], xt[:, :E - s], ALU.add)
                ch.link(v.scalar_tensor_tensor(xs, acc, -1.0, xs, ALU.mult, ALU.add))
                ch.link(v.tensor_scalar(xs, xs, 1.0, float(BLK), ALU.add, ALU.mult))
                tt(xs, xs, C("xrow"), ALU.add)
                ch.link(v.tensor_scalar(r3(3), r3(13), BLK - 0.5, None, ALU.is_gt))
                tt(r3(3), r3(3), bc(xs, 3), ALU.mult)
                tt(r3(13), r3(13), bc(C("erow"), 3), ALU.add)
                tt(r3(13), r3(13), r3(3), ALU.add)
                for k in range(2):
                    tt(r3(3), r3(13), r3(8 + k), ALU.mult)
                    ch.link(v.tensor_reduce(col(15), r3(3), AX.X, ALU.add))
                    last = v.tensor_copy(rowi[:, k, :], col(15))
                    if k == 0:
                        ch.link(last)
                last.then_inc(V.route_ready, 1)
                dve.wait_ge(V.route_ready, 1)

                for sgn in (V.h_act, V.hT_copied):
                    dve.sem_inc(sgn, 2)
                for sgn in (V.x_sel, V.x_xg, V.x_gated, V.x_h, V.x_hs, V.x_h2):
                    dve.sem_inc(sgn, 1)

                def select(dst, pos):
                    for t in range(3):
                        last = v.tensor_scalar(dst[:, t * BLK:(t + 1) * BLK], C("iota"), pos(t), None, ALU.is_equal)
                    return last

                dve.wait_ge(V.mix_conv, 1)
                select(sel[:, 0, :], lambda t: posm[:, t, 0:1]).then_inc(V.sel_ready, 1)
                xn = dve.alloc_register("extra_blocks")
                dve.reg_mov(xn, 1)
                with dve.Fori(0, E // 2) as g:
                    for i in range(2):
                        dve.wait_ge(V.gathered, g * 2 + i + 2)
                        select(sel[:, (i + 1) % 2, :], lambda t: posm[:, t, bass.ds(g * 2 + i + 1, 1)]).then_inc(V.sel_ready, 1)
                        nsub = dve.value_load(nsubi[0:1, bass.ds(g * 2 + i, 1)], min_val=1, max_val=MAXSUB)
                        xlo = dve.alloc_register(f"extra_first{i}")
                        dve.reg_mov(xlo, xn)
                        with dve.If(nsub > 1):
                            v.tensor_copy(posx[:, :].unsqueeze(2), posm[:, :, bass.ds(g * 2 + i, 1)]).then_inc(V.pchain, 1)
                            dve.drain()
                            with dve.Fori(1, nsub) as s:
                                dve.reg_add(xn, xn, 1)
                                v.tensor_scalar(posx[:, :], posx[:, :], -float(BLK), None, ALU.add)
                                dve.drain()
                                select(selx, lambda t: posx[:, t:t + 1]).then_inc(V.x_sel, 1)
                                dve.wait_ge(V.x_gath, xn)
                                v.tensor_copy(xgx, ps[:, 7, :]).then_inc(V.x_xg, 1)
                                dve.wait_ge(V.x_sig, xn)
                                v.tensor_tensor(hx, ps[:, 5, :], gsx, ALU.mult).then_inc(V.x_gated, 1)
                                dve.wait_ge(V.x_gated, xn)
                                v.tensor_tensor(hx, ps[:, 6, :], hx, ALU.mult).then_inc(V.x_h, 1)
                                dve.wait_ge(V.x_t, xn)
                                v.tensor_copy(hxs[:, bass.ds(s * 512 - 512, 512)], ps[:, 7, :]).then_inc(V.x_hs, 1)
                            dve.wait_ge(V.x_hs, xn)
                            dve.sem_inc(tick, 1)
                        dve.wait_ge(V.sig_done, g * 2 + i + 1)
                        dve.wait_ge(V.trans_done, g * 2 + i + 2)
                        v.tensor_tensor(hs, ps[:, 2, :], gs, ALU.mult).then_inc(V.gated, 1)
                        dve.wait_ge(V.gated, g * 2 + i + 1)
                        dve.wait_ge(V.up_done, g * 2 + i + 3)
                        v.tensor_tensor(hs, ps[:, 3, :], hs, ALU.mult).then_inc(V.h_act, 1)
                        dve.wait_ge(V.trans_done, g * 2 + i + 3)
                        dve.wait_ge(V.down_done, g * 2 + i + 2)
                        v.tensor_copy(h2T, ps[:, 4, :]).then_inc(V.hT_copied, 1)
                        with dve.If(nsub > 1):
                            with dve.Fori(1, nsub) as s:
                                dve.wait_ge(V.x_down, xlo)
                                dve.reg_add(xlo, xlo, 1)
                                v.tensor_copy(h2x, hxs[:, bass.ds(s * 512 - 512, 512)]).then_inc(V.x_h2, 1)
                for t, (t0, m) in enumerate(TILES):
                    dve.wait_ge(V.gath0, 16 * (t + 1))
                    dve.wait_ge(V.gath1, 16 * (t + 1))
                    ch.link(v.tensor_scalar(h2tok[0:m, t, :], yg[0:m, 0, :], wts[0:m, 0, t:t + 1], None, ALU.mult))
                    v.scalar_tensor_tensor(h2tok[0:m, t, :], yg[0:m, 1, :], wts[0:m, 1, t:t + 1], h2tok[0:m, t, :],
                                           ALU.mult, ALU.add).then_inc(V.comb_ready, 1)
                add_gated(ch, lambda m: 2 + m % 2, M_GT2, V.yt_trans, V.x_end)
                dve.drain().then_inc(layer_done, 1)
                dve.wait_ge(layer_open, l + 1)
            dve.wait_ge(fin_sum, 1)
            v.tensor_scalar(stat[:, 1, :], ps[:, 6, 0:T], 1.0 / D, EPS, ALU.mult, ALU.add).then_inc(fin_rs, 1)
            dve.wait_ge(fin_rs, 1)
            v.reciprocal(stat[:, 1, :], stat[:, 1, :]).then_inc(fin_rs, 1)
            dve.wait_ge(fin_rs, 3)
            for k in range(KC):
                last = v.scalar_tensor_tensor(hT[:, k, :], xT[:, k, :], vecT[:, 0, R_GFIN + k:R_GFIN + k + 1], stat[:, 1, :],
                                              ALU.mult, ALU.mult)
            last.then_inc(fin_y, 1)

        @block.gpsimd
        def _(pool):
            gp = nc.gpsimd

            gp.memset(big[:, :, :], 0.0).then_inc(zeros_set, 1)
            pool.wait_ge(zeros_set, 1)
            zeros = big[:, :, :].rearrange("p a b -> p (a b)")[:, 0:MAXEXTRA // 2 * BLK * D // P]
            for k in range(2):
                r0 = E * BLK + k * (MAXEXTRA // 2) * BLK
                pool.dma_start(ydram[r0:r0 + MAXEXTRA // 2 * BLK, :].rearrange("(p r) d -> p (r d)", p=P), zeros).then_inc(rows_zeroed, 16)
            pool.wait_ge(mod_added, 3 + 12)
            with pool.Fori(0, L) as l:
                pool.dma_start(cbt[0:120, :, :], state_conv.rearrange("l b t c -> l (b t) c").rearrange("l (r p) c -> l p r c", p=120)
                               [bass.ds(l, 1)].rearrange("a p r c -> (a p) r c")).then_inc(V.cb_loaded, 16)
                pool.dma_start(conv_s[bass.ds(l, 1), :, 0:HIST - T_DEC, :].rearrange("a b t c -> (a b) (t c)"),
                               state_conv[bass.ds(l, 1), :, T_DEC:HIST, :].rearrange("a b t c -> (a b) (t c)")).then_inc(V.hist_stored, 16)
                pool.wait_ge(V.vectors_ready, 1)
                pool.wait_ge(V.cb_copied, CT)
                pool.wait_ge(V.a_ready, CT)
                pc = Chain(pool, V.pchain)
                win = fullv[:, :, FRING:].rearrange("p c (b w) -> p c b w", b=B)
                slot = cprod.rearrange("p (k c s) -> p k c s", k=8, c=CT)
                flat = cprod.rearrange("p (k w) -> p k w", k=8)
                csum = cpsum.rearrange("p (c s) -> p c s", c=CT)
                for rnd in range(4):
                    for k in range(8):
                        tap = rnd * 8 + k
                        if tap < TAPS:
                            last = gp.tensor_tensor(slot[:, k].rearrange("p c (b t) -> p c b t", b=B), win[:, :, :, tap:tap + T_DEC],
                                                    wc[:, tap * CT:(tap + 1) * CT].unsqueeze(2).unsqueeze(3)
                                                    .to_broadcast([P, CT, B, T_DEC]), ALU.mult)
                        else:
                            last = gp.tensor_copy(slot[:, k], vec[:, R_BCONV:R_BCONV + CT].unsqueeze(2).to_broadcast([P, CT, NS]))
                    pc.link(last)
                    for half in (4, 2, 1):
                        if half == 1 and rnd == 0:
                            pc.link(gp.tensor_tensor(csum, slot[:, 0], slot[:, 1], ALU.add))
                        else:
                            pc.link(gp.tensor_tensor(flat[:, 0:half], flat[:, 0:half], flat[:, half:2 * half], ALU.add))
                    if rnd in (1, 2):
                        pc.link(gp.tensor_tensor(csum, csum, slot[:, 0], ALU.add))
                gp.tensor_tensor(cT[:, :, SEQ:T], csum, slot[:, 0], ALU.add).then_inc(V.sconv_ready, 1)
                pool.wait_ge(V.atok_copied, 2)
                pool.dma_start(conv_p[bass.ds(l, 1), 0].rearrange("a t c -> (a t) c"), atok[0:HIST, 0, :]).then_inc(V.atok_stored, 16)
                for b in range(B):
                    last = pool.dma_start(conv_s[bass.ds(l, 1), b, HIST - T_DEC:HIST, :].rearrange("a t c -> (a t) c"),
                                          atok[b * T_DEC:(b + 1) * T_DEC, 1, :])
                    last.then_inc(V.hist_stored, 16)
                ret_v = state_ret.rearrange("l b h d e -> l h d b e")
                rets_v = ret_s.rearrange("l b h d e -> l h d b e")
                pool.wait_ge(V.rot_ready, 1)

                def state(h):
                    return S_h[h].rearrange("p (b e) -> p b e", b=B)

                def dstate(v5, h):
                    return v5[bass.ds(l, 1), h].rearrange("a d b e -> (a d) b e")

                for h in (0, 1):
                    pool.dma_start(state(h), dstate(ret_v, h)).then_inc(V.Sa_loaded, 16)
                pool.wait_ge(V.k_trans, 3)
                pool.wait_ge(V.score_done, 3)
                pool.wait_ge(V.qd_ready, 1)
                for h in (2, 3):
                    pool.dma_start(state(h), dstate(ret_v, h)).then_inc(V.Sb_loaded, 16)
                pool.wait_ge(V.v_copied, 3)
                for h in range(H):
                    if h >= 1:
                        pool.wait_ge(V.snew_done, h)
                    gp.tensor_tensor(vmask[0:NS, :].rearrange("p (b e) -> p b e", b=B),
                                     vt[0:NS, 2, h * P:(h + 1) * P].unsqueeze(1).to_broadcast([NS, B, DH]),
                                     C("smask")[0:NS].unsqueeze(2).to_broadcast([NS, B, DH]), ALU.mult).then_inc(V.vmask_ready, 1)
                    if h == 0:
                        pool.wait_ge(V.sf_ready, 1)
                        pool.dma_start(ret_p[bass.ds(l, 1), 0].rearrange("a h d e -> (a d) h e"),
                                       sf.rearrange("p (h e) -> p h e", h=H)).then_inc(V.sf_stored, 16)
                    if h >= 1:
                        pool.wait_ge(V.snew_ready, h)
                        pool.dma_start(dstate(rets_v, h - 1), state(h - 1)).then_inc(V.Sa_stored if h <= 2 else V.Sb_stored, 16)
                pool.wait_ge(V.snew_ready, H)
                pool.dma_start(dstate(rets_v, H - 1), state(H - 1)).then_inc(V.Sb_stored, 16)
                pool.wait_ge(V.route_ready, 1)
                pool.wait_ge(V.y_copied, E + 2)
                pool.wait_ge(V.down_done, E + 2)
                for i in range(2):
                    pool.wait_ge(y_stored[i], 32 * (E // 2) + 16)
                for t, (t0, m) in enumerate(TILES):
                    if t >= 1:
                        pool.wait_ge(V.comb_ready, t)
                    for k in range(2):
                        gp.indirect_dma_start(yg[0:m, k, :], None, ydram[:, :],
                                              bass.IndirectOffsetOnAxis(ap=rowi[0:m, k, t:t + 1], axis=0)) \
                            .then_inc(V.gath0 if k == 0 else V.gath1, 16)
                pool.wait_ge(V.sf_stored, 16)
                pool.wait_ge(V.Sa_stored, 32)
                pool.wait_ge(V.Sb_stored, 32)
                pool.wait_ge(V.x_end, KC + 1)
                pool.wait_ge(layer_done, 3)
                pool.drain()
                pool.dma_reset(layer_sems)
                pool.sem_clear(layer_sems)
                pool.drain().then_inc(layer_open, 1)


_INS = ['x_prompt', 'x_sample', 'state_ret', 'state_conv', 'c_prompt', 'c_sample', 'w_mod', 'b_mod', 'g_mix_norm', 'w_in',
        'w_conv', 'b_conv', 'g_conv_ln', 'b_conv_ln', 'g_ret_gn', 'w_out', 'g_ffn_norm', 'w_router', 'b_router',
        'w_exp_gate', 'w_exp_up', 'w_exp_down', 'g_final']
_OUTS = [(1, SEQ, D), (B, T_DEC, D), (L, 1, H, DH, DH), (L, 1, HIST, D_CONV), (L, B, H, DH, DH), (L, B, HIST, D_CONV)]


def kernel(**inputs):
    import concourse.bacc as bacc
    from concourse.bass_utils import run_bass_kernel_spmd

    nc = bacc.Bacc("TRN2", target_bir_lowering=False, num_devices=1)
    arrays = {name: np.ascontiguousarray(inputs[name]) for name in _INS}
    arrays["consts"] = constants()
    args = [nc.dram_tensor(f"in_{n}", a.shape, mybir.dt.from_np(a.dtype), kind="ExternalInput").ap() for n, a in arrays.items()]
    args += [nc.dram_tensor(f"out_{i}", s, mybir.dt.float32, kind="ExternalOutput").ap() for i, s in enumerate(_OUTS)]
    hybrid_step_kernel(nc, *args)
    r = run_bass_kernel_spmd(nc, [{f"in_{n}": a for n, a in arrays.items()}], core_ids=[0])
    return tuple(r.results[0][f"out_{i}"] for i in range(len(_OUTS)))
```

```python
import math
from contextlib import ExitStack

import numpy as np

import concourse.bass as bass
from concourse import mybir

L, D, SEQ, B, T_DEC = 2, 1024, 256, 8, 4
NS = B * T_DEC
T = SEQ + NS
P = 128
KC = D // P
TILES = [(0, P), (P, P), (2 * P, NS)]
H, DH = 4, 128
D_RET, D_CONV = 512, 512
CT = D_CONV // P
TAPS, HIST = 31, 30
PAST = 2048
E, GROUPS, EPG = 16, 4, 4
BLK = 64
MAXSUB = -(-T // BLK)
MAXEXTRA = 2 * T // BLK - 1
YROWS = (16 + MAXEXTRA) * BLK
NC = 1 + B
NMOD = 6
EPS = 1e-6
NSLOT = 12
UK = 2
UQ = KC // UK
FRING = HIST + SEQ
SRING = HIST + T_DEC

R_GMIX, R_GFFN, R_BMOD, R_BCONV, R_GCLN, R_BCLN, R_GRET, R_GFIN, NROWS = 0, 8, 16, 64, 68, 72, 76, 80, 88
M_SH1, M_SC1, M_GT1, M_SH2, M_SC2, M_GT2 = 0, 8, 16, 24, 32, 40
NMB = NMOD * KC

LG = [math.log(1.0 - 2.0 ** (-5.0 - h)) for h in range(H)]
CDEC_P = [math.exp(P * g) for g in LG]
CDEC_S = [math.exp(T_DEC * g) for g in LG]

CONST = [("ident", 128), ("tri", 128), ("ones", 128), ("fold", 2 * NC), ("decay", 4 * 128), ("sdecay", 4 * NS),
         ("cos", T), ("sin", T), ("qdec", 4 * (P + NS)), ("kdec", 12), ("smask", B), ("iota", BLK),
         ("erow", E), ("xrow", E), ("ekey", E), ("gkey", GROUPS), ("valid", 3)]
COFF, _o = {}, 0
for _n, _w in CONST:
    COFF[_n] = (_o, _w)
    _o += _w
NCONST = _o


def constants():
    c = {}
    i = np.arange(P)
    c["ident"] = np.eye(P)
    c["tri"] = (i[:, None] < i[None, :]).astype(float)
    c["ones"] = np.ones((P, P))
    fold = np.zeros((P, 2, NC))
    for r in range(P):
        if r % 32 < NC:
            fold[r, (r // 32) % 2, r % 32] = 1.0
    c["fold"] = fold.reshape(P, -1)
    scale = DH ** -0.5
    rel = i[None, :] - i[:, None]
    c["decay"] = np.stack([np.where(rel >= 0, np.exp(np.maximum(rel, 0) * g), 0.0) * scale for g in LG], 1).reshape(P, -1)
    s = np.arange(NS)
    srel = s[None, :] - s[:, None]
    same = (s[None, :] // T_DEC == s[:, None] // T_DEC) & (srel >= 0)
    sd = np.zeros((P, 4, NS))
    for h, g in enumerate(LG):
        sd[:NS, h] = np.where(same, np.exp(np.maximum(srel, 0) * g), 0.0) * scale
    c["sdecay"] = sd.reshape(P, -1)
    half = DH // 2
    inv = (np.float32(10000.0) ** (-np.arange(half, dtype=np.float32) / np.float32(half))).astype(np.float32)
    pos = np.concatenate([np.arange(SEQ), PAST + s % T_DEC]).astype(np.float32)
    ang = (pos[None, :] * inv[:, None]).astype(np.float32).astype(np.float64)
    c["cos"] = np.concatenate([np.cos(ang), np.cos(ang)], 0)
    c["sin"] = np.concatenate([np.sin(ang), -np.sin(ang)], 0)
    qi = np.concatenate([np.arange(P) + 1, s % T_DEC + 1])
    c["qdec"] = np.broadcast_to(np.stack([np.exp(qi * g) for g in LG]).reshape(1, -1), (P, 4 * (P + NS)))
    kd = np.zeros((P, 3, 4))
    for h, g in enumerate(LG):
        kd[:, 0, h] = kd[:, 1, h] = np.exp((P - 1 - i) * g) * scale
        kd[:NS, 2, h] = np.exp((T_DEC - 1 - s % T_DEC) * g) * scale
    c["kdec"] = kd.reshape(P, -1)
    sm = np.zeros((P, B))
    sm[s, s // T_DEC] = 1.0
    c["smask"] = sm
    c["iota"] = np.broadcast_to(np.arange(BLK), (P, BLK))
    c["erow"] = np.broadcast_to(np.arange(E) * BLK, (P, E))
    c["xrow"] = np.broadcast_to(E * BLK - BLK - np.arange(E) * BLK, (P, E))
    c["ekey"] = np.broadcast_to(E - np.arange(E), (P, E))
    c["gkey"] = np.broadcast_to(GROUPS - np.arange(GROUPS), (P, GROUPS))
    v = np.ones((P, 3))
    v[NS:, 2] = 0.0
    c["valid"] = v
    return np.ascontiguousarray(np.concatenate([c[n] for n, _ in CONST], 1).astype(np.float32))


class Chain:

    def __init__(self, eng, sem):
        self.eng, self.sem, self.n = eng, sem, 0

    def link(self, ins):
        ins.then_inc(self.sem, 1)
        self.n += 1
        self.eng.wait_ge(self.sem, self.n)


def hybrid_step_kernel(nc, x_prompt, x_sample, state_ret, state_conv, c_prompt, c_sample, w_mod, b_mod, g_mix_norm,
                       w_in, w_conv, b_conv, g_conv_ln, b_conv_ln, g_ret_gn, w_out, g_ffn_norm, w_router, b_router,
                       w_exp_gate, w_exp_up, w_exp_down, g_final, consts,
                       y_prompt, y_sample, ret_p, conv_p, ret_s, conv_s):
    f32, i32, u32 = mybir.dt.float32, mybir.dt.int32, mybir.dt.uint32
    ALU, ACT, AX = mybir.AluOpType, mybir.ActivationFunctionType, mybir.AxisListType
    ctx = ExitStack()
    with ctx:
        def sb(name, shape, dt=f32):
            return ctx.enter_context(nc.sbuf_tensor(name, shape, dt))

        ring = sb("ring", [P, NSLOT, UK, D])
        xT = sb("xT", [P, KC, T])
        hT = sb("hT", [P, KC, T])
        big = sb("big", [P, KC, T])
        cst = sb("cst", [P, NCONST])
        vecT = sb("vecT", [P, L, NROWS])
        wcT = sb("wcT", [P, L, TAPS * CT])
        modT = sb("modT", [P, L, NMB // 2, NC])
        vec = sb("vec", [P, NROWS])
        wc = sb("wc", [P, TAPS * CT])
        mod = sb("mod", [P, NMB, NC])
        wr = sb("wr", [P, KC, E])
        brow = sb("brow", [P, E])
        condT = sb("condT", [P, KC, 32])
        stat = sb("stat", [P, 2, T])
        rt = sb("rt", [P, 16, 3 * E])
        posm = sb("posm", [P, 3, E + 1])
        wts = sb("wts", [P, 2, 3])
        rowi = sb("rowi", [P, 2, 3], u32)
        nsubi = sb("nsubi", [P, E], i32)
        posx = sb("posx", [P, 3])
        rtmp = sb("rtmp", [P, KC, NS])
        ARENA = 14976
        arena = sb("arena", [P, ARENA])
        ps = ctx.enter_context(nc.psum_tensor("ps", [P, 8, 512], f32))

        def C(name):
            o, w = COFF[name]
            return cst[:, o:o + w]

        ident = C("ident")
        ones = C("ones")
        used = {}

        def cut(phase, *dims):
            n = int(np.prod(dims))
            o = used.get(phase, 0)
            used[phase] = o + n
            assert o + n <= ARENA, (phase, o + n)
            v = arena[:, o:o + n]
            if len(dims) == 2:
                v = v.rearrange("p (a b) -> p a b", a=dims[0])
            elif len(dims) == 3:
                v = v.rearrange("p (a b c) -> p a b c", a=dims[0], b=dims[1])
            return v

        x_tok = cut("setup", 3, D)
        c_tok = cut("setup", D)
        c_sig = cut("setup", D)
        vrows = cut("setup", L, P)
        wcrows = cut("setup", L, P)
        modS = cut("setup", 3, 512)
        proj = cut("mix", 16, T)
        full = cut("mix", KC * T)
        fullv = full[:, 0:CT * (FRING + B * SRING)].rearrange("p (c w) -> p c w", c=CT)
        cT = cut("mix", CT, T)
        kd = cut("mix", 3, 512)
        vt = cut("mix", 3, 512)
        sc = cut("mix", 2, 512)
        scs = cut("mix", H * NS)
        s1 = cut("mix", 512)
        sf = cut("mix", 512)
        qd = cut("mix", H, P + NS)
        vmask = cut("mix", D)
        cpsum = scs
        cprod = vmask
        rot = kd.rearrange("p a b -> p (a b)")[:, 0:H * T].rearrange("p (h t) -> p h t", h=H)
        cbt = arena[:, used["mix"] - D - H * (P + NS) - 1024:used["mix"] - D - H * (P + NS)] \
            .rearrange("p (a b) -> p a b", a=2)
        cbt_start = used["mix"] - D - H * (P + NS) - 1024
        zsig = vt[:, 0:2, 0:T]
        atok = sc
        lnsq = hT[:, 4:8, :]
        gsig = hT[:, 0:4, :]
        oS = proj[:, 8:12, :]
        S_a = big[:, :, :].rearrange("p a b -> p (a b)")[:, 0:2 * B * DH]
        S_b = full[:, 0:2 * B * DH]
        gn_sq, gn_rstd = gsig, cT
        S_h = [S_a[:, 0:B * DH], S_a[:, B * DH:], S_b[:, 0:B * DH], S_b[:, B * DH:]]
        h2tok = cut("moe", 3, D)
        yg = cut("moe", 2, D)
        hxs = yg.rearrange("p a b -> p (a b)")
        after_yg = used["moe"]
        xg = cut("moe", 2, KC * BLK)
        sel = cut("moe", 2, 3 * BLK)
        gs = cut("moe", 512)
        hs = cut("moe", 512)
        h2T = cut("moe", 512)
        ysb = cut("moe", 2, 512)
        xgx = cut("moe", 512)
        gsx = cut("moe", 512)
        hx = cut("moe", 512)
        h2x = cut("moe", 512)
        yx = cut("moe", 512)
        selx = cut("moe", 3 * BLK)
        assert used["moe"] <= cbt_start
        rows = [yg, big[:, :, :].rearrange("p a b -> p (a b)")[:, 0:2 * D].rearrange("p (a b) -> p a b", a=2),
                arena[:, after_yg:after_yg + 2 * D].rearrange("p (a b) -> p a b", a=2)]

        SUM_BANK, VAR_BANK, OUT_BANK = (6, 3, 6, 3), (7, 2, 7, 2), (4, 5, 6, 3)

        ydram = nc.dram_tensor("expert_rows", (YROWS, D), f32, kind="Internal").ap()

        def sem(name):
            return ctx.enter_context(nc.semaphore(name))

        loaded = [sem(f"unit_loaded{s}") for s in range(NSLOT)]
        freed = [sem(f"unit_freed{s}") for s in range(NSLOT)]
        in_const, in_x, in_c, in_rows, in_wr = (sem(n) for n in ("in_const", "in_x", "in_c", "in_rows", "in_wr"))
        (rows_zeroed, zeros_set, cpad, c_sigd, c_act, c_trans, cond_ready, x_trans, x_copied, rows_trans, rows_copied, mod_done, mod_evac,
         fold_done, mod_added) = (sem(n) for n in (
             "rows_zeroed", "zeros_set", "cpad", "c_sigd", "c_act", "c_trans", "cond_ready", "x_trans", "x_copied", "rows_trans", "rows_copied",
             "mod_done", "mod_evac", "fold_done", "mod_added"))
        layer_open, y_out, fin_cp = (sem(n) for n in ("layer_open", "y_out", "fin_cp"))
        cb_loaded, rows_read = sem("cb_loaded"), sem("rows_read")
        tick = sem("tick")
        layer_done = sem("layer_done")
        names = """var_ready rstd_ready vectors_ready norm_sq norm_sum h_ready cb_trans cb_copied pad_ready
        inproj_done z_sig a_ready proj_copied conv_ready sconv_ready a_trans atok_copied atok_stored hist_stored rot_ready
        qd_ready ln_sum ln_centered ln_sq ln_var ln_scaled ln_sig mix_conv score_done sc_ready v_trans v_copied
        k_trans kd_ready g_sig st_done s1_copied sf_ready sf_stored Sa_loaded Sb_loaded vmask_ready snew_done
        snew_ready states_stored o_done o_copied gn_sum gn_centered gn_sq gn_var gn_mixed outproj_done x_mid
        norm2_sq norm2_sum h2_ready h2_trans h2_copied logits_done lg_ready ex_ready m_ready pos_done route_ready
        dchain pchain sel_ready gathered xg_copied gate_done up_done sig_done gated h_act trans_done hT_copied
        down_done y_copied y_stored0 y_stored1 x_sel x_gath x_xg x_gu x_sig x_gated x_h x_t x_hs x_h2 x_down x_yc x_st
        mod2_done mod2_evac mod2_fold mod2_added gath0 gath1 gath2 comb_ready yt_trans x_end""".split()
        S = {n: sem(n) for n in names}
        nums = [layer_done.num] + [S[n].num for n in names]
        assert nums == list(range(nums[0], nums[0] + len(nums)))
        layer_sems = range(nums[0], nums[-1] + 1)
        V = type("Signals", (), S)
        fin_sq, fin_sum, fin_rs, fin_y, fin_tr = V.norm_sq, V.norm_sum, V.var_ready, V.h_ready, V.h2_trans
        y_stored = [V.y_stored0, V.y_stored1]
        row_gathers = [V.gath0, V.gath1, V.gath2]
        block = ctx.enter_context(nc.Block())

        SETUP_USES = L * 3 * UQ // NSLOT
        PRE = [3 if s < UQ else 2 for s in range(NSLOT)]
        PER_LAYER = [p + E for p in PRE]

        FREE0 = 1

        def unit_uses(s, l, k):
            return l * PER_LAYER[s] + (SETUP_USES + k + FREE0)

        @block.sync
        def _(sp):
            mod_v = w_mod.rearrange("l (q k p) c -> l q p k c", q=UQ, p=P)
            in_v = w_in.rearrange("l (q k p) c -> l q p k c", q=UQ, p=P)
            out_v = w_out.rearrange("l (q k p) c -> l q p k c", q=UQ, p=P)
            exp_v = [w.rearrange("l e (q k p) c -> (l e) q p k c", q=UQ, p=P) for w in (w_exp_gate, w_exp_up, w_exp_down)]
            for row, n, src in ((R_GMIX, 8, g_mix_norm), (R_GFFN, 8, g_ffn_norm), (R_BMOD, NMB, b_mod), (R_BCONV, 4, b_conv),
                                (R_GCLN, 4, g_conv_ln), (R_BCLN, 4, b_conv_ln), (R_GRET, 4, g_ret_gn)):
                sp.dma_start(vrows[row:row + n, :, :], src.rearrange("l (r p) -> r l p", p=P)).then_inc(in_rows, 16)
            for l in range(L):
                sp.dma_start(vrows[R_GFIN:R_GFIN + 8, l, :], g_final.rearrange("(r p) -> r p", p=P)).then_inc(in_rows, 16)
            sp.dma_start(wcrows[0:TAPS * CT, :, :], w_conv.rearrange("l t (c p) -> (t c) l p", p=P)).then_inc(in_rows, 16)
            with sp.Fori(0, L) as l:
                for j in range(3):
                    for q in range(UQ):
                        s = j * UQ + q
                        sp.wait_ge(freed[s], l + 1)
                        sp.sem_inc(tick, 1)
                        sp.dma_start(ring[:, s], mod_v[bass.ds(l, 1), q, :, :, j * D:(j + 1) * D]
                                     .rearrange("a p k c -> (a p) k c")).then_inc(loaded[s], 16)
            with sp.Fori(0, L) as l:
                for j, slab in enumerate((2, 0, 1)):
                    if j == 1:
                        sp.wait_ge(rows_read, l + 1)
                        sp.sem_inc(tick, 1)
                    for q in range(UQ):
                        s = j * UQ + q
                        sp.wait_ge(freed[s], unit_uses(s, l, 0))
                        sp.sem_inc(tick, 1)
                        sp.dma_start(ring[:, s], in_v[bass.ds(l, 1), q, :, :, slab * D:(slab + 1) * D]
                                     .rearrange("a p k c -> (a p) k c")).then_inc(loaded[s], 16)
                for j in range(3):
                    for q in range(UQ):
                        s = j * UQ + q
                        sp.wait_ge(freed[s], unit_uses(s, l, 1))
                        sp.sem_inc(tick, 1)
                        sp.dma_start(ring[:, s], mod_v[bass.ds(l, 1), q, :, :, (3 + j) * D:(4 + j) * D]
                                     .rearrange("a p k c -> (a p) k c")).then_inc(loaded[s], 16)
                for q in range(UQ):
                    sp.wait_ge(freed[q], unit_uses(q, l, 2))
                    sp.sem_inc(tick, 1)
                    sp.dma_start(ring[:, q], out_v[bass.ds(l, 1), q].rearrange("a p k c -> (a p) k c")).then_inc(loaded[q], 16)
                with sp.Fori(0, E) as e:
                    for j in range(3):
                        for q in range(UQ):
                            s = j * UQ + q
                            sp.wait_ge(freed[s], l * PER_LAYER[s] + e + (SETUP_USES + PRE[s] + FREE0))
                            sp.sem_inc(tick, 1)
                            sp.dma_start(ring[:, s], exp_v[j][bass.ds(l * E + e, 1), q]
                                         .rearrange("a p k c -> (a p) k c")).then_inc(loaded[s], 16)
            yp = y_prompt[0].rearrange("(r p) d -> p r d", p=P)
            sp.wait_ge(fin_cp, 6)
            sp.dma_start(yp, x_tok[:, 0:2, :]).then_inc(y_out, 16)
            sp.dma_start(y_sample.rearrange("b t d -> (b t) d"), x_tok[0:NS, 2, :]).then_inc(y_out, 16)
            sp.wait_ge(y_out, 32)

        @block.tensor
        def _(pe):
            def mm(out, lhsT, rhs, start, stop):
                return nc.tensor.matmul(out, lhsT, rhs, start=start, stop=stop, skip_group_check=True)

            def tr(out, in_, n):
                return nc.tensor.transpose(out, in_, ident[0:n, 0:n])

            for s in range(NSLOT):
                pe.sem_inc(freed[s], 1)
            pe.wait_ge(in_const, 16)
            pe.wait_ge(c_act, 1)
            for k in range(KC):
                last = tr(ps[:, 2, k * 16:k * 16 + NC], c_tok[0:NC, k * P:(k + 1) * P], NC)
            last.then_inc(c_trans, 1)
            pe.wait_ge(in_rows, 16 * 10)
            for l in range(L):
                tr(ps[:, 0, l * P:l * P + NROWS], vrows[0:NROWS, l, :], NROWS)
                last = tr(ps[:, 1, l * P:l * P + TAPS * CT], wcrows[0:TAPS * CT, l, :], TAPS * CT)
            last.then_inc(rows_trans, 1)
            pe.wait_ge(in_x, 48)
            for k in range(KC):
                if k >= 2:
                    pe.wait_ge(x_copied, k - 1)
                for t0, n in TILES:
                    last = tr(ps[:, 6 + k % 2, t0:t0 + n], x_tok[0:n, t0 // P, k * P:(k + 1) * P], n)
                last.then_inc(x_trans, 1)
            pe.wait_ge(cond_ready, 1)
            pe.wait_ge(rows_copied, 2)
            pe.sem_inc(fold_done, 3)

            def mod_slab(bank, j, loads):
                for q in range(UQ):
                    s = j * UQ + q
                    pe.wait_ge(loaded[s], loads(s))
                    for kk in range(UK):
                        for nh in range(2):
                            t = 32 * (kk * 2 + nh)
                            last = mm(ps[t:t + 32, bank, :], condT[:, q * UK + kk, :], ring[:, s, kk, nh * 512:nh * 512 + 512],
                                      q == 0, q == UQ - 1)
                    last.then_inc(freed[s], 1)

            def mod_folds(bank, c0, src):
                for m in range(4):
                    last = mm(ps[:, bank, c0 + m * 2 * NC:c0 + (m + 1) * 2 * NC], src[:, m * P:(m + 1) * P], C("fold"), True, True)
                return last

            with pe.Fori(0, L) as r:
                for j in range(3):
                    pe.wait_ge(mod_evac, r * 3 + j + 1)
                    mod_slab(j, j, lambda s: r * 16 + 16)
                    pe.drain().then_inc(mod_done, 1)
                    pe.wait_ge(mod_evac, r * 3 + j + 4)
                    pe.wait_ge(mod_added, r * 3 + j + 1)
                    mod_folds(3 + j, 0, modS[:, j, :]).then_inc(fold_done, 1)
            pe.wait_ge(mod_added, 3 + 3 * L)
            pe.wait_ge(x_copied, KC)
            pe.wait_ge(in_wr, 32)

            def feature_sum(bank, src, n, width=T):
                for k in range(n):
                    last = mm(ps[:, bank, 0:width], ones, src[:, k, :], k == 0, k == n - 1)
                return last

            with pe.Fori(0, L) as l:
                pe.wait_ge(cb_loaded, l * 16 + 16)
                for ct in range(CT):
                    for r in range(2):
                        last = tr(ps[:, 4 + ct // 2, (ct % 2) * 240 + r * 120:(ct % 2) * 240 + r * 120 + 120],
                                  cbt[0:120, r, ct * P:(ct + 1) * P], 120)
                    last.then_inc(V.cb_trans, 1)
                pe.wait_ge(V.norm_sq, 1)
                feature_sum(6, big, KC).then_inc(V.norm_sum, 1)
                pe.wait_ge(V.h_ready, 1)
                n = 0
                for j, cols in enumerate(([0, 4, 1, 5, 2, 6, 3, 7], range(8), range(8))):
                    for q in range(UQ):
                        s = j * UQ + q
                        pe.wait_ge(loaded[s], l * (16 * PER_LAYER[s]) + 16 * (SETUP_USES + 1))
                    for m in cols:
                        if n >= 4:
                            if n - 4 >= 8:
                                pe.wait_ge(V.proj_copied, n - 4 - 8 + 1)
                            elif n % 2 == 0:
                                pe.wait_ge(V.a_ready, (n - 4) // 2 + 1)
                            else:
                                pe.wait_ge(V.z_sig, (n - 4) // 2 + 1)
                        for k in range(KC):
                            last = mm(ps[:, n % 4, 0:T], ring[:, j * UQ + k // UK, k % UK, m * P:(m + 1) * P], hT[:, k, :],
                                      k == 0, k == KC - 1)
                            if m == cols[-1] and k % UK == UK - 1 and k < KC - 1:
                                last.then_inc(freed[j * UQ + k // UK], 1)
                            if n in (8, 16) and k == 0:
                                last.then_inc(freed[j * UQ - 1], 1)
                        last.then_inc(V.inproj_done, 1)
                        n += 1
                    if j == 1:
                        pe.wait_ge(V.a_ready, 4)
                        pe.wait_ge(V.cb_copied, 4)
                        for ct in range(CT):
                            tr(ps[0:HIST, 4, ct * P:(ct + 1) * P], fullv[:, ct, FRING - HIST:FRING], P)
                        for ct in range(CT):
                            last = tr(ps[0:NS, 5, ct * P:(ct + 1) * P], rtmp[:, ct, :], P)
                        last.then_inc(V.a_trans, 1)
                for t, bank in enumerate((3, 7, 2)):
                    t0, m = TILES[t]
                    pe.wait_ge(V.proj_copied, 16)
                    for h in range(H):
                        last = tr(ps[0:m, bank, h * P:(h + 1) * P], proj[:, 8 + h, t0:t0 + m], P)
                        if t == 0 and h == 0:
                            last.then_inc(freed[3 * UQ - 1], 1)
                    last.then_inc(V.v_trans, 1)
                pe.wait_ge(V.conv_ready, 1)
                pe.wait_ge(V.sconv_ready, 1)
                feature_sum(6, cT, CT).then_inc(V.ln_sum, 1)
                pe.wait_ge(V.rot_ready, 1)
                pe.wait_ge(V.atok_copied, 2)
                for c in range(2):
                    for h in range(H):
                        last = mm(ps[:, 4 + c, h * P:(h + 1) * P], proj[:, 4 + h, c * P:(c + 1) * P], proj[:, h, c * P:(c + 1) * P],
                                  True, True)
                    last.then_inc(V.score_done, 1)
                for h in range(H):
                    last = mm(ps[0:NS, 0, h * NS:(h + 1) * NS], proj[:, 4 + h, SEQ:T], proj[:, h, SEQ:T], True, True)
                last.then_inc(V.score_done, 1)
                pe.wait_ge(V.ln_centered, 1)
                pe.wait_ge(V.sc_ready, 3)
                for t, bank in enumerate((0, 1, 6)):
                    t0, m = TILES[t]
                    for h in range(H):
                        last = tr(ps[0:m, bank, h * P:(h + 1) * P], proj[:, 4 + h, t0:t0 + m], P)
                    last.then_inc(V.k_trans, 1)
                pe.wait_ge(V.v_copied, 3)
                for c, bank in enumerate((3, 7)):
                    pe.wait_ge(V.kd_ready, c + 1)
                    for h in range(H):
                        last = mm(ps[:, bank, h * P:(h + 1) * P], kd[:, c, h * P:(h + 1) * P], vt[:, c, h * P:(h + 1) * P], True, True)
                    last.then_inc(V.st_done, 1)
                pe.wait_ge(V.ln_sq, 1)
                feature_sum(2, lnsq, CT).then_inc(V.ln_var, 1)
                pe.wait_ge(V.kd_ready, 3)
                for j in range(2):
                    mod_slab(j, j, lambda s: l * (16 * PER_LAYER[s]) + 16 * (SETUP_USES + 2))
                pe.drain().then_inc(V.mod2_done, 1)
                pe.wait_ge(V.s1_copied, 1)
                pe.wait_ge(V.sf_ready, 1)
                pe.wait_ge(V.qd_ready, 1)

                def head_output(h):
                    bank = 4 + h % 2
                    if h >= 2:
                        pe.wait_ge(V.o_copied, h - 1)
                    hp = slice(h * P, (h + 1) * P)
                    mm(ps[:, bank, 0:P], vt[:, 0, hp], sc[:, 0, hp], True, False)
                    mm(ps[:, bank, P:2 * P], vt[:, 1, hp], sc[:, 1, hp], False, False)
                    mm(ps[:, bank, P:2 * P], s1[:, hp], qd[:, h, 0:P], False, False)
                    mm(ps[:, bank, SEQ:T], vt[0:NS, 2, hp], scs[0:NS, h * NS:(h + 1) * NS], False, False)
                    pe.wait_ge(V.Sa_loaded if h < 2 else V.Sb_loaded, 32)
                    for b in range(B):
                        last = mm(ps[:, bank, SEQ + b * T_DEC:SEQ + (b + 1) * T_DEC], S_h[h][:, b * P:(b + 1) * P],
                                  qd[:, h, P + b * T_DEC:P + (b + 1) * T_DEC], False, b == B - 1)
                    last.then_inc(V.o_done, 1)

                def head_states(h):
                    hp = slice(h * P, (h + 1) * P)
                    pe.wait_ge(V.vmask_ready, h + 1)
                    if h >= 1:
                        pe.wait_ge(V.snew_ready, h)
                    for g in range(2):
                        last = mm(ps[:, g, :], kd[0:NS, 2, hp], vmask[0:NS, g * 512:(g + 1) * 512], True, True)
                    last.then_inc(V.snew_done, 1)

                def head_sum(h):
                    pe.wait_ge(V.o_copied, h + 1)
                    if h >= 2:
                        pe.wait_ge(V.gn_centered, h - 1)
                    mm(ps[:, SUM_BANK[h], 0:T], ones, oS[:, h, :], True, True).then_inc(V.gn_sum, 1)

                def head_squares(h):
                    pe.wait_ge(V.gn_sq, h + 1)
                    if h >= 1:
                        pe.wait_ge(V.var_ready, h + 1)
                    mm(ps[:, VAR_BANK[h], 0:T], ones, gn_sq[:, h, :], True, True).then_inc(V.gn_var, 1)

                def out_block(m, ks):
                    for k in ks:
                        last = mm(ps[:, OUT_BANK[m % 4], 0:T], ring[:, k // UK, k % UK, m * P:(m + 1) * P], hT[:, k, :],
                                  k == KC // 2, k == KC // 2 - 1)
                    return last

                CONV_K, RET_K = range(KC // 2, KC), range(0, KC // 2)
                head_output(0)
                head_output(1)
                pe.wait_ge(V.mod2_evac, 2)
                for j in range(2):
                    mod_folds(3, j * 128, kd[:, j, :]).then_inc(V.mod2_fold, 1)
                head_states(0)
                head_sum(0)
                head_output(2)
                pe.wait_ge(V.mod2_added, 2)
                head_sum(1)
                head_states(1)
                head_squares(0)
                head_output(3)
                head_sum(2)
                head_states(2)
                head_squares(1)
                head_sum(3)
                for q in range(UQ):
                    pe.wait_ge(loaded[q], l * (16 * PER_LAYER[q]) + 16 * (SETUP_USES + 3))
                pe.wait_ge(V.mix_conv, 1)
                head_squares(2)
                out_block(0, CONV_K)
                head_squares(3)
                head_states(3)
                out_block(1, CONV_K)
                pe.wait_ge(V.gn_centered, H)
                out_block(2, CONV_K)
                out_block(3, CONV_K)
                for m in range(4):
                    for k in RET_K:
                        if m == 0:
                            pe.wait_ge(V.gn_mixed, k + 1)
                        last = out_block(m, [k])
                    last.then_inc(V.outproj_done, 1)
                for m in range(4, KC):
                    pe.wait_ge(V.x_mid, m - 3)
                    out_block(m, CONV_K)
                    out_block(m, RET_K).then_inc(V.outproj_done, 1)
                pe.wait_ge(V.outproj_done, KC)
                for q in range(UQ):
                    pe.sem_inc(freed[q], 1)
                pe.wait_ge(V.norm2_sq, 1)
                feature_sum(6, big, KC).then_inc(V.norm2_sum, 1)
                pe.wait_ge(V.h2_ready, 1)
                for t, (t0, m) in enumerate(TILES):
                    for k in range(KC):
                        last = mm(ps[0:m, 4, t * E:(t + 1) * E], hT[:, k, t0:t0 + m], wr[:, k, :], k == 0, k == KC - 1)
                last.then_inc(V.logits_done, 1)
                n = 0
                for t, (t0, m) in enumerate(TILES):
                    for hf in range(2):
                        if n >= 4:
                            pe.wait_ge(V.h2_copied, n - 3)
                        for k in range(4):
                            last = tr(ps[0:m, n % 4, k * P:(k + 1) * P], hT[:, hf * 4 + k, t0:t0 + m], P)
                        last.then_inc(V.h2_trans, 1)
                        n += 1
                mod_slab(6, 2, lambda s: l * (16 * PER_LAYER[s]) + 16 * (SETUP_USES + 2))
                pe.drain().then_inc(V.mod2_done, 1)
                pe.wait_ge(V.m_ready, 1)
                M = rt[:, 10, :]
                for t in range(3):
                    for u in range(t + 1):
                        mm(ps[:, 5, t * E:(t + 1) * E], C("tri") if u == t else ones, M[:, u * E:(u + 1) * E], u == 0, u == t)
                for u in range(3):
                    last = mm(ps[:, 5, 3 * E:4 * E], ones, M[:, u * E:(u + 1) * E], u == 0, u == 2)
                last.then_inc(V.pos_done, 1)

                pe.wait_ge(V.mod2_evac, 3)
                mod_folds(7, 0, gs).then_inc(V.mod2_fold, 1)

                pe.wait_ge(V.h2_copied, 6)
                for sgn in (V.gathered, V.up_done, V.trans_done, V.down_done):
                    pe.sem_inc(sgn, 2)
                for sgn in (V.x_gath, V.x_gu, V.x_t, V.x_down):
                    pe.sem_inc(sgn, 1)

                def gather(selb, bank, free=None):
                    for k in range(KC):
                        for t, (t0, m) in enumerate(TILES):
                            last = mm(ps[:, bank, k * BLK:(k + 1) * BLK], h2tok[0:m, t, k * P:(k + 1) * P],
                                      selb[0:m, t * BLK:(t + 1) * BLK], t == 0, t == 2)
                            if free and k == 0 and t == 0:
                                last.then_inc(free, 1)
                    return last

                def half_products(bank, lhs, s0, free, unit):
                    for k in range(KC):
                        s = s0 + k // UK
                        if k % UK == 0:
                            unit(s)
                        for nh in range(2):
                            last = mm(ps[nh * 64:nh * 64 + 64, bank, :], lhs(k), ring[:, s, k % UK, nh * 512:nh * 512 + 512],
                                      k == 0, k == KC - 1)
                        if free and k % UK == UK - 1 and k < KC - 1:
                            last.then_inc(freed[s], 1)
                        if free and k == 0 and s0 == UQ:
                            last.then_inc(freed[UQ - 1], 1)
                    return last

                def transposes(bank, src):
                    for j in range(4):
                        last = tr(ps[:, bank, j * P:(j + 1) * P], src[:, j * P:(j + 1) * P], P)
                    return last

                def down_lhs(src):
                    return lambda k: src[:, (k % 4) * P + (k // 4) * BLK:(k % 4) * P + (k // 4) * BLK + BLK]

                pe.wait_ge(V.sel_ready, 1)
                gather(sel[:, 0, :], 1).then_inc(V.gathered, 1)
                pe.wait_ge(V.route_ready, 1)
                xn = pe.alloc_register("extra_blocks")
                pe.reg_mov(xn, 1)
                with pe.Fori(0, E // 2) as g:
                    for i in range(2):
                        def unit(s):
                            pe.wait_ge(loaded[s], l * (16 * PER_LAYER[s]) + g * 32 + 16 * (SETUP_USES + PRE[s] + i + 1))

                        nsub = pe.value_load(nsubi[0:1, bass.ds(g * 2 + i, 1)], min_val=1, max_val=MAXSUB)
                        xlo = pe.alloc_register(f"extra_first{i}")
                        pe.reg_mov(xlo, xn)
                        with pe.If(nsub > 1):
                            with pe.Fori(1, nsub):
                                pe.wait_ge(V.x_hs, xn)
                                pe.reg_add(xn, xn, 1)
                                pe.wait_ge(V.x_sel, xn)
                                gather(selx, 7).then_inc(V.x_gath, 1)
                                pe.wait_ge(V.x_xg, xn)
                                half_products(5, lambda k: xgx[:, k * BLK:(k + 1) * BLK], 0, False, unit)
                                half_products(6, lambda k: xgx[:, k * BLK:(k + 1) * BLK], UQ, False, unit).then_inc(V.x_gu, 1)
                                pe.wait_ge(V.x_h, xn)
                                transposes(7, hx).then_inc(V.x_t, 1)
                            pe.wait_ge(V.x_hs, xn)
                            pe.sem_inc(tick, 1)
                        pe.wait_ge(V.xg_copied, g * 2 + i + 1)
                        pe.wait_ge(V.h_act, g * 2 + i + 2)
                        last = half_products(2, lambda k: xg[:, i, k * BLK:(k + 1) * BLK], 0, True, unit)
                        last.then_inc(V.gate_done, 1)
                        last = half_products(3, lambda k: xg[:, i, k * BLK:(k + 1) * BLK], UQ, True, unit)
                        last.then_inc(V.up_done, 1)
                        pe.wait_ge(V.sel_ready, g * 2 + i + 2)
                        pe.wait_ge(V.xg_copied, g * 2 + i + 1)
                        gather(sel[:, (i + 1) % 2, :], 1, freed[2 * UQ - 1]).then_inc(V.gathered, 1)
                        pe.wait_ge(V.h_act, g * 2 + i + 3)
                        pe.wait_ge(V.hT_copied, g * 2 + i + 2)
                        transposes(4, hs).then_inc(V.trans_done, 1)
                        with pe.If(nsub > 1):
                            with pe.Fori(1, nsub):
                                pe.wait_ge(V.x_yc, xlo)
                                pe.reg_add(xlo, xlo, 1)
                                pe.wait_ge(V.x_h2, xlo)
                                half_products(7, down_lhs(h2x), 2 * UQ, False, unit).then_inc(V.x_down, 1)
                            pe.wait_ge(V.x_yc, xn)
                            pe.sem_inc(tick, 1)
                        pe.wait_ge(V.hT_copied, g * 2 + i + 3)
                        pe.wait_ge(V.y_copied, g * 2 + i + 2)
                        half_products(0, down_lhs(h2T), 2 * UQ, True, unit).then_inc(V.down_done, 1)
                        pe.wait_ge(V.down_done, g * 2 + i + 3)
                        pe.sem_inc(freed[3 * UQ - 1], 1)
                pe.wait_ge(V.comb_ready, 3)
                for k in range(KC):
                    if k >= 2:
                        pe.wait_ge(V.x_end, k - 1)
                    for t, (t0, m) in enumerate(TILES):
                        last = tr(ps[:, 2 + k % 2, t0:t0 + m], h2tok[0:m, t, k * P:(k + 1) * P], m)
                    last.then_inc(V.yt_trans, 1)
                pe.drain().then_inc(layer_done, 1)
                pe.wait_ge(layer_open, l + 1)
            pe.wait_ge(fin_sq, 1)
            feature_sum(6, big, KC).then_inc(fin_sum, 1)
            pe.wait_ge(fin_y, 1)
            n = 0
            for t, (t0, m) in enumerate(TILES):
                for hf in range(2):
                    if n >= 4:
                        pe.wait_ge(fin_cp, n - 3)
                    for k in range(4):
                        last = tr(ps[0:m, n % 4, k * P:(k + 1) * P], hT[:, hf * 4 + k, t0:t0 + m], P)
                    last.then_inc(fin_tr, 1)
                    n += 1

        @block.scalar
        def _(act):
            def a(out, in_, f=ACT.Copy, **kw):
                return nc.scalar.activation(out, in_, f, **kw)

            def root(buf):
                a(buf, buf, ACT.Sqrt).then_inc(V.rstd_ready, 1)

            act.dma_start(c_tok[0:1, :], c_prompt).then_inc(in_c, 16)
            act.dma_start(c_tok[1:NC, :], c_sample).then_inc(in_c, 16)
            act.dma_start(cst[:, :], consts).then_inc(in_const, 16)
            act.dma_start(x_tok[:, 0:2, :], x_prompt[0].rearrange("(r p) d -> p r d", p=P)).then_inc(in_x, 16)
            act.dma_start(x_tok[0:NS, 2, :], x_sample.rearrange("b t d -> (b t) d")).then_inc(in_x, 32)
            act.dma_start(wr[:, :, :], w_router.rearrange("(k p) e -> p k e", p=P)).then_inc(in_wr, 16)
            act.dma_start(brow[:, :], b_router.partition_broadcast(P)).then_inc(in_wr, 16)
            act.wait_ge(in_c, 32)
            a(c_sig[0:NC, :], c_tok[0:NC, :], ACT.Sigmoid).then_inc(c_sigd, 1)
            act.wait_ge(c_trans, 1)
            act.wait_ge(cpad, 1)
            a(condT[:, :, 0:NC], ps[:, 2, 0:KC * 16].rearrange("p (k c) -> p k c", k=KC)[:, :, 0:NC]).then_inc(cond_ready, 1)
            for k in range(0, KC):
                act.wait_ge(x_trans, k + 1)
                a(xT[:, k, :], ps[:, 6 + k % 2, 0:T]).then_inc(x_copied, 1)
            act.sem_inc(mod_evac, 3)
            with act.Fori(0, L) as r:
                for j in range(3):
                    act.wait_ge(mod_done, r * 3 + j + 1)
                    act.wait_ge(fold_done, r * 3 + j + 1)
                    a(modS[:, j, :], ps[:, j, :]).then_inc(mod_evac, 1)
            act.wait_ge(mod_added, 3 + 3 * L)
            act.wait_ge(rows_zeroed, 32)

            with act.Fori(0, L) as l:
                a(big[:, :, :], xT[:, :, :], ACT.Square).then_inc(V.norm_sq, 1)
                act.wait_ge(V.pad_ready, 1)
                for ct in range(CT):
                    act.wait_ge(V.cb_trans, ct // 2 * 2 + 2)
                    a(fullv[:, ct, FRING:].rearrange("p (b w) -> p b w", b=B)[:, :, 0:HIST],
                      ps[:, 4 + ct // 2, (ct % 2) * 240:(ct % 2) * 240 + 240].rearrange("p (b w) -> p b w", b=B)) \
                        .then_inc(V.cb_copied, 1)
                act.wait_ge(V.var_ready, 1)
                root(stat[:, 1, :])
                for i in range(4):
                    act.wait_ge(V.inproj_done, 2 * i + 2)
                    if i >= 2:
                        act.wait_ge(V.a_ready, i - 1)
                    a(zsig[:, i % 2, :], ps[:, (2 * i + 1) % 4, 0:T], ACT.Sigmoid).then_inc(V.z_sig, 1)
                for n in range(16):
                    act.wait_ge(V.inproj_done, 8 + n + 1)
                    a(proj[:, n, :], ps[:, n % 4, 0:T]).then_inc(V.proj_copied, 1)
                    if n == 11:
                        act.wait_ge(V.a_trans, 1)
                        a(atok[0:HIST, 0, :], ps[0:HIST, 4, :]).then_inc(V.atok_copied, 1)
                        a(atok[0:NS, 1, :], ps[0:NS, 5, :]).then_inc(V.atok_copied, 1)
                for t, bank in enumerate((3, 7, 2)):
                    m = TILES[t][1]
                    act.wait_ge(V.v_trans, t + 1)
                    a(vt[0:m, t, :], ps[0:m, bank, :]).then_inc(V.v_copied, 1)
                act.wait_ge(V.inproj_done, 24)
                act.wait_ge(V.ln_centered, 1)
                a(lnsq, cT, ACT.Square).then_inc(V.ln_sq, 1)
                act.wait_ge(V.proj_copied, 16)
                a(gsig, proj[:, 12:16, :], ACT.Sigmoid).then_inc(V.g_sig, 1)
                act.wait_ge(V.st_done, 1)
                a(s1, ps[:, 3, :]).then_inc(V.s1_copied, 1)
                act.wait_ge(V.var_ready, 2)
                root(stat[:, 1, :])
                act.wait_ge(V.ln_scaled, 1)
                act.wait_ge(V.ln_var, 1)
                for ct in range(CT):
                    last = a(lnsq[:, ct, :], cT[:, ct, :], ACT.Sigmoid, scale=vec[:, R_GCLN + ct:R_GCLN + ct + 1],
                             bias=vec[:, R_BCLN + ct:R_BCLN + ct + 1])
                last.then_inc(V.ln_sig, 1)
                act.wait_ge(V.mod2_done, 1)
                act.wait_ge(V.st_done, 2)
                for j in range(2):
                    a(kd[:, j, :], ps[:, j, :]).then_inc(V.mod2_evac, 1)

                def copy_head(h):
                    act.wait_ge(V.o_done, h + 1)
                    a(oS[:, h, :], ps[:, 4 + h % 2, 0:T]).then_inc(V.o_copied, 1)

                def square_head(h):
                    act.wait_ge(V.gn_centered, h + 1)
                    a(gn_sq[:, h, :], oS[:, h, :], ACT.Square).then_inc(V.gn_sq, 1)

                def root_head(h):
                    act.wait_ge(V.var_ready, 3 + h)
                    root(gn_rstd[:, h, :])

                act.wait_ge(V.mix_conv, 1)
                copy_head(0)
                copy_head(1)
                square_head(0)
                copy_head(2)
                square_head(1)
                root_head(0)
                copy_head(3)
                square_head(2)
                root_head(1)
                square_head(3)
                root_head(2)
                root_head(3)
                act.wait_ge(V.x_mid, KC + 1)
                act.wait_ge(V.states_stored, 64)
                a(big[:, :, :], xT[:, :, :], ACT.Square).then_inc(V.norm2_sq, 1)
                act.wait_ge(V.var_ready, 3 + H)
                root(stat[:, 1, :])
                n = 0
                for t, (t0, m) in enumerate(TILES):
                    for hf in range(2):
                        act.wait_ge(V.h2_trans, n + 1)
                        a(h2tok[0:m, t, hf * 512:hf * 512 + 512], ps[0:m, n % 4, :]).then_inc(V.h2_copied, 1)
                        n += 1
                act.wait_ge(V.lg_ready, 1)
                a(rt[:, 1, :], rt[:, 0, :], ACT.Exp).then_inc(V.ex_ready, 1)
                act.wait_ge(V.mod2_done, 2)
                a(gs, ps[:, 6, :]).then_inc(V.mod2_evac, 1)

                act.wait_ge(V.route_ready, 1)
                act.wait_ge(V.sf_stored, 16)
                act.sem_inc(V.y_copied, 2)
                for sgn in y_stored:
                    act.sem_inc(sgn, 16)
                for sgn in (V.x_sig, V.x_yc):
                    act.sem_inc(sgn, 1)
                act.wait_ge(V.gathered, 3)
                a(xg[:, 0, :], ps[:, 1, :]).then_inc(V.xg_copied, 1)
                xn = act.alloc_register("extra_blocks")
                act.reg_mov(xn, 1)
                x16 = act.alloc_register("extra_stored")
                act.reg_mov(x16, 0)
                with act.Fori(0, E // 2) as g:
                    for i in range(2):
                        nsub = act.value_load(nsubi[0:1, bass.ds(g * 2 + i, 1)], min_val=1, max_val=MAXSUB)
                        xlo = act.alloc_register(f"extra_first{i}")
                        act.reg_mov(xlo, xn)
                        with act.If(nsub > 1):
                            with act.Fori(1, nsub):
                                act.reg_add(xn, xn, 1)
                                act.wait_ge(V.x_gu, xn)
                                a(gsx, ps[:, 5, :], ACT.Sigmoid).then_inc(V.x_sig, 1)
                        act.wait_ge(V.gate_done, g * 2 + i + 1)
                        act.wait_ge(V.h_act, g * 2 + i + 2)
                        a(gs, ps[:, 2, :], ACT.Sigmoid).then_inc(V.sig_done, 1)
                        act.wait_ge(V.gathered, g * 2 + i + 4)
                        act.wait_ge(V.up_done, g * 2 + i + 2)
                        a(xg[:, (i + 1) % 2, :], ps[:, 1, :]).then_inc(V.xg_copied, 1)
                        with act.If(nsub > 1):
                            with act.Fori(1, nsub) as s:
                                act.reg_add(xlo, xlo, 1)
                                act.wait_ge(V.x_down, xlo)
                                a(yx, ps[:, 7, :]).then_inc(V.x_yc, 1)
                                act.wait_ge(V.x_yc, xlo)
                                row = act.snap(act.snap(xlo) * BLK + (E - 2) * BLK, min_val=0, max_val=YROWS - BLK)
                                for hf in range(2):
                                    act.dma_start(ydram[bass.ds(row, BLK), hf * 512:hf * 512 + 512],
                                                  yx[hf * 64:hf * 64 + 64, :]).then_inc(V.x_st, 16)
                                act.reg_add(x16, x16, 32)
                                act.wait_ge(V.x_st, x16)
                                act.sem_inc(tick, 1)
                        act.wait_ge(V.down_done, g * 2 + i + 3)
                        act.wait_ge(y_stored[i], g * 32 + 16)
                        a(ysb[:, i, :], ps[:, 0, :]).then_inc(V.y_copied, 1)
                        act.wait_ge(V.y_copied, g * 2 + i + 3)
                        for hf in range(2):
                            act.dma_start(ydram[bass.ds(g * (2 * BLK) + i * BLK, BLK), hf * 512:hf * 512 + 512],
                                          ysb[hf * 64:hf * 64 + 64, i, :]).then_inc(y_stored[i], 16)
                act.drain().then_inc(layer_done, 1)
                act.wait_ge(layer_open, l + 1)
            a(big[:, :, :], xT[:, :, :], ACT.Square).then_inc(fin_sq, 1)
            act.wait_ge(fin_rs, 2)
            a(stat[:, 1, :], stat[:, 1, :], ACT.Sqrt).then_inc(fin_rs, 1)
            n = 0
            for t, (t0, m) in enumerate(TILES):
                for hf in range(2):
                    act.wait_ge(fin_tr, n + 1)
                    a(x_tok[0:m, t, hf * 512:hf * 512 + 512], ps[0:m, n % 4, :]).then_inc(fin_cp, 1)
                    n += 1

        @block.vector
        def _(dve):
            v = nc.vector

            def bc(ap2, n):
                return ap2.unsqueeze(1).to_broadcast([ap2.shape[0], n, ap2.shape[1]])

            def bl(ap2, n):
                return ap2.unsqueeze(2).to_broadcast([ap2.shape[0], ap2.shape[1], n])

            v.memset(condT[:, :, :], 0.0).then_inc(cpad, 1)
            dve.wait_ge(c_sigd, 1)
            v.tensor_tensor(c_tok[0:NC, :], c_tok[0:NC, :], c_sig[0:NC, :], ALU.mult).then_inc(c_act, 1)
            dve.wait_ge(rows_trans, 1)
            v.tensor_copy(vecT[:, :, :], ps[:, 0, 0:L * P].rearrange("p (l r) -> p l r", l=L)[:, :, 0:NROWS]).then_inc(rows_copied, 1)
            v.tensor_copy(wcT[:, :, :], ps[:, 1, 0:L * P].rearrange("p (l r) -> p l r", l=L)[:, :, 0:TAPS * CT]).then_inc(rows_copied, 1)
            dve.wait_ge(rows_copied, 2)
            dve.sem_inc(mod_added, 3)
            with dve.Fori(0, L) as l:
                for j in range(3):
                    dve.wait_ge(fold_done, l * 3 + j + 4)
                    o = modT[:, bass.ds(l, 1), j * KC:(j + 1) * KC, :].rearrange("p a (n m) c -> p (a n) m c", n=2)
                    bm = vecT[:, bass.ds(l, 1), R_BMOD + j * KC:R_BMOD + (j + 1) * KC].rearrange("p a (n m) -> p (a n) m", n=2)
                    src = ps[:, 3 + j, 0:8 * NC].rearrange("p (m n c) -> p n m c", m=4, n=2)
                    v.tensor_tensor(o, src, bm.unsqueeze(3).to_broadcast([P, 2, 4, NC]), ALU.add).then_inc(mod_added, 1)
            dve.wait_ge(mod_added, 3 + 3 * L)
            dve.wait_ge(in_const, 16)
            dve.wait_ge(x_copied, KC)

            def inverse_var(ch, dst, src, n):
                ch.link(v.tensor_scalar(dst, src, 1.0 / n, EPS, ALU.mult, ALU.add))
                v.reciprocal(dst, dst).then_inc(V.var_ready, 1)

            def modulated(ch, bank, sh, sca, nth, done):
                inverse_var(ch, stat[:, 1, :], ps[:, bank, 0:T], D)
                dve.wait_ge(V.rstd_ready, nth)
                ch.link(v.tensor_tensor(hT[:, :, :], xT[:, :, :], bc(stat[:, 1, :], KC), ALU.mult))
                smp = hT[:, :, SEQ:T].rearrange("p k (b t) -> p k b t", b=B)
                ch.link(v.tensor_tensor(smp, smp, mod[:, sca:sca + KC, 1:NC].unsqueeze(3).to_broadcast([P, KC, B, T_DEC]), ALU.mult))
                v.tensor_tensor(smp, smp, mod[:, sh:sh + KC, 1:NC].unsqueeze(3).to_broadcast([P, KC, B, T_DEC]), ALU.add)
                for k in range(KC):
                    last = v.tensor_scalar(hT[:, k, 0:SEQ], hT[:, k, 0:SEQ], mod[:, sca + k, 0:1], mod[:, sh + k, 0:1],
                                           ALU.mult, ALU.add)
                last.then_inc(done, 1)

            def add_gated(ch, bank_of, gt, arrived, done):
                for m in range(KC):
                    dve.wait_ge(arrived, m + 1)
                    src = ps[:, bank_of(m), :]
                    v.tensor_tensor(rtmp[:, m, :].rearrange("p (b t) -> p b t", b=B), src[:, SEQ:T].rearrange("p (b t) -> p b t", b=B),
                                    bl(mod[:, gt + m, 1:NC], T_DEC), ALU.mult)
                    v.scalar_tensor_tensor(xT[:, m, 0:SEQ], src[:, 0:SEQ], mod[:, gt + m, 0:1], xT[:, m, 0:SEQ],
                                           ALU.mult, ALU.add).then_inc(done, 1)
                dve.wait_ge(done, KC)
                v.tensor_tensor(xT[:, :, SEQ:T], xT[:, :, SEQ:T], rtmp[:, :, :], ALU.add).then_inc(done, 1)

            with dve.Fori(0, L) as l:
                ch = Chain(dve, V.dchain)
                v.tensor_copy(vec[:, :], vecT[:, bass.ds(l, 1), :].rearrange("p a r -> p (a r)"))
                v.tensor_copy(wc[:, :], wcT[:, bass.ds(l, 1), :].rearrange("p a r -> p (a r)"))
                v.memset(fullv[:, :, 0:HIST], 0.0).then_inc(V.pad_ready, 1)
                ch.link(v.tensor_copy(mod[:, 0:NMB // 2, :], modT[:, bass.ds(l, 1), :, :].rearrange("p a m c -> p (a m) c")))
                def add_mod_bias(bank, c0, j):
                    o = mod[:, j * KC:(j + 1) * KC, :].rearrange("p (n m) c -> p n m c", n=2)
                    bm = vec[:, R_BMOD + j * KC:R_BMOD + (j + 1) * KC].rearrange("p (n m) -> p n m", n=2)
                    src = ps[:, bank, c0:c0 + 8 * NC].rearrange("p (m n c) -> p n m c", m=4, n=2)
                    return v.tensor_tensor(o, src, bm.unsqueeze(3).to_broadcast([P, 2, 4, NC]), ALU.add)

                def scale_to_gain(sca, gain):
                    return v.scalar_tensor_tensor(mod[:, sca:sca + KC, :], mod[:, sca:sca + KC, :], 1.0,
                                                  bl(vec[:, gain:gain + KC], NC), ALU.add, ALU.mult)

                ch.link(scale_to_gain(M_SC1, R_GMIX))
                dve.sem_inc(V.vectors_ready, 1)
                dve.wait_ge(V.norm_sum, 1)
                modulated(ch, 6, M_SH1, M_SC1, 1, V.h_ready)
                for i in range(4):
                    dve.wait_ge(V.z_sig, i + 1)
                    src = ps[:, (2 * i) % 4, :]
                    dve.wait_ge(V.inproj_done, 2 * i + 1)
                    v.tensor_tensor(fullv[:, i, HIST:FRING], src[:, 0:SEQ], zsig[:, i % 2, 0:SEQ], ALU.mult)
                    v.tensor_tensor(rtmp[:, i, :], src[:, SEQ:T], zsig[:, i % 2, SEQ:T], ALU.mult)
                    v.tensor_tensor(fullv[:, i, FRING:].rearrange("p (b w) -> p b w", b=B)[:, :, HIST:],
                                    src[:, SEQ:T].rearrange("p (b t) -> p b t", b=B),
                                    zsig[:, i % 2, SEQ:T].rearrange("p (b t) -> p b t", b=B), ALU.mult).then_inc(V.a_ready, 1)
                dve.wait_ge(V.a_ready, 4)
                base = ch.n
                for tap in range(TAPS):
                    for ct in range(CT):
                        wcol = wc[:, tap * CT + ct:tap * CT + ct + 1]
                        src = fullv[:, ct, tap:tap + SEQ]
                        if tap == 0:
                            ins = v.tensor_scalar(cT[:, ct, 0:SEQ], src, wcol, vec[:, R_BCONV + ct:R_BCONV + ct + 1], ALU.mult, ALU.add)
                        else:
                            dve.wait_ge(V.dchain, ch.n - CT + 1)
                            ins = v.scalar_tensor_tensor(cT[:, ct, 0:SEQ], src, wcol, cT[:, ct, 0:SEQ], ALU.mult, ALU.add)
                        ins.then_inc(V.dchain, 1)
                        ch.n += 1
                dve.wait_ge(V.dchain, ch.n)
                dve.sem_inc(V.conv_ready, 1)
                dve.wait_ge(V.proj_copied, 8)
                for c in range(2):
                    qk = proj[:, c * H:(c + 1) * H, :]
                    v.tensor_tensor(rot[0:64, :, :], qk[64:128], bc(C("sin")[64:128], H), ALU.mult)
                    ch.link(v.tensor_tensor(rot[64:128, :, :], qk[0:64], bc(C("sin")[0:64], H), ALU.mult))
                    ch.link(v.tensor_tensor(qk, qk, bc(C("cos"), H), ALU.mult))
                    last = v.tensor_tensor(qk, qk, rot, ALU.add)
                    if c == 0:
                        ch.link(last)
                last.then_inc(V.rot_ready, 1)
                dve.wait_ge(V.rot_ready, 1)
                v.tensor_tensor(qd, proj[:, 0:4, P:T], C("qdec").rearrange("p (h t) -> p h t", h=H), ALU.mult).then_inc(V.qd_ready, 1)
                dve.wait_ge(V.ln_sum, 1)
                ch.link(v.tensor_scalar(stat[:, 0, :], ps[:, 6, 0:T], 1.0 / D_CONV, None, ALU.mult))
                v.tensor_tensor(cT, cT, bc(stat[:, 0, :], CT), ALU.subtract).then_inc(V.ln_centered, 1)
                dve.wait_ge(V.atok_stored, 16)
                dve.wait_ge(V.hist_stored, 16 * (1 + B))
                for c in range(2):
                    dve.wait_ge(V.score_done, c + 1)
                    v.tensor_tensor(sc[:, c, :], ps[:, 4 + c, :], C("decay"), ALU.mult).then_inc(V.sc_ready, 1)
                dve.wait_ge(V.score_done, 3)
                v.tensor_tensor(scs[0:NS, :], ps[0:NS, 0, 0:H * NS], C("sdecay")[0:NS], ALU.mult).then_inc(V.sc_ready, 1)
                for t, bank in enumerate((0, 1, 6)):
                    m = TILES[t][1]
                    dve.wait_ge(V.k_trans, t + 1)
                    v.tensor_tensor(kd[0:m, t, :].rearrange("p (h d) -> p h d", h=H), ps[0:m, bank, :].rearrange("p (h d) -> p h d", h=H),
                                    bl(C("kdec")[0:m, t * H:(t + 1) * H], P), ALU.mult).then_inc(V.kd_ready, 1)
                dve.wait_ge(V.s1_copied, 1)
                dve.wait_ge(V.st_done, 2)
                for h in range(H):
                    hp = slice(h * P, (h + 1) * P)
                    last = v.scalar_tensor_tensor(sf[:, hp], s1[:, hp], CDEC_P[h], ps[:, 7, hp], ALU.mult, ALU.add)
                last.then_inc(V.sf_ready, 1)
                dve.wait_ge(V.ln_var, 1)
                inverse_var(ch, stat[:, 1, :], ps[:, 2, 0:T], D_CONV)
                dve.wait_ge(V.g_sig, 1)
                for h in range(H):
                    last = v.scalar_tensor_tensor(proj[:, 12 + h, :], proj[:, 12 + h, :], vec[:, R_GRET + h:R_GRET + h + 1],
                                                  gsig[:, h, :], ALU.mult, ALU.mult)
                ch.link(last)
                dve.wait_ge(V.rstd_ready, 2)
                v.tensor_tensor(cT, cT, bc(stat[:, 1, :], CT), ALU.mult).then_inc(V.ln_scaled, 1)
                dve.wait_ge(V.ln_sig, 1)
                for ct in range(CT):
                    last = v.tensor_scalar(cT[:, ct, :], cT[:, ct, :], vec[:, R_GCLN + ct:R_GCLN + ct + 1],
                                           vec[:, R_BCLN + ct:R_BCLN + ct + 1], ALU.mult, ALU.add)
                ch.link(last)
                dve.wait_ge(V.inproj_done, 24)
                v.tensor_tensor(hT[:, 4:8, :], cT, lnsq, ALU.mult).then_inc(V.mix_conv, 1)
                dve.wait_ge(V.mod2_fold, 2)
                for j in range(2):
                    add_mod_bias(3, j * 128, 3 + j).then_inc(V.mod2_added, 1)
                dve.wait_ge(V.mod2_added, 2)
                ch.link(scale_to_gain(M_SC2, R_GFFN))

                def center(h):
                    dve.wait_ge(V.gn_sum, h + 1)
                    v.scalar_tensor_tensor(oS[:, h, :], ps[:, SUM_BANK[h], 0:T], -1.0 / DH, oS[:, h, :],
                                           ALU.mult, ALU.add).then_inc(V.gn_centered, 1)

                def sample_state(h):
                    dve.wait_ge(V.snew_done, h + 1)
                    dve.wait_ge(V.o_done, h + 1)
                    for g in range(2):
                        part = S_h[h][:, g * 512:(g + 1) * 512]
                        last = v.scalar_tensor_tensor(part, part, CDEC_S[h], ps[:, g, :], ALU.mult, ALU.add)
                    last.then_inc(V.snew_ready, 1)

                def head_var(h):
                    dve.wait_ge(V.gn_var, h + 1)
                    inverse_var(ch, gn_rstd[:, h, :], ps[:, VAR_BANK[h], 0:T], DH)

                def head_mix(h):
                    dve.wait_ge(V.rstd_ready, 3 + h)
                    ch.link(v.tensor_tensor(oS[:, h, :], oS[:, h, :], gn_rstd[:, h, :], ALU.mult))
                    v.tensor_tensor(hT[:, h, :], oS[:, h, :], proj[:, 12 + h, :], ALU.mult).then_inc(V.gn_mixed, 1)

                center(0)
                sample_state(0)
                center(1)
                head_var(0)
                sample_state(1)
                center(2)
                head_var(1)
                head_mix(0)
                sample_state(2)
                center(3)
                head_var(2)
                head_mix(1)
                head_var(3)
                head_mix(2)
                sample_state(3)
                head_mix(3)
                add_gated(ch, lambda m: OUT_BANK[m % 4], M_GT1, V.outproj_done, V.x_mid)
                dve.wait_ge(V.norm2_sum, 1)
                modulated(ch, 6, M_SH2, M_SC2, 3 + H, V.h2_ready)

                def r3(n):
                    return rt[:, n, :].rearrange("p (t e) -> p t e", t=3)

                def r4(n):
                    return rt[:, n, :].rearrange("p (a e) -> p a e", e=EPG)

                def col(n, k=3):
                    return rt[:, n, 0:k]

                def over_e(ap, n=E):
                    return ap.unsqueeze(2).to_broadcast([P, ap.shape[1], n])

                def tt(o, x, y, op):
                    ch.link(v.tensor_tensor(o, x, y, op))

                dve.wait_ge(in_wr, 32)
                v.memset(posm[:, :, :], -1000.0)
                ch.link(v.memset(rt[:, 0, :], 0.0))
                dve.wait_ge(V.logits_done, 1)
                v.tensor_tensor(r3(0)[:, 0:2], ps[:, 4, 0:2 * E].rearrange("p (t e) -> p t e", t=2), bc(brow[:, :], 2), ALU.add)
                ch.link(v.tensor_tensor(r3(0)[0:NS, 2], ps[0:NS, 4, 2 * E:3 * E], brow[0:NS, :], ALU.add))
                ch.link(v.tensor_reduce(col(2), r3(0), AX.X, ALU.max))
                v.tensor_tensor(r3(0), r3(0), over_e(col(2)), ALU.subtract).then_inc(V.lg_ready, 1)
                dve.wait_ge(V.ex_ready, 1)
                ch.link(v.tensor_reduce(col(2), r3(1), AX.X, ALU.add))
                ch.link(v.reciprocal(col(2), col(2)))
                tt(r3(1), r3(1), over_e(col(2)), ALU.mult)
                pv = r4(1)
                hi, lo = rt[:, 3, 0:24].rearrange("p (a e) -> p a e", e=2), rt[:, 3, 24:48].rearrange("p (a e) -> p a e", e=2)
                v.tensor_tensor(hi, pv[:, :, 0:2], pv[:, :, 2:4], ALU.max)
                ch.link(v.tensor_tensor(lo, pv[:, :, 0:2], pv[:, :, 2:4], ALU.min))
                t1, t2, t3 = (rt[:, 4, k * 12:(k + 1) * 12] for k in range(3))
                v.tensor_tensor(t1, hi[:, :, 0], hi[:, :, 1], ALU.max)
                v.tensor_tensor(t2, hi[:, :, 0], hi[:, :, 1], ALU.min)
                ch.link(v.tensor_tensor(t3, lo[:, :, 0], lo[:, :, 1], ALU.max))
                tt(t2, t2, t3, ALU.max)
                tt(t1, t1, t2, ALU.add)
                gsc = t1.rearrange("p (t g) -> p t g", t=3)
                gm = rt[:, 5, 0:12].rearrange("p (t g) -> p t g", t=3)

                def first_of(score, key, onehot, width):
                    ch.link(v.tensor_reduce(col(2), score, AX.X, ALU.max))
                    tt(onehot, score, over_e(col(2), width), ALU.is_equal)
                    tt(onehot, onehot, bc(key, 3), ALU.mult)
                    ch.link(v.tensor_reduce(col(6), onehot, AX.X, ALU.max))
                    tt(onehot, onehot, over_e(col(6), width), ALU.is_equal)

                first_of(gsc, C("gkey"), gm, GROUPS)
                gme = rt[:, 5, 0:12].unsqueeze(2).to_broadcast([P, 12, EPG])
                tt(r4(7), pv, gme, ALU.mult)
                ch.link(v.tensor_scalar(rt[:, 5, 12:24], rt[:, 5, 0:12], -1.0, None, ALU.add))
                tt(r4(7), r4(7), rt[:, 5, 12:24].unsqueeze(2).to_broadcast([P, 12, EPG]), ALU.add)
                first_of(r3(7), C("ekey"), r3(8), E)
                ch.link(v.tensor_copy(col(11), col(2)))
                ch.link(v.scalar_tensor_tensor(rt[:, 7, :], rt[:, 8, :], -4.0, rt[:, 7, :], ALU.mult, ALU.add))
                first_of(r3(7), C("ekey"), r3(9), E)
                tt(col(12), col(11), col(2), ALU.add)
                ch.link(v.reciprocal(col(12), col(12)))
                v.tensor_tensor(wts[:, 0, :], col(11), col(12), ALU.mult)
                v.tensor_tensor(wts[:, 1, :], col(2), col(12), ALU.mult)
                tt(r3(10), r3(8), r3(9), ALU.add)
                v.tensor_tensor(r3(10), r3(10), over_e(C("valid")), ALU.mult).then_inc(V.m_ready, 1)
                dve.wait_ge(V.pos_done, 1)
                dve.wait_ge(V.m_ready, 1)
                ch.link(v.tensor_copy(rt[:, 13, :], ps[:, 5, 0:3 * E]))
                ch.link(v.tensor_copy(rt[:, 14, 0:E], ps[:, 5, 3 * E:4 * E]))
                ch.link(v.scalar_tensor_tensor(r3(3), r3(13), 1000.0, r3(10), ALU.add, ALU.mult))
                ch.link(v.tensor_scalar(posm[:, :, 0:E], r3(3), -1000.0, None, ALU.add))

                def select(dst, pos):
                    for t in range(3):
                        last = v.tensor_scalar(dst[:, t * BLK:(t + 1) * BLK], C("iota"), pos(t), None, ALU.is_equal)
                    return last

                dve.wait_ge(V.states_stored, 64)
                select(sel[:, 0, :], lambda t: posm[:, t, 0:1]).then_inc(V.sel_ready, 1)
                cnt, acc, xs, xt = rt[:, 14, 0:E], rt[:, 14, E:2 * E], rt[:, 14, 2 * E:3 * E], rt[:, 12, 0:E]
                ch.link(v.tensor_scalar(acc, cnt, float(BLK), 1.0, ALU.is_gt, ALU.add))
                for s in range(2, MAXSUB):
                    ch.link(v.scalar_tensor_tensor(acc, cnt, float(s * BLK), acc, ALU.is_gt, ALU.add))
                v.tensor_copy(nsubi[:, :], acc)
                ch.link(v.tensor_scalar(xs, acc, -1.0, None, ALU.add))
                for s in (1, 2, 4, 8):
                    ch.link(v.tensor_copy(xt, xs))
                    tt(xs[:, s:], xt[:, s:], xt[:, :E - s], ALU.add)
                ch.link(v.scalar_tensor_tensor(xs, acc, -1.0, xs, ALU.mult, ALU.add))
                ch.link(v.tensor_scalar(xs, xs, 1.0, float(BLK), ALU.add, ALU.mult))
                tt(xs, xs, C("xrow"), ALU.add)
                ch.link(v.tensor_scalar(r3(3), r3(13), BLK - 0.5, None, ALU.is_gt))
                tt(r3(3), r3(3), bc(xs, 3), ALU.mult)
                tt(r3(13), r3(13), bc(C("erow"), 3), ALU.add)
                tt(r3(13), r3(13), r3(3), ALU.add)
                for k in range(2):
                    tt(r3(3), r3(13), r3(8 + k), ALU.mult)
                    ch.link(v.tensor_reduce(col(15), r3(3), AX.X, ALU.add))
                    last = v.tensor_copy(rowi[:, k, :], col(15))
                    if k == 0:
                        ch.link(last)
                ch.link(last)
                dve.wait_ge(V.mod2_fold, 3)
                add_mod_bias(7, 0, 5).then_inc(V.route_ready, 1)
                dve.wait_ge(V.route_ready, 1)

                for sgn in (V.h_act, V.hT_copied):
                    dve.sem_inc(sgn, 2)
                for sgn in (V.x_sel, V.x_xg, V.x_gated, V.x_h, V.x_hs, V.x_h2):
                    dve.sem_inc(sgn, 1)

                xn = dve.alloc_register("extra_blocks")
                dve.reg_mov(xn, 1)
                with dve.Fori(0, E // 2) as g:
                    for i in range(2):
                        dve.wait_ge(V.gathered, g * 2 + i + 2)
                        select(sel[:, (i + 1) % 2, :], lambda t: posm[:, t, bass.ds(g * 2 + i + 1, 1)]).then_inc(V.sel_ready, 1)
                        nsub = dve.value_load(nsubi[0:1, bass.ds(g * 2 + i, 1)], min_val=1, max_val=MAXSUB)
                        xlo = dve.alloc_register(f"extra_first{i}")
                        dve.reg_mov(xlo, xn)
                        with dve.If(nsub > 1):
                            v.tensor_copy(posx[:, :].unsqueeze(2), posm[:, :, bass.ds(g * 2 + i, 1)]).then_inc(V.pchain, 1)
                            dve.drain()
                            with dve.Fori(1, nsub) as s:
                                dve.reg_add(xn, xn, 1)
                                v.tensor_scalar(posx[:, :], posx[:, :], -float(BLK), None, ALU.add)
                                dve.drain()
                                select(selx, lambda t: posx[:, t:t + 1]).then_inc(V.x_sel, 1)
                                dve.wait_ge(V.x_gath, xn)
                                v.tensor_copy(xgx, ps[:, 7, :]).then_inc(V.x_xg, 1)
                                dve.wait_ge(V.x_sig, xn)
                                v.tensor_tensor(hx, ps[:, 5, :], gsx, ALU.mult).then_inc(V.x_gated, 1)
                                dve.wait_ge(V.x_gated, xn)
                                v.tensor_tensor(hx, ps[:, 6, :], hx, ALU.mult).then_inc(V.x_h, 1)
                                dve.wait_ge(V.x_t, xn)
                                v.tensor_copy(hxs[:, bass.ds(s * 512 - 512, 512)], ps[:, 7, :]).then_inc(V.x_hs, 1)
                            dve.wait_ge(V.x_hs, xn)
                            dve.sem_inc(tick, 1)
                        dve.wait_ge(V.sig_done, g * 2 + i + 1)
                        dve.wait_ge(V.trans_done, g * 2 + i + 2)
                        v.tensor_tensor(hs, ps[:, 2, :], gs, ALU.mult).then_inc(V.gated, 1)
                        dve.wait_ge(V.gated, g * 2 + i + 1)
                        dve.wait_ge(V.up_done, g * 2 + i + 3)
                        v.tensor_tensor(hs, ps[:, 3, :], hs, ALU.mult).then_inc(V.h_act, 1)
                        dve.wait_ge(V.trans_done, g * 2 + i + 3)
                        dve.wait_ge(V.down_done, g * 2 + i + 2)
                        v.tensor_copy(h2T, ps[:, 4, :]).then_inc(V.hT_copied, 1)
                        with dve.If(nsub > 1):
                            with dve.Fori(1, nsub) as s:
                                dve.wait_ge(V.x_down, xlo)
                                dve.reg_add(xlo, xlo, 1)
                                v.tensor_copy(h2x, hxs[:, bass.ds(s * 512 - 512, 512)]).then_inc(V.x_h2, 1)
                for t, (t0, m) in enumerate(TILES):
                    dve.wait_ge(row_gathers[t], 32)
                    ch.link(v.tensor_scalar(h2tok[0:m, t, :], rows[t][0:m, 0, :], wts[0:m, 0, t:t + 1], None, ALU.mult))
                    v.scalar_tensor_tensor(h2tok[0:m, t, :], rows[t][0:m, 1, :], wts[0:m, 1, t:t + 1], h2tok[0:m, t, :],
                                           ALU.mult, ALU.add).then_inc(V.comb_ready, 1)
                add_gated(ch, lambda m: 2 + m % 2, M_GT2, V.yt_trans, V.x_end)
                dve.drain().then_inc(layer_done, 1)
                dve.wait_ge(layer_open, l + 1)
            dve.wait_ge(fin_sum, 1)
            v.tensor_scalar(stat[:, 1, :], ps[:, 6, 0:T], 1.0 / D, EPS, ALU.mult, ALU.add).then_inc(fin_rs, 1)
            dve.wait_ge(fin_rs, 1)
            v.reciprocal(stat[:, 1, :], stat[:, 1, :]).then_inc(fin_rs, 1)
            dve.wait_ge(fin_rs, 3)
            for k in range(KC):
                last = v.scalar_tensor_tensor(hT[:, k, :], xT[:, k, :], vecT[:, 0, R_GFIN + k:R_GFIN + k + 1], stat[:, 1, :],
                                              ALU.mult, ALU.mult)
            last.then_inc(fin_y, 1)

        @block.gpsimd
        def _(pool):
            gp = nc.gpsimd

            gp.memset(big[:, :, :], 0.0).then_inc(zeros_set, 1)
            pool.wait_ge(zeros_set, 1)
            zeros = big[:, :, :].rearrange("p a b -> p (a b)")[:, 0:MAXEXTRA // 2 * BLK * D // P]
            for k in range(2):
                r0 = E * BLK + k * (MAXEXTRA // 2) * BLK
                pool.dma_start(ydram[r0:r0 + MAXEXTRA // 2 * BLK, :].rearrange("(p r) d -> p (r d)", p=P), zeros).then_inc(rows_zeroed, 16)
            hist_v = state_conv.rearrange("l b t c -> l (b t) c").rearrange("l (r p) c -> l p r c", p=120)
            pool.dma_start(cbt[0:120, :, :], hist_v[0]).then_inc(cb_loaded, 16)
            pool.sem_inc(rows_read, 1)
            next_layer = pool.alloc_register("next_layer")
            pool.reg_mov(next_layer, 0)
            pool.wait_ge(mod_added, 3 + 3 * L)
            with pool.Fori(0, L) as l:
                pool.dma_start(conv_s[bass.ds(l, 1), :, 0:HIST - T_DEC, :].rearrange("a b t c -> (a b) (t c)"),
                               state_conv[bass.ds(l, 1), :, T_DEC:HIST, :].rearrange("a b t c -> (a b) (t c)")).then_inc(V.hist_stored, 16)
                ret_v = state_ret.rearrange("l b h d e -> l h d b e")
                rets_v = ret_s.rearrange("l b h d e -> l h d b e")

                def state(h):
                    return S_h[h].rearrange("p (b e) -> p b e", b=B)

                def dstate(v5, h):
                    return v5[bass.ds(l, 1), h].rearrange("a d b e -> (a d) b e")

                pool.wait_ge(V.norm_sum, 1)
                for h in (0, 1):
                    pool.dma_start(state(h), dstate(ret_v, h)).then_inc(V.Sa_loaded, 16)
                pool.wait_ge(V.vectors_ready, 1)
                pool.wait_ge(V.cb_copied, CT)
                pool.wait_ge(V.a_ready, CT)
                pc = Chain(pool, V.pchain)
                win = fullv[:, :, FRING:].rearrange("p c (b w) -> p c b w", b=B)
                slot = cprod.rearrange("p (k c s) -> p k c s", k=8, c=CT)
                flat = cprod.rearrange("p (k w) -> p k w", k=8)
                csum = cpsum.rearrange("p (c s) -> p c s", c=CT)
                for rnd in range(4):
                    for k in range(8):
                        tap = rnd * 8 + k
                        if tap < TAPS:
                            last = gp.tensor_tensor(slot[:, k].rearrange("p c (b t) -> p c b t", b=B), win[:, :, :, tap:tap + T_DEC],
                                                    wc[:, tap * CT:(tap + 1) * CT].unsqueeze(2).unsqueeze(3)
                                                    .to_broadcast([P, CT, B, T_DEC]), ALU.mult)
                        else:
                            last = gp.tensor_copy(slot[:, k], vec[:, R_BCONV:R_BCONV + CT].unsqueeze(2).to_broadcast([P, CT, NS]))
                    pc.link(last)
                    for half in (4, 2, 1):
                        if half == 1 and rnd == 0:
                            pc.link(gp.tensor_tensor(csum, slot[:, 0], slot[:, 1], ALU.add))
                        else:
                            pc.link(gp.tensor_tensor(flat[:, 0:half], flat[:, 0:half], flat[:, half:2 * half], ALU.add))
                    if rnd in (1, 2):
                        pc.link(gp.tensor_tensor(csum, csum, slot[:, 0], ALU.add))
                gp.tensor_tensor(cT[:, :, SEQ:T], csum, slot[:, 0], ALU.add).then_inc(V.sconv_ready, 1)
                pool.wait_ge(V.atok_copied, 2)
                pool.dma_start(conv_p[bass.ds(l, 1), 0].rearrange("a t c -> (a t) c"), atok[0:HIST, 0, :]).then_inc(V.atok_stored, 16)
                for b in range(B):
                    last = pool.dma_start(conv_s[bass.ds(l, 1), b, HIST - T_DEC:HIST, :].rearrange("a t c -> (a t) c"),
                                          atok[b * T_DEC:(b + 1) * T_DEC, 1, :])
                    last.then_inc(V.hist_stored, 16)
                pool.wait_ge(V.a_trans, 1)
                pool.wait_ge(V.sconv_ready, 1)
                pool.wait_ge(V.conv_ready, 1)
                for h in (2, 3):
                    pool.dma_start(state(h), dstate(ret_v, h)).then_inc(V.Sb_loaded, 16)
                pool.wait_ge(V.v_copied, 3)
                for h in range(H):
                    if h >= 1:
                        pool.wait_ge(V.snew_done, h)
                    gp.tensor_tensor(vmask[0:NS, :].rearrange("p (b e) -> p b e", b=B),
                                     vt[0:NS, 2, h * P:(h + 1) * P].unsqueeze(1).to_broadcast([NS, B, DH]),
                                     C("smask")[0:NS].unsqueeze(2).to_broadcast([NS, B, DH]), ALU.mult).then_inc(V.vmask_ready, 1)
                    if h == 0:
                        pool.wait_ge(V.sf_ready, 1)
                        pool.dma_start(ret_p[bass.ds(l, 1), 0].rearrange("a h d e -> (a d) h e"),
                                       sf.rearrange("p (h e) -> p h e", h=H)).then_inc(V.sf_stored, 16)
                    if h >= 1:
                        pool.wait_ge(V.snew_ready, h)
                        pool.dma_start(dstate(rets_v, h - 1), state(h - 1)).then_inc(V.states_stored, 16)
                pool.wait_ge(V.snew_ready, H)
                pool.dma_start(dstate(rets_v, H - 1), state(H - 1)).then_inc(V.states_stored, 16)
                pool.wait_ge(V.sf_stored, 16)
                with pool.If(l < L - 1):
                    pool.reg_add(next_layer, next_layer, 1)
                    nxt = pool.snap(pool.snap(next_layer) + 0, min_val=1, max_val=L - 1)
                    pool.dma_start(cbt[0:120, :, :], hist_v[bass.ds(nxt, 1)].rearrange("a p r c -> (a p) r c")).then_inc(cb_loaded, 16)
                pool.wait_ge(V.route_ready, 1)
                pool.wait_ge(V.y_copied, E + 2)
                pool.wait_ge(V.down_done, E + 2)
                for i in range(2):
                    pool.wait_ge(y_stored[i], 32 * (E // 2) + 16)
                pool.wait_ge(V.gathered, E + 3)
                pool.wait_ge(V.xg_copied, E + 1)
                for t, (t0, m) in enumerate(TILES):
                    for k in range(2):
                        gp.indirect_dma_start(rows[t][0:m, k, :], None, ydram[:, :],
                                              bass.IndirectOffsetOnAxis(ap=rowi[0:m, k, t:t + 1], axis=0)) \
                            .then_inc(row_gathers[t], 16)
                for sgn in row_gathers:
                    pool.wait_ge(sgn, 32)
                pool.sem_inc(rows_read, 1)
                pool.wait_ge(V.x_end, KC + 1)
                pool.wait_ge(layer_done, 3)
                pool.drain()
                pool.dma_reset(layer_sems)
                pool.sem_clear(layer_sems)
                pool.drain().then_inc(layer_open, 1)


_INS = ['x_prompt', 'x_sample', 'state_ret', 'state_conv', 'c_prompt', 'c_sample', 'w_mod', 'b_mod', 'g_mix_norm', 'w_in',
        'w_conv', 'b_conv', 'g_conv_ln', 'b_conv_ln', 'g_ret_gn', 'w_out', 'g_ffn_norm', 'w_router', 'b_router',
        'w_exp_gate', 'w_exp_up', 'w_exp_down', 'g_final']
_OUTS = [(1, SEQ, D), (B, T_DEC, D), (L, 1, H, DH, DH), (L, 1, HIST, D_CONV), (L, B, H, DH, DH), (L, B, HIST, D_CONV)]


def kernel(**inputs):
    import concourse.bacc as bacc
    from concourse.bass_utils import run_bass_kernel_spmd

    nc = bacc.Bacc("TRN2", target_bir_lowering=False, num_devices=1)
    arrays = {name: np.ascontiguousarray(inputs[name]) for name in _INS}
    arrays["consts"] = constants()
    args = [nc.dram_tensor(f"in_{n}", a.shape, mybir.dt.from_np(a.dtype), kind="ExternalInput").ap() for n, a in arrays.items()]
    args += [nc.dram_tensor(f"out_{i}", s, mybir.dt.float32, kind="ExternalOutput").ap() for i, s in enumerate(_OUTS)]
    hybrid_step_kernel(nc, *args)
    r = run_bass_kernel_spmd(nc, [{f"in_{n}": a for n, a in arrays.items()}], core_ids=[0])
    return tuple(r.results[0][f"out_{i}"] for i in range(len(_OUTS)))
```

```python
import math
from contextlib import ExitStack

import numpy as np

import concourse.bass as bass
from concourse import mybir

L, D, SEQ, B, T_DEC = 2, 1024, 256, 8, 4
NS = B * T_DEC
T = SEQ + NS
P = 128
KC = D // P
TILES = [(0, P), (P, P), (2 * P, NS)]
H, DH = 4, 128
D_RET, D_CONV = 512, 512
CT = D_CONV // P
TAPS, HIST = 31, 30
PAST = 2048
E, GROUPS, EPG = 16, 4, 4
BLK = 64
XBLK = 32
MAXSUB = 1 + -(-(T - BLK) // XBLK)
MAXEXTRA = max(min(n * (MAXSUB - 1), (2 * T - BLK * n - n) // XBLK + n) for n in range(1, 2 * T // BLK + 1))
XROWS = -(-MAXEXTRA * XBLK // 256) * 256
YROWS = 16 * BLK + XROWS
NC = 1 + B
NMOD = 6
EPS = 1e-6
NSLOT = 12
UK = 2
UQ = KC // UK
FRING = HIST + SEQ
SRING = HIST + T_DEC

R_GMIX, R_GFFN, R_BMOD, R_BCONV, R_GCLN, R_BCLN, R_GRET, R_GFIN, NROWS = 0, 8, 16, 64, 68, 72, 76, 80, 88
M_SH1, M_SC1, M_GT1, M_SH2, M_SC2, M_GT2 = 0, 8, 16, 24, 32, 40
NMB = NMOD * KC

LG = [math.log(1.0 - 2.0 ** (-5.0 - h)) for h in range(H)]
CDEC_P = [math.exp(P * g) for g in LG]
CDEC_S = [math.exp(T_DEC * g) for g in LG]

CONST = [("ident", 128), ("tri", 128), ("ones", 128), ("fold", 2 * NC), ("decay", 4 * 128), ("sdecay", 4 * NS),
         ("cos", T), ("sin", T), ("qdec", 4 * (P + NS)), ("kdec", 12), ("smask", B), ("iota", BLK),
         ("erow", E), ("xrow", E), ("ekey", E), ("gkey", GROUPS), ("valid", 3)]
COFF, _o = {}, 0
for _n, _w in CONST:
    COFF[_n] = (_o, _w)
    _o += _w
NCONST = _o


def constants():
    c = {}
    i = np.arange(P)
    c["ident"] = np.eye(P)
    c["tri"] = (i[:, None] < i[None, :]).astype(float)
    c["ones"] = np.ones((P, P))
    fold = np.zeros((P, 2, NC))
    for r in range(P):
        if r % 32 < NC:
            fold[r, (r // 32) % 2, r % 32] = 1.0
    c["fold"] = fold.reshape(P, -1)
    scale = DH ** -0.5
    rel = i[None, :] - i[:, None]
    c["decay"] = np.stack([np.where(rel >= 0, np.exp(np.maximum(rel, 0) * g), 0.0) * scale for g in LG], 1).reshape(P, -1)
    s = np.arange(NS)
    srel = s[None, :] - s[:, None]
    same = (s[None, :] // T_DEC == s[:, None] // T_DEC) & (srel >= 0)
    sd = np.zeros((P, 4, NS))
    for h, g in enumerate(LG):
        sd[:NS, h] = np.where(same, np.exp(np.maximum(srel, 0) * g), 0.0) * scale
    c["sdecay"] = sd.reshape(P, -1)
    half = DH // 2
    inv = (np.float32(10000.0) ** (-np.arange(half, dtype=np.float32) / np.float32(half))).astype(np.float32)
    pos = np.concatenate([np.arange(SEQ), PAST + s % T_DEC]).astype(np.float32)
    ang = (pos[None, :] * inv[:, None]).astype(np.float32).astype(np.float64)
    c["cos"] = np.concatenate([np.cos(ang), np.cos(ang)], 0)
    c["sin"] = np.concatenate([np.sin(ang), -np.sin(ang)], 0)
    qi = np.concatenate([np.arange(P) + 1, s % T_DEC + 1])
    c["qdec"] = np.broadcast_to(np.stack([np.exp(qi * g) for g in LG]).reshape(1, -1), (P, 4 * (P + NS)))
    kd = np.zeros((P, 3, 4))
    for h, g in enumerate(LG):
        kd[:, 0, h] = kd[:, 1, h] = np.exp((P - 1 - i) * g) * scale
        kd[:NS, 2, h] = np.exp((T_DEC - 1 - s % T_DEC) * g) * scale
    c["kdec"] = kd.reshape(P, -1)
    sm = np.zeros((P, B))
    sm[s, s // T_DEC] = 1.0
    c["smask"] = sm
    c["iota"] = np.broadcast_to(np.arange(BLK), (P, BLK))
    c["erow"] = np.broadcast_to(np.arange(E) * BLK, (P, E))
    c["xrow"] = np.broadcast_to(E * BLK - BLK - np.arange(E) * BLK, (P, E))
    c["ekey"] = np.broadcast_to(E - np.arange(E), (P, E))
    c["gkey"] = np.broadcast_to(GROUPS - np.arange(GROUPS), (P, GROUPS))
    v = np.ones((P, 3))
    v[NS:, 2] = 0.0
    c["valid"] = v
    return np.ascontiguousarray(np.concatenate([c[n] for n, _ in CONST], 1).astype(np.float32))


class Chain:

    def __init__(self, eng, sem):
        self.eng, self.sem, self.n = eng, sem, 0

    def link(self, ins):
        ins.then_inc(self.sem, 1)
        self.n += 1
        self.eng.wait_ge(self.sem, self.n)


def hybrid_step_kernel(nc, x_prompt, x_sample, state_ret, state_conv, c_prompt, c_sample, w_mod, b_mod, g_mix_norm,
                       w_in, w_conv, b_conv, g_conv_ln, b_conv_ln, g_ret_gn, w_out, g_ffn_norm, w_router, b_router,
                       w_exp_gate, w_exp_up, w_exp_down, g_final, consts,
                       y_prompt, y_sample, ret_p, conv_p, ret_s, conv_s):
    f32, i32, u32 = mybir.dt.float32, mybir.dt.int32, mybir.dt.uint32
    ALU, ACT, AX = mybir.AluOpType, mybir.ActivationFunctionType, mybir.AxisListType
    ctx = ExitStack()
    with ctx:
        def sb(name, shape, dt=f32):
            return ctx.enter_context(nc.sbuf_tensor(name, shape, dt))

        ring = sb("ring", [P, NSLOT, UK, D])
        xT = sb("xT", [P, KC, T])
        hT = sb("hT", [P, KC, T])
        big = sb("big", [P, KC, T])
        cst = sb("cst", [P, NCONST])
        vecT = sb("vecT", [P, L, NROWS])
        wcT = sb("wcT", [P, L, TAPS * CT])
        modT = sb("modT", [P, L, NMB // 2, NC])
        vec = sb("vec", [P, NROWS])
        wc = sb("wc", [P, TAPS * CT])
        mod = sb("mod", [P, NMB, NC])
        wr = sb("wr", [P, KC, E])
        brow = sb("brow", [P, E])
        condT = sb("condT", [P, KC, 32])
        stat = sb("stat", [P, 2, T])
        rt = sb("rt", [P, 16, 3 * E])
        posm = sb("posm", [P, 3, E + 1])
        wts = sb("wts", [P, 2, 3])
        rowi = sb("rowi", [P, 2, 3], u32)
        nsubi = sb("nsubi", [P, E], i32)
        posx = sb("posx", [P, 3])
        rtmp = sb("rtmp", [P, KC, NS])
        ARENA = 14976
        arena = sb("arena", [P, ARENA])
        ps = ctx.enter_context(nc.psum_tensor("ps", [P, 8, 512], f32))

        def C(name):
            o, w = COFF[name]
            return cst[:, o:o + w]

        ident = C("ident")
        ones = C("ones")
        used = {}

        def cut(phase, *dims):
            n = int(np.prod(dims))
            o = used.get(phase, 0)
            used[phase] = o + n
            assert o + n <= ARENA, (phase, o + n)
            v = arena[:, o:o + n]
            if len(dims) == 2:
                v = v.rearrange("p (a b) -> p a b", a=dims[0])
            elif len(dims) == 3:
                v = v.rearrange("p (a b c) -> p a b c", a=dims[0], b=dims[1])
            return v

        x_tok = cut("setup", 3, D)
        c_tok = cut("setup", D)
        c_sig = cut("setup", D)
        vrows = cut("setup", L, P)
        wcrows = cut("setup", L, P)
        modS = cut("setup", 3, 512)
        proj = cut("mix", 16, T)
        full = cut("mix", KC * T)
        fullv = full[:, 0:CT * (FRING + B * SRING)].rearrange("p (c w) -> p c w", c=CT)
        cT = cut("mix", CT, T)
        kd = cut("mix", 3, 512)
        vt = cut("mix", 3, 512)
        sc = cut("mix", 2, 512)
        scs = cut("mix", H * NS)
        s1 = cut("mix", 512)
        sf = cut("mix", 512)
        qd = cut("mix", H, P + NS)
        vmask = cut("mix", D)
        cpsum = scs
        cprod = vmask
        rot = kd.rearrange("p a b -> p (a b)")[:, 0:H * T].rearrange("p (h t) -> p h t", h=H)
        cbt = arena[:, used["mix"] - D - H * (P + NS) - 1024:used["mix"] - D - H * (P + NS)] \
            .rearrange("p (a b) -> p a b", a=2)
        cbt_start = used["mix"] - D - H * (P + NS) - 1024
        zsig = vt[:, 0:2, 0:T]
        atok = sc
        lnsq = hT[:, 4:8, :]
        gsig = hT[:, 0:4, :]
        oS = proj[:, 8:12, :]
        S_a = big[:, :, :].rearrange("p a b -> p (a b)")[:, 0:2 * B * DH]
        S_b = full[:, 0:2 * B * DH]
        gn_rstd, gn_sq = proj[:, 0:4, :], proj[:, 4:8, :]
        sq2 = proj[:, 0:8, :]
        modM = vmask.rearrange("p (a b) -> p a b", a=2)
        vmasks = [vmask, sc.rearrange("p a b -> p (a b)")]
        S_h = [S_a[:, 0:B * DH], S_a[:, B * DH:], S_b[:, 0:B * DH], S_b[:, B * DH:]]
        h2tok = cut("moe", 3, D)
        yg = cut("moe", 2, D)
        hxs = yg.rearrange("p a b -> p (a b)")
        after_yg = used["moe"]
        xg = cut("moe", 2, KC * BLK)
        gs = cut("moe", 512)
        assert used["mix"] >= used["moe"] >= 16 * T + 2 * B * DH
        sel = cut("moe", 2, 3 * BLK)
        hs = cut("moe", 512)
        h2T = cut("moe", 512)
        ysb = cut("moe", 2, 512)
        XW = KC * XBLK
        xgx = cut("moe", XW)
        gsx = cut("moe", XW)
        hx = cut("moe", XW)
        h2x = cut("moe", XW)
        yx = cut("moe", XW)
        selx = cut("moe", 3 * XBLK)
        assert (MAXSUB - 1) * XW <= 2 * D
        assert used["moe"] <= cbt_start
        rows = [yg, big[:, :, :].rearrange("p a b -> p (a b)")[:, 0:2 * D].rearrange("p (a b) -> p a b", a=2),
                arena[:, after_yg:after_yg + 2 * D].rearrange("p (a b) -> p a b", a=2)]

        HEAD_BANK, SUM_BANK, VAR_BANK, OUT_BANK = (4, 5, 2, 0), (3, 7, 4, 5), (1, 2, 0, 3), (7, 4, 5, 6)
        STATE_BANKS = ((0, 1), (2, 3))
        STATE_ORDER = (2, 3, 0, 1)

        ydram = nc.dram_tensor("expert_rows", (YROWS, D), f32, kind="Internal").ap()

        def sem(name):
            return ctx.enter_context(nc.semaphore(name))

        loaded = [sem(f"unit_loaded{s}") for s in range(NSLOT)]
        freed = [sem(f"unit_freed{s}") for s in range(NSLOT)]
        in_const, in_x, in_c, in_rows, in_wr = (sem(n) for n in ("in_const", "in_x", "in_c", "in_rows", "in_wr"))
        (rows_zeroed, zeros_set, cpad, c_sigd, c_act, c_trans, cond_ready, x_trans, x_copied, rows_trans, rows_copied, mod_done, mod_evac,
         fold_done, mod_added) = (sem(n) for n in (
             "rows_zeroed", "zeros_set", "cpad", "c_sigd", "c_act", "c_trans", "cond_ready", "x_trans", "x_copied", "rows_trans", "rows_copied",
             "mod_done", "mod_evac", "fold_done", "mod_added"))
        layer_open, y_out, fin_cp = (sem(n) for n in ("layer_open", "y_out", "fin_cp"))
        cb_loaded, rows_read, x_summed = sem("cb_loaded"), sem("rows_read"), sem("x_summed")
        tick = sem("tick")
        layer_done = sem("layer_done")
        names = """var_ready rstd_ready vectors_ready next_sq h_ready cb_trans cb_copied pad_ready
        inproj_done z_sig a_ready proj_copied conv_ready sconv_ready a_trans atok_copied atok_stored hist_stored rot_ready
        qd_ready ln_sum ln_centered ln_sq ln_var ln_scaled ln_sig mix_conv score_done sc_ready v_trans v_copied
        k_trans kd_ready g_sig st_done s1_copied sf_ready sf_stored Sa_loaded Sb_loaded vmask_ready snew_done
        snew_ready states_stored Sa_stored o_done o_copied gn_sum gn_centered gn_sq gn_var gn_mixed outproj_done x_mid
        norm2_sq norm2_sum h2_ready h2_trans h2_copied logits_done lg_ready ex_ready m_ready pos_done route_ready
        dchain pchain sel_ready gathered xg_copied gate_done up_done sig_done gated h_act trans_done hT_copied
        down_done y_copied y_stored0 y_stored1 x_sel x_gath x_xg x_gu x_sig x_gated x_h x_t x_hs x_h2 x_down x_yc x_st
        mod2_done mod2_evac mod2_fold mod2_added gath0 gath1 gath2 comb_ready yt_trans x_end""".split()
        S = {n: sem(n) for n in names}
        nums = [layer_done.num] + [S[n].num for n in names]
        assert nums == list(range(nums[0], nums[0] + len(nums)))
        layer_sems = range(nums[0], nums[-1] + 1)
        V = type("Signals", (), S)
        fin_rs, fin_y, fin_tr = V.var_ready, V.h_ready, V.h2_trans
        y_stored = [V.y_stored0, V.y_stored1]
        row_gathers = [V.gath0, V.gath1, V.gath2]
        block = ctx.enter_context(nc.Block())

        SETUP_USES = L * 3 * UQ // NSLOT
        PRE = [3 if s < UQ else 2 for s in range(NSLOT)]
        PER_LAYER = [p + E for p in PRE]

        FREE0 = 1

        def unit_uses(s, l, k):
            return l * PER_LAYER[s] + (SETUP_USES + k + FREE0)

        @block.sync
        def _(sp):
            mod_v = w_mod.rearrange("l (q k p) c -> l q p k c", q=UQ, p=P)
            in_v = w_in.rearrange("l (q k p) c -> l q p k c", q=UQ, p=P)
            out_v = w_out.rearrange("l (q k p) c -> l q p k c", q=UQ, p=P)
            exp_v = [w.rearrange("l e (q k p) c -> (l e) q p k c", q=UQ, p=P) for w in (w_exp_gate, w_exp_up, w_exp_down)]
            for row, n, src in ((R_GMIX, 8, g_mix_norm), (R_GFFN, 8, g_ffn_norm), (R_BMOD, NMB, b_mod), (R_BCONV, 4, b_conv),
                                (R_GCLN, 4, g_conv_ln), (R_BCLN, 4, b_conv_ln), (R_GRET, 4, g_ret_gn)):
                sp.dma_start(vrows[row:row + n, :, :], src.rearrange("l (r p) -> r l p", p=P)).then_inc(in_rows, 16)
            for l in range(L):
                sp.dma_start(vrows[R_GFIN:R_GFIN + 8, l, :], g_final.rearrange("(r p) -> r p", p=P)).then_inc(in_rows, 16)
            sp.dma_start(wcrows[0:TAPS * CT, :, :], w_conv.rearrange("l t (c p) -> (t c) l p", p=P)).then_inc(in_rows, 16)
            with sp.Fori(0, L) as l:
                for j in range(3):
                    for q in range(UQ):
                        s = j * UQ + q
                        sp.wait_ge(freed[s], l + 1)
                        sp.sem_inc(tick, 1)
                        sp.dma_start(ring[:, s], mod_v[bass.ds(l, 1), q, :, :, j * D:(j + 1) * D]
                                     .rearrange("a p k c -> (a p) k c")).then_inc(loaded[s], 16)
            with sp.Fori(0, L) as l:
                sp.wait_ge(rows_read, l + 1)
                sp.sem_inc(tick, 1)
                for j, slab in enumerate((2, 0, 1)):
                    for q in range(UQ):
                        s = j * UQ + q
                        sp.wait_ge(freed[s], unit_uses(s, l, 0))
                        sp.sem_inc(tick, 1)
                        sp.dma_start(ring[:, s], in_v[bass.ds(l, 1), q, :, :, slab * D:(slab + 1) * D]
                                     .rearrange("a p k c -> (a p) k c")).then_inc(loaded[s], 16)
                for j in range(3):
                    for q in range(UQ):
                        s = j * UQ + q
                        sp.wait_ge(freed[s], unit_uses(s, l, 1))
                        sp.sem_inc(tick, 1)
                        sp.dma_start(ring[:, s], mod_v[bass.ds(l, 1), q, :, :, (3 + j) * D:(4 + j) * D]
                                     .rearrange("a p k c -> (a p) k c")).then_inc(loaded[s], 16)
                for q in range(UQ):
                    sp.wait_ge(freed[q], unit_uses(q, l, 2))
                    sp.sem_inc(tick, 1)
                    sp.dma_start(ring[:, q], out_v[bass.ds(l, 1), q].rearrange("a p k c -> (a p) k c")).then_inc(loaded[q], 16)
                with sp.Fori(0, E) as e:
                    for j in range(3):
                        for q in range(UQ):
                            s = j * UQ + q
                            sp.wait_ge(freed[s], l * PER_LAYER[s] + e + (SETUP_USES + PRE[s] + FREE0))
                            sp.sem_inc(tick, 1)
                            sp.dma_start(ring[:, s], exp_v[j][bass.ds(l * E + e, 1), q]
                                         .rearrange("a p k c -> (a p) k c")).then_inc(loaded[s], 16)
            yp = y_prompt[0].rearrange("(r p) d -> p r d", p=P)
            for t in range(2):
                sp.wait_ge(fin_cp, 2 * t + 2)
                sp.dma_start(yp[:, t, :], x_tok[:, t, :]).then_inc(y_out, 16)
            sp.wait_ge(fin_cp, 6)
            sp.dma_start(y_sample.rearrange("b t d -> (b t) d"), x_tok[0:NS, 2, :]).then_inc(y_out, 16)
            sp.wait_ge(y_out, 48)

        @block.tensor
        def _(pe):
            def mm(out, lhsT, rhs, start, stop):
                return nc.tensor.matmul(out, lhsT, rhs, start=start, stop=stop, skip_group_check=True)

            def tr(out, in_, n):
                return nc.tensor.transpose(out, in_, ident[0:n, 0:n])

            for s in range(NSLOT):
                pe.sem_inc(freed[s], 1)
            pe.wait_ge(in_const, 16)
            pe.wait_ge(c_act, 1)
            for k in range(KC):
                last = tr(ps[:, 2, k * 16:k * 16 + NC], c_tok[0:NC, k * P:(k + 1) * P], NC)
            last.then_inc(c_trans, 1)
            pe.wait_ge(in_rows, 16 * 10)
            for l in range(L):
                tr(ps[:, 0, l * P:l * P + NROWS], vrows[0:NROWS, l, :], NROWS)
                last = tr(ps[:, 1, l * P:l * P + TAPS * CT], wcrows[0:TAPS * CT, l, :], TAPS * CT)
            last.then_inc(rows_trans, 1)
            pe.wait_ge(in_x, 48)
            for k in range(KC):
                if k >= 2:
                    pe.wait_ge(x_copied, k - 1)
                for t0, n in TILES:
                    last = tr(ps[:, 6 + k % 2, t0:t0 + n], x_tok[0:n, t0 // P, k * P:(k + 1) * P], n)
                last.then_inc(x_trans, 1)
            def feature_sum(bank, src, n, width=T, arrived=None):
                for k in range(n):
                    if arrived:
                        pe.wait_ge(arrived, k + 1)
                    last = mm(ps[:, bank, 0:width], ones, src[:, k, :], k == 0, k == n - 1)
                return last

            pe.wait_ge(x_copied, KC + 1)
            feature_sum(6, big, KC).then_inc(x_summed, 1)
            pe.wait_ge(cond_ready, 1)
            pe.wait_ge(rows_copied, 2)
            pe.sem_inc(fold_done, 3)

            def mod_slab(bank, j, loads):
                for q in range(UQ):
                    s = j * UQ + q
                    pe.wait_ge(loaded[s], loads(s))
                    for kk in range(UK):
                        for nh in range(2):
                            t = 32 * (kk * 2 + nh)
                            last = mm(ps[t:t + 32, bank, :], condT[:, q * UK + kk, :], ring[:, s, kk, nh * 512:nh * 512 + 512],
                                      q == 0, q == UQ - 1)
                    last.then_inc(freed[s], 1)

            def mod_folds(bank, c0, src):
                for m in range(4):
                    last = mm(ps[:, bank, c0 + m * 2 * NC:c0 + (m + 1) * 2 * NC], src[:, m * P:(m + 1) * P], C("fold"), True, True)
                return last

            with pe.Fori(0, L) as r:
                for j in range(3):
                    pe.wait_ge(mod_evac, r * 3 + j + 1)
                    mod_slab(j, j, lambda s: r * 16 + 16)
                    pe.drain().then_inc(mod_done, 1)
                    pe.wait_ge(mod_evac, r * 3 + j + 4)
                    pe.wait_ge(mod_added, r * 3 + j + 1)
                    mod_folds(3 + j, 0, modS[:, j, :]).then_inc(fold_done, 1)
            pe.wait_ge(mod_added, 3 + 3 * L)
            pe.wait_ge(x_copied, KC)
            pe.wait_ge(in_wr, 32)

            with pe.Fori(0, L) as l:
                pe.wait_ge(cb_loaded, l * 16 + 16)
                for ct in range(CT):
                    for r in range(2):
                        last = tr(ps[:, 4 + ct // 2, (ct % 2) * 240 + r * 120:(ct % 2) * 240 + r * 120 + 120],
                                  cbt[0:120, r, ct * P:(ct + 1) * P], 120)
                    last.then_inc(V.cb_trans, 1)
                pe.wait_ge(V.h_ready, 1)
                n = 0
                for j, cols in enumerate(([0, 4, 1, 5, 2, 6, 3, 7], range(8), range(8))):
                    for q in range(UQ):
                        s = j * UQ + q
                        pe.wait_ge(loaded[s], l * (16 * PER_LAYER[s]) + 16 * (SETUP_USES + 1))
                    for m in cols:
                        if n >= 4:
                            if n - 4 >= 8:
                                pe.wait_ge(V.proj_copied, n - 4 - 8 + 1)
                            elif n % 2 == 0:
                                pe.wait_ge(V.a_ready, (n - 4) // 2 + 1)
                            else:
                                pe.wait_ge(V.z_sig, (n - 4) // 2 + 1)
                        for k in range(KC):
                            last = mm(ps[:, n % 4, 0:T], ring[:, j * UQ + k // UK, k % UK, m * P:(m + 1) * P], hT[:, k, :],
                                      k == 0, k == KC - 1)
                            if m == cols[-1] and k % UK == UK - 1 and k < KC - 1:
                                last.then_inc(freed[j * UQ + k // UK], 1)
                            if n in (8, 16) and k == 0:
                                last.then_inc(freed[j * UQ - 1], 1)
                        last.then_inc(V.inproj_done, 1)
                        n += 1
                    if j == 1:
                        pe.wait_ge(V.a_ready, 4)
                        pe.wait_ge(V.cb_copied, 4)
                        for ct in range(CT):
                            tr(ps[0:HIST, 4, ct * P:(ct + 1) * P], fullv[:, ct, FRING - HIST:FRING], P)
                        for ct in range(CT):
                            last = tr(ps[0:NS, 5, ct * P:(ct + 1) * P], rtmp[:, ct, :], P)
                        last.then_inc(V.a_trans, 1)
                for t, bank in enumerate((3, 7, 2)):
                    t0, m = TILES[t]
                    pe.wait_ge(V.proj_copied, 16)
                    for h in range(H):
                        last = tr(ps[0:m, bank, h * P:(h + 1) * P], proj[:, 8 + h, t0:t0 + m], P)
                        if t == 0 and h == 0:
                            last.then_inc(freed[3 * UQ - 1], 1)
                    last.then_inc(V.v_trans, 1)
                pe.wait_ge(V.conv_ready, 1)
                pe.wait_ge(V.sconv_ready, 1)
                feature_sum(1, cT, CT).then_inc(V.ln_sum, 1)
                pe.wait_ge(V.rot_ready, 1)
                pe.wait_ge(V.atok_copied, 2)
                for c in range(2):
                    for h in range(H):
                        last = mm(ps[:, 4 + c, h * P:(h + 1) * P], proj[:, 4 + h, c * P:(c + 1) * P], proj[:, h, c * P:(c + 1) * P],
                                  True, True)
                    last.then_inc(V.score_done, 1)
                for h in range(H):
                    last = mm(ps[0:NS, 0, h * NS:(h + 1) * NS], proj[:, 4 + h, SEQ:T], proj[:, h, SEQ:T], True, True)
                last.then_inc(V.score_done, 1)
                mod_slab(6, 0, lambda s: l * (16 * PER_LAYER[s]) + 16 * (SETUP_USES + 2))
                pe.drain().then_inc(V.mod2_done, 1)
                pe.wait_ge(V.v_copied, 3)
                for t, bank in enumerate((2, 7, 0)):
                    if t == 2:
                        pe.wait_ge(V.sc_ready, 3)
                    t0, m = TILES[t]
                    for h in range(H):
                        last = tr(ps[0:m, bank, h * P:(h + 1) * P], proj[:, 4 + h, t0:t0 + m], P)
                    last.then_inc(V.k_trans, 1)
                for c, bank in enumerate((3, 7)):
                    pe.wait_ge(V.kd_ready, c + 1)
                    for h in range(H):
                        last = mm(ps[:, bank, h * P:(h + 1) * P], kd[:, c, h * P:(h + 1) * P], vt[:, c, h * P:(h + 1) * P], True, True)
                    last.then_inc(V.st_done, 1)
                pe.wait_ge(V.ln_sq, 1)
                feature_sum(1, lnsq, CT).then_inc(V.ln_var, 1)
                pe.wait_ge(V.mod2_evac, 1)
                mod_slab(6, 1, lambda s: l * (16 * PER_LAYER[s]) + 16 * (SETUP_USES + 2))
                pe.drain().then_inc(V.mod2_done, 1)
                pe.wait_ge(V.kd_ready, 3)
                pe.wait_ge(V.s1_copied, 1)
                pe.wait_ge(V.qd_ready, 1)

                def head_output(h):
                    bank = HEAD_BANK[h]
                    hp = slice(h * P, (h + 1) * P)
                    mm(ps[:, bank, 0:P], vt[:, 0, hp], sc[:, 0, hp], True, False)
                    mm(ps[:, bank, P:2 * P], vt[:, 1, hp], sc[:, 1, hp], False, False)
                    mm(ps[:, bank, P:2 * P], s1[:, hp], qd[:, h, 0:P], False, False)
                    mm(ps[:, bank, SEQ:T], vt[0:NS, 2, hp], scs[0:NS, h * NS:(h + 1) * NS], False, False)
                    pe.wait_ge(V.Sa_loaded if h < 2 else V.Sb_loaded, 32)
                    for b in range(B):
                        last = mm(ps[:, bank, SEQ + b * T_DEC:SEQ + (b + 1) * T_DEC], S_h[h][:, b * P:(b + 1) * P],
                                  qd[:, h, P + b * T_DEC:P + (b + 1) * T_DEC], False, b == B - 1)
                    last.then_inc(V.o_done, 1)

                def head_states(i):
                    hp = slice(STATE_ORDER[i] * P, (STATE_ORDER[i] + 1) * P)
                    pe.wait_ge(V.vmask_ready, i + 1)
                    if i >= 2:
                        pe.wait_ge(V.snew_ready, i - 1)
                    for g in range(2):
                        last = mm(ps[:, STATE_BANKS[i % 2][g], :], kd[0:NS, 2, hp], vmasks[i % 2][0:NS, g * 512:(g + 1) * 512],
                                  True, True)
                    last.then_inc(V.snew_done, 1)

                def head_sum(h):
                    pe.wait_ge(V.o_copied, h + 1)
                    mm(ps[:, SUM_BANK[h], 0:T], ones, oS[:, h, :], True, True).then_inc(V.gn_sum, 1)

                def head_squares(h):
                    pe.wait_ge(V.gn_sq, h + 1)
                    if h == 0:
                        pe.wait_ge(V.var_ready, 2)
                    elif h < 3:
                        pe.wait_ge(V.o_copied, h + 2)
                    mm(ps[:, VAR_BANK[h], 0:T], ones, gn_sq[:, h, :], True, True).then_inc(V.gn_var, 1)

                def out_block(m, ks):
                    for k in ks:
                        last = mm(ps[:, OUT_BANK[m % 4], 0:T], ring[:, k // UK, k % UK, m * P:(m + 1) * P], hT[:, k, :],
                                  k == KC // 2, k == KC // 2 - 1)
                    return last

                CONV_K, RET_K = range(KC // 2, KC), range(0, KC // 2)
                head_output(0)
                head_output(1)
                pe.wait_ge(V.sf_ready, 1)
                head_sum(0)
                head_output(2)
                head_sum(1)
                head_output(3)
                head_sum(2)
                pe.wait_ge(V.mod2_evac, 2)
                for j in range(2):
                    last = mod_folds(6, j * 128, modM[:, j, :])
                last.then_inc(V.mod2_fold, 1)
                head_sum(3)
                head_squares(0)
                head_squares(1)
                for q in range(UQ):
                    pe.wait_ge(loaded[q], l * (16 * PER_LAYER[q]) + 16 * (SETUP_USES + 3))
                pe.wait_ge(V.mix_conv, 1)
                pe.wait_ge(V.gn_centered, H)
                out_block(0, CONV_K)
                head_squares(2)
                out_block(1, CONV_K)
                head_squares(3)
                out_block(2, CONV_K)
                pe.wait_ge(V.mod2_added, 2)
                out_block(3, CONV_K)
                for m in range(4):
                    for k in RET_K:
                        if m == 0:
                            pe.wait_ge(V.gn_mixed, k + 1)
                        last = out_block(m, [k])
                    last.then_inc(V.outproj_done, 1)
                for m in range(4, KC):
                    pe.wait_ge(V.x_mid, m - 3)
                    out_block(m, CONV_K)
                    out_block(m, RET_K).then_inc(V.outproj_done, 1)
                pe.wait_ge(V.outproj_done, KC)
                for q in range(UQ):
                    pe.sem_inc(freed[q], 1)
                pe.wait_ge(V.x_mid, 5)
                feature_sum(7, sq2, KC, arrived=V.norm2_sq).then_inc(V.norm2_sum, 1)
                head_states(0)
                head_states(1)
                pe.wait_ge(V.x_mid, KC)
                mod_slab(6, 2, lambda s: l * (16 * PER_LAYER[s]) + 16 * (SETUP_USES + 2))
                pe.drain().then_inc(V.mod2_done, 1)
                pe.wait_ge(V.h2_ready, 1)
                for t, (t0, m) in enumerate(TILES):
                    for k in range(KC):
                        last = mm(ps[0:m, 4, t * E:(t + 1) * E], hT[:, k, t0:t0 + m], wr[:, k, :], k == 0, k == KC - 1)
                last.then_inc(V.logits_done, 1)
                n = 0
                pe.wait_ge(V.snew_ready, 2)
                for t, (t0, m) in enumerate(TILES):
                    for hf in range(2):
                        if n >= 4:
                            pe.wait_ge(V.h2_copied, n - 3)
                        for k in range(4):
                            last = tr(ps[0:m, n % 4, k * P:(k + 1) * P], hT[:, hf * 4 + k, t0:t0 + m], P)
                        last.then_inc(V.h2_trans, 1)
                        n += 1
                pe.wait_ge(V.h2_copied, 6)
                head_states(2)
                head_states(3)
                pe.wait_ge(V.mod2_evac, 3)
                mod_folds(7, 0, kd[:, 0, :]).then_inc(V.mod2_fold, 1)
                pe.wait_ge(V.m_ready, 1)
                M = rt[:, 10, :]
                for t in range(3):
                    for u in range(t + 1):
                        mm(ps[:, 5, t * E:(t + 1) * E], C("tri") if u == t else ones, M[:, u * E:(u + 1) * E], u == 0, u == t)
                for u in range(3):
                    last = mm(ps[:, 5, 3 * E:4 * E], ones, M[:, u * E:(u + 1) * E], u == 0, u == 2)
                last.then_inc(V.pos_done, 1)

                pe.wait_ge(V.h2_copied, 6)
                for sgn in (V.gathered, V.up_done, V.trans_done, V.down_done):
                    pe.sem_inc(sgn, 2)
                for sgn in (V.x_gath, V.x_gu, V.x_t, V.x_down):
                    pe.sem_inc(sgn, 1)

                def gather(selb, bank, free=None, n=BLK):
                    for k in range(KC):
                        for t, (t0, m) in enumerate(TILES):
                            last = mm(ps[:, bank, k * n:(k + 1) * n], h2tok[0:m, t, k * P:(k + 1) * P],
                                      selb[0:m, t * n:(t + 1) * n], t == 0, t == 2)
                            if free and k == 0 and t == 0:
                                last.then_inc(free, 1)
                    return last

                def quarter_products(bank, lhs, s, k):
                    for q in range(4):
                        last = mm(ps[q * XBLK:(q + 1) * XBLK, bank, 0:XW], lhs(k), ring[:, s, k % UK, q * XW:(q + 1) * XW],
                                  k == 0, k == KC - 1)
                    return last

                def extra_products(bank, lhs, s0, unit):
                    for k in range(KC):
                        if k % UK == 0:
                            unit(s0 + k // UK)
                        last = quarter_products(bank, lhs, s0 + k // UK, k)
                    return last

                def half_products(bank, lhs, s0, free, unit):
                    for k in range(KC):
                        s = s0 + k // UK
                        if k % UK == 0:
                            unit(s)
                        for nh in range(2):
                            last = mm(ps[nh * 64:nh * 64 + 64, bank, :], lhs(k), ring[:, s, k % UK, nh * 512:nh * 512 + 512],
                                      k == 0, k == KC - 1)
                        if free and k % UK == UK - 1 and k < KC - 1:
                            last.then_inc(freed[s], 1)
                        if free and k == 0 and s0 == UQ:
                            last.then_inc(freed[UQ - 1], 1)
                    return last

                def joint_products(bank, xbank, lhs, xlhs, s0, unit):
                    for k in range(KC):
                        s = s0 + k // UK
                        if k % UK == 0:
                            unit(s)
                        xlast = quarter_products(xbank, xlhs, s, k)
                        for nh in range(2):
                            last = mm(ps[nh * 64:nh * 64 + 64, bank, :], lhs(k), ring[:, s, k % UK, nh * 512:nh * 512 + 512],
                                      k == 0, k == KC - 1)
                        if k % UK == UK - 1 and k < KC - 1:
                            last.then_inc(freed[s], 1)
                        if k == 0 and s0 == UQ:
                            last.then_inc(freed[UQ - 1], 1)
                    return last, xlast

                def transposes(bank, src, n=4):
                    for j in range(n):
                        last = tr(ps[:, bank, j * P:(j + 1) * P], src[:, j * P:(j + 1) * P], P)
                    return last

                def down_lhs(src):
                    return lambda k: src[:, (k % 4) * P + (k // 4) * BLK:(k % 4) * P + (k // 4) * BLK + BLK]

                def extra_down(k):
                    return h2x[:, (k % 2) * P + (k // 2) * XBLK:(k % 2) * P + (k // 2) * XBLK + XBLK]

                pe.wait_ge(V.sel_ready, 1)
                gather(sel[:, 0, :], 1).then_inc(V.gathered, 1)
                pe.wait_ge(V.route_ready, 1)
                xn = pe.alloc_register("extra_blocks")
                pe.reg_mov(xn, 1)
                with pe.Fori(0, E // 2) as g:
                    for i in range(2):
                        def unit(s):
                            pe.wait_ge(loaded[s], l * (16 * PER_LAYER[s]) + g * 32 + 16 * (SETUP_USES + PRE[s] + i + 1))

                        nsub = pe.value_load(nsubi[0:1, bass.ds(g * 2 + i, 1)], min_val=1, max_val=MAXSUB)
                        xlo = pe.alloc_register(f"extra_first{i}")
                        pe.reg_mov(xlo, xn)
                        def tokens(k):
                            return xg[:, i, k * BLK:(k + 1) * BLK]

                        def extra_tokens(k):
                            return xgx[:, k * XBLK:(k + 1) * XBLK]

                        def extra_gather():
                            pe.wait_ge(V.x_hs, xn)
                            pe.reg_add(xn, xn, 1)
                            pe.wait_ge(V.x_sel, xn)
                            gather(selx, 7, n=XBLK).then_inc(V.x_gath, 1)
                            pe.wait_ge(V.x_xg, xn)

                        def extra_transposes():
                            pe.wait_ge(V.x_h, xn)
                            transposes(7, hx, 2).then_inc(V.x_t, 1)

                        def main_may_start():
                            pe.wait_ge(V.xg_copied, g * 2 + i + 1)
                            pe.wait_ge(V.h_act, g * 2 + i + 2)

                        def next_gather():
                            pe.wait_ge(V.sel_ready, g * 2 + i + 2)
                            gather(sel[:, (i + 1) % 2, :], 1, freed[2 * UQ - 1]).then_inc(V.gathered, 1)

                        def extra_down_may_start():
                            pe.wait_ge(V.x_yc, xlo)
                            pe.reg_add(xlo, xlo, 1)
                            pe.wait_ge(V.x_h2, xlo)

                        with pe.If(nsub > 1):
                            pe.wait_ge(V.x_yc, xn)
                            pe.sem_inc(tick, 1)
                            with pe.If(nsub > 2):
                                with pe.Fori(2, nsub):
                                    extra_gather()
                                    extra_products(5, extra_tokens, 0, unit)
                                    extra_products(6, extra_tokens, UQ, unit).then_inc(V.x_gu, 1)
                                    extra_transposes()
                            extra_gather()
                            main_may_start()
                            last, xlast = joint_products(2, 5, tokens, extra_tokens, 0, unit)
                            last.then_inc(V.gate_done, 1)
                            last, xlast = joint_products(3, 6, tokens, extra_tokens, UQ, unit)
                            xlast.then_inc(V.x_gu, 1)
                            last.then_inc(V.up_done, 1)
                            next_gather()
                            extra_transposes()
                        with pe.If(nsub < 2):
                            main_may_start()
                            half_products(2, tokens, 0, True, unit).then_inc(V.gate_done, 1)
                            half_products(3, tokens, UQ, True, unit).then_inc(V.up_done, 1)
                            next_gather()
                        pe.wait_ge(V.h_act, g * 2 + i + 3)
                        pe.wait_ge(V.hT_copied, g * 2 + i + 2)
                        transposes(4, hs).then_inc(V.trans_done, 1)
                        with pe.If(nsub > 1):
                            with pe.If(nsub > 2):
                                with pe.Fori(2, nsub):
                                    extra_down_may_start()
                                    extra_products(7, extra_down, 2 * UQ, unit).then_inc(V.x_down, 1)
                            extra_down_may_start()
                            pe.wait_ge(V.hT_copied, g * 2 + i + 3)
                            pe.wait_ge(V.y_copied, g * 2 + i + 2)
                            last, xlast = joint_products(0, 7, down_lhs(h2T), extra_down, 2 * UQ, unit)
                            xlast.then_inc(V.x_down, 1)
                            last.then_inc(V.down_done, 1)
                        with pe.If(nsub < 2):
                            pe.wait_ge(V.hT_copied, g * 2 + i + 3)
                            pe.wait_ge(V.y_copied, g * 2 + i + 2)
                            half_products(0, down_lhs(h2T), 2 * UQ, True, unit).then_inc(V.down_done, 1)
                        pe.wait_ge(V.down_done, g * 2 + i + 3)
                        pe.sem_inc(freed[3 * UQ - 1], 1)
                pe.wait_ge(V.comb_ready, 3)
                for k in range(KC):
                    if k >= 2:
                        pe.wait_ge(V.x_end, k - 1)
                    for t, (t0, m) in enumerate(TILES):
                        last = tr(ps[:, 2 + k % 2, t0:t0 + m], h2tok[0:m, t, k * P:(k + 1) * P], m)
                    last.then_inc(V.yt_trans, 1)
                feature_sum(6, big, KC, arrived=V.next_sq).then_inc(x_summed, 1)
                pe.drain().then_inc(layer_done, 1)
                pe.wait_ge(layer_open, l + 1)
            pe.wait_ge(fin_y, 1)
            n = 0
            for t, (t0, m) in enumerate(TILES):
                for hf in range(2):
                    if n >= 4:
                        pe.wait_ge(fin_cp, n - 3)
                    for k in range(4):
                        last = tr(ps[0:m, n % 4, k * P:(k + 1) * P], hT[:, hf * 4 + k, t0:t0 + m], P)
                    last.then_inc(fin_tr, 1)
                    n += 1

        @block.scalar
        def _(act):
            def a(out, in_, f=ACT.Copy, **kw):
                return nc.scalar.activation(out, in_, f, **kw)

            def root(buf):
                a(buf, buf, ACT.Sqrt).then_inc(V.rstd_ready, 1)

            act.dma_start(c_tok[0:1, :], c_prompt).then_inc(in_c, 16)
            act.dma_start(c_tok[1:NC, :], c_sample).then_inc(in_c, 16)
            act.dma_start(cst[:, :], consts).then_inc(in_const, 16)
            act.dma_start(x_tok[:, 0:2, :], x_prompt[0].rearrange("(r p) d -> p r d", p=P)).then_inc(in_x, 16)
            act.dma_start(x_tok[0:NS, 2, :], x_sample.rearrange("b t d -> (b t) d")).then_inc(in_x, 32)
            act.dma_start(wr[:, :, :], w_router.rearrange("(k p) e -> p k e", p=P)).then_inc(in_wr, 16)
            act.dma_start(brow[:, :], b_router.partition_broadcast(P)).then_inc(in_wr, 16)
            act.wait_ge(in_c, 32)
            a(c_sig[0:NC, :], c_tok[0:NC, :], ACT.Sigmoid).then_inc(c_sigd, 1)
            act.wait_ge(c_trans, 1)
            act.wait_ge(cpad, 1)
            a(condT[:, :, 0:NC], ps[:, 2, 0:KC * 16].rearrange("p (k c) -> p k c", k=KC)[:, :, 0:NC]).then_inc(cond_ready, 1)
            for k in range(0, KC):
                act.wait_ge(x_trans, k + 1)
                a(xT[:, k, :], ps[:, 6 + k % 2, 0:T]).then_inc(x_copied, 1)
            act.wait_ge(x_copied, KC)
            a(big[:, :, :], xT[:, :, :], ACT.Square).then_inc(x_copied, 1)
            act.sem_inc(mod_evac, 3)
            with act.Fori(0, L) as r:
                for j in range(3):
                    act.wait_ge(mod_done, r * 3 + j + 1)
                    act.wait_ge(fold_done, r * 3 + j + 1)
                    a(modS[:, j, :], ps[:, j, :]).then_inc(mod_evac, 1)
            act.wait_ge(mod_added, 3 + 3 * L)

            with act.Fori(0, L) as l:
                act.wait_ge(V.pad_ready, 1)
                for ct in range(CT):
                    act.wait_ge(V.cb_trans, ct // 2 * 2 + 2)
                    a(fullv[:, ct, FRING:].rearrange("p (b w) -> p b w", b=B)[:, :, 0:HIST],
                      ps[:, 4 + ct // 2, (ct % 2) * 240:(ct % 2) * 240 + 240].rearrange("p (b w) -> p b w", b=B)) \
                        .then_inc(V.cb_copied, 1)
                act.wait_ge(V.var_ready, 1)
                root(stat[:, 1, :])
                for i in range(4):
                    act.wait_ge(V.inproj_done, 2 * i + 2)
                    if i >= 2:
                        act.wait_ge(V.a_ready, i - 1)
                    a(zsig[:, i % 2, :], ps[:, (2 * i + 1) % 4, 0:T], ACT.Sigmoid).then_inc(V.z_sig, 1)
                for n in range(16):
                    act.wait_ge(V.inproj_done, 8 + n + 1)
                    a(proj[:, n, :], ps[:, n % 4, 0:T]).then_inc(V.proj_copied, 1)
                    if n == 11:
                        act.wait_ge(V.a_trans, 1)
                        a(atok[0:HIST, 0, :], ps[0:HIST, 4, :]).then_inc(V.atok_copied, 1)
                        a(atok[0:NS, 1, :], ps[0:NS, 5, :]).then_inc(V.atok_copied, 1)
                for t, bank in enumerate((3, 7, 2)):
                    m = TILES[t][1]
                    act.wait_ge(V.v_trans, t + 1)
                    a(vt[0:m, t, :], ps[0:m, bank, :]).then_inc(V.v_copied, 1)
                act.wait_ge(V.sconv_ready, 1)
                act.wait_ge(V.mod2_done, 1)
                a(modM[:, 0, :], ps[:, 6, :]).then_inc(V.mod2_evac, 1)
                act.wait_ge(V.inproj_done, 24)
                act.wait_ge(V.ln_centered, 1)
                a(lnsq, cT, ACT.Square).then_inc(V.ln_sq, 1)
                act.wait_ge(V.proj_copied, 16)
                a(gsig, proj[:, 12:16, :], ACT.Sigmoid).then_inc(V.g_sig, 1)
                act.wait_ge(V.st_done, 1)
                act.wait_ge(V.cb_trans, CT)
                a(s1, ps[:, 3, :]).then_inc(V.s1_copied, 1)

                def copy_head(h):
                    act.wait_ge(V.o_done, h + 1)
                    a(oS[:, h, :], ps[:, HEAD_BANK[h], 0:T]).then_inc(V.o_copied, 1)

                def square_head(h):
                    act.wait_ge(V.gn_centered, h + 1)
                    a(gn_sq[:, h, :], oS[:, h, :], ACT.Square).then_inc(V.gn_sq, 1)

                def root_head(h):
                    act.wait_ge(V.var_ready, 3 + h)
                    root(gn_rstd[:, h, :])

                act.wait_ge(V.k_trans, 3)
                act.wait_ge(V.qd_ready, 1)
                act.wait_ge(V.mod2_done, 2)
                a(modM[:, 1, :], ps[:, 6, :]).then_inc(V.mod2_evac, 1)
                act.wait_ge(V.var_ready, 2)
                root(stat[:, 1, :])
                copy_head(0)
                act.wait_ge(V.ln_scaled, 1)
                act.wait_ge(V.ln_var, 1)
                for ct in range(CT):
                    last = a(lnsq[:, ct, :], cT[:, ct, :], ACT.Sigmoid, scale=vec[:, R_GCLN + ct:R_GCLN + ct + 1],
                             bias=vec[:, R_BCLN + ct:R_BCLN + ct + 1])
                last.then_inc(V.ln_sig, 1)
                copy_head(1)
                copy_head(2)
                square_head(0)
                copy_head(3)
                square_head(1)
                square_head(2)
                square_head(3)
                for h in range(H):
                    root_head(h)
                act.wait_ge(V.gn_mixed, H)
                for k in range(KC):
                    act.wait_ge(V.x_mid, k + 1)
                    a(sq2[:, k, :], xT[:, k, :], ACT.Square).then_inc(V.norm2_sq, 1)
                act.wait_ge(V.var_ready, 3 + H)
                root(stat[:, 1, :])
                act.wait_ge(V.mod2_done, 3)
                a(kd[:, 0, :], ps[:, 6, :]).then_inc(V.mod2_evac, 1)
                act.wait_ge(V.lg_ready, 1)
                a(rt[:, 1, :], rt[:, 0, :], ACT.Exp).then_inc(V.ex_ready, 1)
                n = 0
                for t, (t0, m) in enumerate(TILES):
                    for hf in range(2):
                        act.wait_ge(V.h2_trans, n + 1)
                        a(h2tok[0:m, t, hf * 512:hf * 512 + 512], ps[0:m, n % 4, :]).then_inc(V.h2_copied, 1)
                        n += 1
                act.wait_ge(V.states_stored, 32)

                act.wait_ge(V.route_ready, 1)
                act.wait_ge(V.sf_stored, 16)
                act.sem_inc(V.y_copied, 2)
                for sgn in y_stored:
                    act.sem_inc(sgn, 16)
                for sgn in (V.x_sig, V.x_yc):
                    act.sem_inc(sgn, 1)
                act.wait_ge(V.gathered, 3)
                a(xg[:, 0, :], ps[:, 1, :]).then_inc(V.xg_copied, 1)
                xn = act.alloc_register("extra_blocks")
                act.reg_mov(xn, 1)
                x16 = act.alloc_register("extra_stored")
                act.reg_mov(x16, 0)
                with act.Fori(0, E // 2) as g:
                    for i in range(2):
                        nsub = act.value_load(nsubi[0:1, bass.ds(g * 2 + i, 1)], min_val=1, max_val=MAXSUB)
                        xlo = act.alloc_register(f"extra_first{i}")
                        act.reg_mov(xlo, xn)
                        with act.If(nsub > 1):
                            with act.Fori(1, nsub):
                                act.reg_add(xn, xn, 1)
                                act.wait_ge(V.x_gu, xn)
                                a(gsx, ps[:, 5, 0:XW], ACT.Sigmoid).then_inc(V.x_sig, 1)
                        act.wait_ge(V.gate_done, g * 2 + i + 1)
                        act.wait_ge(V.h_act, g * 2 + i + 2)
                        a(gs, ps[:, 2, :], ACT.Sigmoid).then_inc(V.sig_done, 1)
                        act.wait_ge(V.gathered, g * 2 + i + 4)
                        act.wait_ge(V.up_done, g * 2 + i + 2)
                        a(xg[:, (i + 1) % 2, :], ps[:, 1, :]).then_inc(V.xg_copied, 1)
                        with act.If(nsub > 1):
                            with act.Fori(1, nsub) as s:
                                act.reg_add(xlo, xlo, 1)
                                act.wait_ge(V.x_down, xlo)
                                a(yx, ps[:, 7, 0:XW]).then_inc(V.x_yc, 1)
                                act.wait_ge(V.x_yc, xlo)
                                row = act.snap(act.snap(xlo) * XBLK + (E * BLK - 2 * XBLK), min_val=0, max_val=YROWS - XBLK)
                                for q in range(4):
                                    act.dma_start(ydram[bass.ds(row, XBLK), q * XW:(q + 1) * XW],
                                                  yx[q * XBLK:(q + 1) * XBLK, :]).then_inc(V.x_st, 16)
                                act.reg_add(x16, x16, 64)
                                act.wait_ge(V.x_st, x16)
                                act.sem_inc(tick, 1)
                        act.wait_ge(V.down_done, g * 2 + i + 3)
                        act.wait_ge(y_stored[i], g * 32 + 16)
                        a(ysb[:, i, :], ps[:, 0, :]).then_inc(V.y_copied, 1)
                        act.wait_ge(V.y_copied, g * 2 + i + 3)
                        for hf in range(2):
                            act.dma_start(ydram[bass.ds(g * (2 * BLK) + i * BLK, BLK), hf * 512:hf * 512 + 512],
                                          ysb[hf * 64:hf * 64 + 64, i, :]).then_inc(y_stored[i], 16)
                act.wait_ge(V.comb_ready, 3)
                for k in range(KC):
                    act.wait_ge(V.x_end, k + 1)
                    a(big[:, k, :], xT[:, k, :], ACT.Square).then_inc(V.next_sq, 1)
                act.drain().then_inc(layer_done, 1)
                act.wait_ge(layer_open, l + 1)
            act.wait_ge(fin_rs, 2)
            a(stat[:, 1, :], stat[:, 1, :], ACT.Sqrt).then_inc(fin_rs, 1)
            n = 0
            for t, (t0, m) in enumerate(TILES):
                for hf in range(2):
                    act.wait_ge(fin_tr, n + 1)
                    a(x_tok[0:m, t, hf * 512:hf * 512 + 512], ps[0:m, n % 4, :]).then_inc(fin_cp, 1)
                    n += 1

        @block.vector
        def _(dve):
            v = nc.vector

            def bc(ap2, n):
                return ap2.unsqueeze(1).to_broadcast([ap2.shape[0], n, ap2.shape[1]])

            def bl(ap2, n):
                return ap2.unsqueeze(2).to_broadcast([ap2.shape[0], ap2.shape[1], n])

            v.memset(condT[:, :, :], 0.0).then_inc(cpad, 1)
            dve.wait_ge(c_sigd, 1)
            v.tensor_tensor(c_tok[0:NC, :], c_tok[0:NC, :], c_sig[0:NC, :], ALU.mult).then_inc(c_act, 1)
            dve.wait_ge(rows_trans, 1)
            v.tensor_copy(vecT[:, :, :], ps[:, 0, 0:L * P].rearrange("p (l r) -> p l r", l=L)[:, :, 0:NROWS]).then_inc(rows_copied, 1)
            v.tensor_copy(wcT[:, :, :], ps[:, 1, 0:L * P].rearrange("p (l r) -> p l r", l=L)[:, :, 0:TAPS * CT]).then_inc(rows_copied, 1)
            dve.wait_ge(rows_copied, 2)
            dve.sem_inc(mod_added, 3)
            with dve.Fori(0, L) as l:
                for j in range(3):
                    dve.wait_ge(fold_done, l * 3 + j + 4)
                    o = modT[:, bass.ds(l, 1), j * KC:(j + 1) * KC, :].rearrange("p a (n m) c -> p (a n) m c", n=2)
                    bm = vecT[:, bass.ds(l, 1), R_BMOD + j * KC:R_BMOD + (j + 1) * KC].rearrange("p a (n m) -> p (a n) m", n=2)
                    src = ps[:, 3 + j, 0:8 * NC].rearrange("p (m n c) -> p n m c", m=4, n=2)
                    v.tensor_tensor(o, src, bm.unsqueeze(3).to_broadcast([P, 2, 4, NC]), ALU.add).then_inc(mod_added, 1)
            dve.wait_ge(mod_added, 3 + 3 * L)
            dve.wait_ge(in_const, 16)
            dve.wait_ge(x_copied, KC)

            def inverse_var(ch, dst, src, n):
                ch.link(v.tensor_scalar(dst, src, 1.0 / n, EPS, ALU.mult, ALU.add))
                v.reciprocal(dst, dst).then_inc(V.var_ready, 1)

            def modulated(ch, bank, sh, sca, nth, done):
                inverse_var(ch, stat[:, 1, :], ps[:, bank, 0:T], D)
                dve.wait_ge(V.rstd_ready, nth)
                ch.link(v.tensor_tensor(hT[:, :, :], xT[:, :, :], bc(stat[:, 1, :], KC), ALU.mult))
                smp = hT[:, :, SEQ:T].rearrange("p k (b t) -> p k b t", b=B)
                ch.link(v.tensor_tensor(smp, smp, mod[:, sca:sca + KC, 1:NC].unsqueeze(3).to_broadcast([P, KC, B, T_DEC]), ALU.mult))
                v.tensor_tensor(smp, smp, mod[:, sh:sh + KC, 1:NC].unsqueeze(3).to_broadcast([P, KC, B, T_DEC]), ALU.add)
                for k in range(KC):
                    last = v.tensor_scalar(hT[:, k, 0:SEQ], hT[:, k, 0:SEQ], mod[:, sca + k, 0:1], mod[:, sh + k, 0:1],
                                           ALU.mult, ALU.add)
                last.then_inc(done, 1)

            def add_gated(ch, bank_of, gt, arrived, done):
                for m in range(KC):
                    dve.wait_ge(arrived, m + 1)
                    src = ps[:, bank_of(m), :]
                    v.tensor_tensor(rtmp[:, m, :].rearrange("p (b t) -> p b t", b=B), src[:, SEQ:T].rearrange("p (b t) -> p b t", b=B),
                                    bl(mod[:, gt + m, 1:NC], T_DEC), ALU.mult).then_inc(V.dchain, 1)
                    ch.n += 1
                    v.scalar_tensor_tensor(xT[:, m, 0:SEQ], src[:, 0:SEQ], mod[:, gt + m, 0:1], xT[:, m, 0:SEQ],
                                           ALU.mult, ALU.add)
                    dve.wait_ge(V.dchain, ch.n)
                    v.tensor_tensor(xT[:, m, SEQ:T], xT[:, m, SEQ:T], rtmp[:, m, :], ALU.add).then_inc(done, 1)

            with dve.Fori(0, L) as l:
                ch = Chain(dve, V.dchain)
                v.tensor_copy(vec[:, :], vecT[:, bass.ds(l, 1), :].rearrange("p a r -> p (a r)"))
                v.tensor_copy(wc[:, :], wcT[:, bass.ds(l, 1), :].rearrange("p a r -> p (a r)"))
                v.memset(fullv[:, :, 0:HIST], 0.0).then_inc(V.pad_ready, 1)
                ch.link(v.tensor_copy(mod[:, 0:NMB // 2, :], modT[:, bass.ds(l, 1), :, :].rearrange("p a m c -> p (a m) c")))
                def add_mod_bias(bank, c0, j):
                    o = mod[:, j * KC:(j + 1) * KC, :].rearrange("p (n m) c -> p n m c", n=2)
                    bm = vec[:, R_BMOD + j * KC:R_BMOD + (j + 1) * KC].rearrange("p (n m) -> p n m", n=2)
                    src = ps[:, bank, c0:c0 + 8 * NC].rearrange("p (m n c) -> p n m c", m=4, n=2)
                    return v.tensor_tensor(o, src, bm.unsqueeze(3).to_broadcast([P, 2, 4, NC]), ALU.add)

                def scale_to_gain(sca, gain):
                    return v.scalar_tensor_tensor(mod[:, sca:sca + KC, :], mod[:, sca:sca + KC, :], 1.0,
                                                  bl(vec[:, gain:gain + KC], NC), ALU.add, ALU.mult)

                ch.link(scale_to_gain(M_SC1, R_GMIX))
                dve.sem_inc(V.vectors_ready, 1)
                dve.wait_ge(x_summed, l + 1)
                modulated(ch, 6, M_SH1, M_SC1, 1, V.h_ready)
                for i in range(4):
                    dve.wait_ge(V.z_sig, i + 1)
                    src = ps[:, (2 * i) % 4, :]
                    dve.wait_ge(V.inproj_done, 2 * i + 1)
                    v.tensor_tensor(fullv[:, i, HIST:FRING], src[:, 0:SEQ], zsig[:, i % 2, 0:SEQ], ALU.mult)
                    v.tensor_tensor(rtmp[:, i, :], src[:, SEQ:T], zsig[:, i % 2, SEQ:T], ALU.mult)
                    v.tensor_tensor(fullv[:, i, FRING:].rearrange("p (b w) -> p b w", b=B)[:, :, HIST:],
                                    src[:, SEQ:T].rearrange("p (b t) -> p b t", b=B),
                                    zsig[:, i % 2, SEQ:T].rearrange("p (b t) -> p b t", b=B), ALU.mult).then_inc(V.a_ready, 1)
                dve.wait_ge(V.a_ready, 4)
                base = ch.n
                for tap in range(TAPS):
                    for ct in range(CT):
                        wcol = wc[:, tap * CT + ct:tap * CT + ct + 1]
                        src = fullv[:, ct, tap:tap + SEQ]
                        if tap == 0:
                            ins = v.tensor_scalar(cT[:, ct, 0:SEQ], src, wcol, vec[:, R_BCONV + ct:R_BCONV + ct + 1], ALU.mult, ALU.add)
                        else:
                            dve.wait_ge(V.dchain, ch.n - CT + 1)
                            ins = v.scalar_tensor_tensor(cT[:, ct, 0:SEQ], src, wcol, cT[:, ct, 0:SEQ], ALU.mult, ALU.add)
                        ins.then_inc(V.dchain, 1)
                        ch.n += 1
                dve.wait_ge(V.dchain, ch.n)
                dve.sem_inc(V.conv_ready, 1)
                dve.wait_ge(V.proj_copied, 8)
                for c in range(2):
                    qk = proj[:, c * H:(c + 1) * H, :]
                    v.tensor_tensor(rot[0:64, :, :], qk[64:128], bc(C("sin")[64:128], H), ALU.mult)
                    ch.link(v.tensor_tensor(rot[64:128, :, :], qk[0:64], bc(C("sin")[0:64], H), ALU.mult))
                    ch.link(v.tensor_tensor(qk, qk, bc(C("cos"), H), ALU.mult))
                    last = v.tensor_tensor(qk, qk, rot, ALU.add)
                    if c == 0:
                        ch.link(last)
                last.then_inc(V.rot_ready, 1)
                dve.wait_ge(V.rot_ready, 1)
                dve.wait_ge(rows_zeroed, 32)
                v.tensor_tensor(qd, proj[:, 0:4, P:T], C("qdec").rearrange("p (h t) -> p h t", h=H), ALU.mult).then_inc(V.qd_ready, 1)
                dve.wait_ge(V.ln_sum, 1)
                ch.link(v.tensor_scalar(stat[:, 0, :], ps[:, 1, 0:T], 1.0 / D_CONV, None, ALU.mult))
                v.tensor_tensor(cT, cT, bc(stat[:, 0, :], CT), ALU.subtract).then_inc(V.ln_centered, 1)
                dve.wait_ge(V.atok_stored, 16)
                dve.wait_ge(V.hist_stored, 16 * (1 + B))
                for c in range(2):
                    dve.wait_ge(V.score_done, c + 1)
                    v.tensor_tensor(sc[:, c, :], ps[:, 4 + c, :], C("decay"), ALU.mult).then_inc(V.sc_ready, 1)
                dve.wait_ge(V.score_done, 3)
                v.tensor_tensor(scs[0:NS, :], ps[0:NS, 0, 0:H * NS], C("sdecay")[0:NS], ALU.mult).then_inc(V.sc_ready, 1)
                for t, bank in enumerate((2, 7, 0)):
                    m = TILES[t][1]
                    dve.wait_ge(V.k_trans, t + 1)
                    v.tensor_tensor(kd[0:m, t, :].rearrange("p (h d) -> p h d", h=H), ps[0:m, bank, :].rearrange("p (h d) -> p h d", h=H),
                                    bl(C("kdec")[0:m, t * H:(t + 1) * H], P), ALU.mult).then_inc(V.kd_ready, 1)
                dve.wait_ge(V.g_sig, 1)
                for h in range(H):
                    last = v.scalar_tensor_tensor(proj[:, 12 + h, :], proj[:, 12 + h, :], vec[:, R_GRET + h:R_GRET + h + 1],
                                                  gsig[:, h, :], ALU.mult, ALU.mult)
                ch.link(last)
                dve.wait_ge(V.s1_copied, 1)
                dve.wait_ge(V.st_done, 2)
                for h in range(H):
                    hp = slice(h * P, (h + 1) * P)
                    last = v.scalar_tensor_tensor(sf[:, hp], s1[:, hp], CDEC_P[h], ps[:, 7, hp], ALU.mult, ALU.add)
                last.then_inc(V.sf_ready, 1)

                def center(h):
                    dve.wait_ge(V.gn_sum, h + 1)
                    v.scalar_tensor_tensor(oS[:, h, :], ps[:, SUM_BANK[h], 0:T], -1.0 / DH, oS[:, h, :],
                                           ALU.mult, ALU.add).then_inc(V.gn_centered, 1)

                def sample_state(i):
                    h = STATE_ORDER[i]
                    dve.wait_ge(V.snew_done, i + 1)
                    for g in range(2):
                        part = S_h[h][:, g * 512:(g + 1) * 512]
                        last = v.scalar_tensor_tensor(part, part, CDEC_S[h], ps[:, STATE_BANKS[i % 2][g], :], ALU.mult, ALU.add)
                    last.then_inc(V.snew_ready, 1)

                def head_var(h):
                    dve.wait_ge(V.gn_var, h + 1)
                    inverse_var(ch, gn_rstd[:, h, :], ps[:, VAR_BANK[h], 0:T], DH)

                def head_mix(h):
                    dve.wait_ge(V.rstd_ready, 3 + h)
                    ch.link(v.tensor_tensor(oS[:, h, :], oS[:, h, :], gn_rstd[:, h, :], ALU.mult))
                    v.tensor_tensor(hT[:, h, :], oS[:, h, :], proj[:, 12 + h, :], ALU.mult).then_inc(V.gn_mixed, 1)

                dve.wait_ge(V.ln_var, 1)
                inverse_var(ch, stat[:, 1, :], ps[:, 1, 0:T], D_CONV)
                dve.wait_ge(V.rstd_ready, 2)
                v.tensor_tensor(cT, cT, bc(stat[:, 1, :], CT), ALU.mult).then_inc(V.ln_scaled, 1)
                center(0)
                center(1)
                dve.wait_ge(V.ln_sig, 1)
                for ct in range(CT):
                    last = v.tensor_scalar(cT[:, ct, :], cT[:, ct, :], vec[:, R_GCLN + ct:R_GCLN + ct + 1],
                                           vec[:, R_BCLN + ct:R_BCLN + ct + 1], ALU.mult, ALU.add)
                ch.link(last)
                center(2)
                v.tensor_tensor(hT[:, 4:8, :], cT, lnsq, ALU.mult).then_inc(V.mix_conv, 1)
                center(3)
                dve.wait_ge(V.mod2_fold, 1)
                for j in range(2):
                    add_mod_bias(6, j * 128, 3 + j).then_inc(V.mod2_added, 1)
                head_var(0)
                head_var(1)
                head_mix(0)
                head_var(2)
                head_mix(1)
                head_var(3)
                head_mix(2)
                head_mix(3)
                dve.wait_ge(V.mod2_added, 2)
                ch.link(scale_to_gain(M_SC2, R_GFFN))
                add_gated(ch, lambda m: OUT_BANK[m % 4], M_GT1, V.outproj_done, V.x_mid)
                dve.wait_ge(V.norm2_sum, 1)
                modulated(ch, 7, M_SH2, M_SC2, 3 + H, V.h2_ready)
                sample_state(0)
                sample_state(1)

                def r3(n):
                    return rt[:, n, :].rearrange("p (t e) -> p t e", t=3)

                def r4(n):
                    return rt[:, n, :].rearrange("p (a e) -> p a e", e=EPG)

                def col(n, k=3):
                    return rt[:, n, 0:k]

                def over_e(ap, n=E):
                    return ap.unsqueeze(2).to_broadcast([P, ap.shape[1], n])

                def tt(o, x, y, op):
                    ch.link(v.tensor_tensor(o, x, y, op))

                dve.wait_ge(in_wr, 32)
                v.memset(posm[:, :, :], -1000.0)
                ch.link(v.memset(rt[:, 0, :], 0.0))
                dve.wait_ge(V.logits_done, 1)
                v.tensor_tensor(r3(0)[:, 0:2], ps[:, 4, 0:2 * E].rearrange("p (t e) -> p t e", t=2), bc(brow[:, :], 2), ALU.add)
                ch.link(v.tensor_tensor(r3(0)[0:NS, 2], ps[0:NS, 4, 2 * E:3 * E], brow[0:NS, :], ALU.add))
                ch.link(v.tensor_reduce(col(2), r3(0), AX.X, ALU.max))
                v.tensor_tensor(r3(0), r3(0), over_e(col(2)), ALU.subtract).then_inc(V.lg_ready, 1)
                dve.wait_ge(V.ex_ready, 1)
                ch.link(v.tensor_reduce(col(2), r3(1), AX.X, ALU.add))
                ch.link(v.reciprocal(col(2), col(2)))
                tt(r3(1), r3(1), over_e(col(2)), ALU.mult)
                pv = r4(1)
                hi, lo = rt[:, 3, 0:24].rearrange("p (a e) -> p a e", e=2), rt[:, 3, 24:48].rearrange("p (a e) -> p a e", e=2)
                v.tensor_tensor(hi, pv[:, :, 0:2], pv[:, :, 2:4], ALU.max)
                ch.link(v.tensor_tensor(lo, pv[:, :, 0:2], pv[:, :, 2:4], ALU.min))
                t1, t2, t3 = (rt[:, 4, k * 12:(k + 1) * 12] for k in range(3))
                v.tensor_tensor(t1, hi[:, :, 0], hi[:, :, 1], ALU.max)
                v.tensor_tensor(t2, hi[:, :, 0], hi[:, :, 1], ALU.min)
                ch.link(v.tensor_tensor(t3, lo[:, :, 0], lo[:, :, 1], ALU.max))
                tt(t2, t2, t3, ALU.max)
                tt(t1, t1, t2, ALU.add)
                gsc = t1.rearrange("p (t g) -> p t g", t=3)
                gm = rt[:, 5, 0:12].rearrange("p (t g) -> p t g", t=3)

                def first_of(score, key, onehot, width):
                    ch.link(v.tensor_reduce(col(2), score, AX.X, ALU.max))
                    tt(onehot, score, over_e(col(2), width), ALU.is_equal)
                    tt(onehot, onehot, bc(key, 3), ALU.mult)
                    ch.link(v.tensor_reduce(col(6), onehot, AX.X, ALU.max))
                    tt(onehot, onehot, over_e(col(6), width), ALU.is_equal)

                first_of(gsc, C("gkey"), gm, GROUPS)
                gme = rt[:, 5, 0:12].unsqueeze(2).to_broadcast([P, 12, EPG])
                tt(r4(7), pv, gme, ALU.mult)
                ch.link(v.tensor_scalar(rt[:, 5, 12:24], rt[:, 5, 0:12], -1.0, None, ALU.add))
                tt(r4(7), r4(7), rt[:, 5, 12:24].unsqueeze(2).to_broadcast([P, 12, EPG]), ALU.add)
                first_of(r3(7), C("ekey"), r3(8), E)
                ch.link(v.tensor_copy(col(11), col(2)))
                ch.link(v.scalar_tensor_tensor(rt[:, 7, :], rt[:, 8, :], -4.0, rt[:, 7, :], ALU.mult, ALU.add))
                first_of(r3(7), C("ekey"), r3(9), E)
                tt(col(12), col(11), col(2), ALU.add)
                ch.link(v.reciprocal(col(12), col(12)))
                v.tensor_tensor(wts[:, 0, :], col(11), col(12), ALU.mult)
                v.tensor_tensor(wts[:, 1, :], col(2), col(12), ALU.mult)
                tt(r3(10), r3(8), r3(9), ALU.add)
                v.tensor_tensor(r3(10), r3(10), over_e(C("valid")), ALU.mult).then_inc(V.m_ready, 1)
                sample_state(2)
                sample_state(3)
                dve.wait_ge(V.pos_done, 1)
                dve.wait_ge(V.m_ready, 1)
                ch.link(v.tensor_copy(rt[:, 13, :], ps[:, 5, 0:3 * E]))
                ch.link(v.tensor_copy(rt[:, 14, 0:E], ps[:, 5, 3 * E:4 * E]))
                ch.link(v.scalar_tensor_tensor(r3(3), r3(13), 1000.0, r3(10), ALU.add, ALU.mult))
                ch.link(v.tensor_scalar(posm[:, :, 0:E], r3(3), -1000.0, None, ALU.add))

                def select(dst, pos, n=BLK):
                    for t in range(3):
                        last = v.tensor_scalar(dst[:, t * n:(t + 1) * n], C("iota")[:, 0:n], pos(t), None, ALU.is_equal)
                    return last

                select(sel[:, 0, :], lambda t: posm[:, t, 0:1]).then_inc(V.sel_ready, 1)
                cnt, acc, xs, xt = rt[:, 14, 0:E], rt[:, 14, E:2 * E], rt[:, 14, 2 * E:3 * E], rt[:, 12, 0:E]
                ch.link(v.tensor_scalar(acc, cnt, float(BLK), 1.0, ALU.is_gt, ALU.add))
                for s in range(1, MAXSUB - 1):
                    ch.link(v.scalar_tensor_tensor(acc, cnt, float(BLK + s * XBLK), acc, ALU.is_gt, ALU.add))
                v.tensor_copy(nsubi[:, :], acc)
                ch.link(v.tensor_scalar(xs, acc, -1.0, None, ALU.add))
                for s in (1, 2, 4, 8):
                    ch.link(v.tensor_copy(xt, xs))
                    tt(xs[:, s:], xt[:, s:], xt[:, :E - s], ALU.add)
                ch.link(v.scalar_tensor_tensor(xs, acc, -1.0, xs, ALU.mult, ALU.add))
                ch.link(v.tensor_scalar(xs, xs, 1.0, float(XBLK), ALU.add, ALU.mult))
                tt(xs, xs, C("xrow"), ALU.add)
                ch.link(v.tensor_scalar(r3(3), r3(13), BLK - 0.5, None, ALU.is_gt))
                tt(r3(3), r3(3), bc(xs, 3), ALU.mult)
                tt(r3(13), r3(13), bc(C("erow"), 3), ALU.add)
                tt(r3(13), r3(13), r3(3), ALU.add)
                for k in range(2):
                    tt(r3(3), r3(13), r3(8 + k), ALU.mult)
                    ch.link(v.tensor_reduce(col(15), r3(3), AX.X, ALU.add))
                    last = v.tensor_copy(rowi[:, k, :], col(15))
                    if k == 0:
                        ch.link(last)
                ch.link(last)
                dve.wait_ge(V.mod2_fold, 2)
                add_mod_bias(7, 0, 5).then_inc(V.route_ready, 1)
                dve.wait_ge(V.route_ready, 1)

                dve.wait_ge(V.states_stored, 32)
                for sgn in (V.h_act, V.hT_copied):
                    dve.sem_inc(sgn, 2)
                for sgn in (V.x_sel, V.x_xg, V.x_gated, V.x_h, V.x_hs, V.x_h2):
                    dve.sem_inc(sgn, 1)

                xn = dve.alloc_register("extra_blocks")
                dve.reg_mov(xn, 1)
                with dve.Fori(0, E // 2) as g:
                    for i in range(2):
                        dve.wait_ge(V.gathered, g * 2 + i + 2)
                        select(sel[:, (i + 1) % 2, :], lambda t: posm[:, t, bass.ds(g * 2 + i + 1, 1)]).then_inc(V.sel_ready, 1)
                        nsub = dve.value_load(nsubi[0:1, bass.ds(g * 2 + i, 1)], min_val=1, max_val=MAXSUB)
                        xlo = dve.alloc_register(f"extra_first{i}")
                        dve.reg_mov(xlo, xn)
                        with dve.If(nsub > 1):
                            v.tensor_scalar(posx[:, :].unsqueeze(2), posm[:, :, bass.ds(g * 2 + i, 1)], float(XBLK - BLK), None,
                                            ALU.add).then_inc(V.pchain, 1)
                            dve.drain()
                            with dve.Fori(1, nsub) as s:
                                dve.reg_add(xn, xn, 1)
                                v.tensor_scalar(posx[:, :], posx[:, :], -float(XBLK), None, ALU.add)
                                dve.drain()
                                select(selx, lambda t: posx[:, t:t + 1], XBLK).then_inc(V.x_sel, 1)
                                dve.wait_ge(V.x_gath, xn)
                                v.tensor_copy(xgx, ps[:, 7, 0:XW]).then_inc(V.x_xg, 1)
                                dve.wait_ge(V.x_sig, xn)
                                v.tensor_tensor(hx, ps[:, 5, 0:XW], gsx, ALU.mult).then_inc(V.x_gated, 1)
                                dve.wait_ge(V.x_gated, xn)
                                v.tensor_tensor(hx, ps[:, 6, 0:XW], hx, ALU.mult).then_inc(V.x_h, 1)
                                dve.wait_ge(V.x_t, xn)
                                v.tensor_copy(hxs[:, bass.ds(s * XW - XW, XW)], ps[:, 7, 0:XW]).then_inc(V.x_hs, 1)
                            dve.wait_ge(V.x_hs, xn)
                            dve.sem_inc(tick, 1)
                        dve.wait_ge(V.sig_done, g * 2 + i + 1)
                        dve.wait_ge(V.trans_done, g * 2 + i + 2)
                        v.tensor_tensor(hs, ps[:, 2, :], gs, ALU.mult).then_inc(V.gated, 1)
                        dve.wait_ge(V.gated, g * 2 + i + 1)
                        dve.wait_ge(V.up_done, g * 2 + i + 3)
                        v.tensor_tensor(hs, ps[:, 3, :], hs, ALU.mult).then_inc(V.h_act, 1)
                        dve.wait_ge(V.trans_done, g * 2 + i + 3)
                        dve.wait_ge(V.down_done, g * 2 + i + 2)
                        v.tensor_copy(h2T, ps[:, 4, :]).then_inc(V.hT_copied, 1)
                        with dve.If(nsub > 1):
                            with dve.Fori(1, nsub) as s:
                                dve.wait_ge(V.x_down, xlo)
                                dve.reg_add(xlo, xlo, 1)
                                v.tensor_copy(h2x, hxs[:, bass.ds(s * XW - XW, XW)]).then_inc(V.x_h2, 1)
                for t, (t0, m) in enumerate(TILES):
                    dve.wait_ge(row_gathers[t], 32)
                    ch.link(v.tensor_scalar(h2tok[0:m, t, :], rows[t][0:m, 0, :], wts[0:m, 0, t:t + 1], None, ALU.mult))
                    v.scalar_tensor_tensor(h2tok[0:m, t, :], rows[t][0:m, 1, :], wts[0:m, 1, t:t + 1], h2tok[0:m, t, :],
                                           ALU.mult, ALU.add).then_inc(V.comb_ready, 1)
                add_gated(ch, lambda m: 2 + m % 2, M_GT2, V.yt_trans, V.x_end)
                dve.drain().then_inc(layer_done, 1)
                dve.wait_ge(layer_open, l + 1)
            dve.wait_ge(x_summed, L + 1)
            v.tensor_scalar(stat[:, 1, :], ps[:, 6, 0:T], 1.0 / D, EPS, ALU.mult, ALU.add).then_inc(fin_rs, 1)
            dve.wait_ge(fin_rs, 1)
            v.reciprocal(stat[:, 1, :], stat[:, 1, :]).then_inc(fin_rs, 1)
            dve.wait_ge(fin_rs, 3)
            for k in range(KC):
                last = v.scalar_tensor_tensor(hT[:, k, :], xT[:, k, :], vecT[:, 0, R_GFIN + k:R_GFIN + k + 1], stat[:, 1, :],
                                              ALU.mult, ALU.mult)
            last.then_inc(fin_y, 1)

        @block.gpsimd
        def _(pool):
            gp = nc.gpsimd

            zeros = qd.rearrange("p h t -> p (h t)")[:, 0:512]
            gp.memset(zeros, 0.0).then_inc(zeros_set, 1)
            hist_v = state_conv.rearrange("l b t c -> l (b t) c").rearrange("l (r p) c -> l p r c", p=120)
            pool.dma_start(cbt[0:120, :, :], hist_v[0]).then_inc(cb_loaded, 16)
            pool.sem_inc(rows_read, 1)
            next_layer = pool.alloc_register("next_layer")
            pool.reg_mov(next_layer, 0)
            pool.wait_ge(mod_added, 3 + 3 * L)
            pool.wait_ge(zeros_set, 1)
            for k in range(2):
                r0 = E * BLK + k * (XROWS // 2)
                pool.dma_start(ydram[r0:r0 + XROWS // 2, :].rearrange("(p r) (a d) -> p (r a) d", p=P, d=512),
                               zeros.unsqueeze(1).to_broadcast([P, XROWS // 2 * D // P // 512, 512])).then_inc(rows_zeroed, 16)
            pool.wait_ge(x_summed, 1)
            with pool.Fori(0, L) as l:
                pool.dma_start(conv_s[bass.ds(l, 1), :, 0:HIST - T_DEC, :].rearrange("a b t c -> (a b) (t c)"),
                               state_conv[bass.ds(l, 1), :, T_DEC:HIST, :].rearrange("a b t c -> (a b) (t c)")).then_inc(V.hist_stored, 16)
                ret_v = state_ret.rearrange("l b h d e -> l h d b e")
                rets_v = ret_s.rearrange("l b h d e -> l h d b e")

                def state(h):
                    return S_h[h].rearrange("p (b e) -> p b e", b=B)

                def dstate(v5, h):
                    return v5[bass.ds(l, 1), h].rearrange("a d b e -> (a d) b e")

                for h in (0, 1):
                    pool.dma_start(state(h), dstate(ret_v, h)).then_inc(V.Sa_loaded, 16)
                pool.wait_ge(V.vectors_ready, 1)
                pool.wait_ge(V.cb_copied, CT)
                pool.wait_ge(V.a_ready, CT)
                pc = Chain(pool, V.pchain)
                win = fullv[:, :, FRING:].rearrange("p c (b w) -> p c b w", b=B)
                slot = cprod.rearrange("p (k c s) -> p k c s", k=8, c=CT)
                flat = cprod.rearrange("p (k w) -> p k w", k=8)
                csum = cpsum.rearrange("p (c s) -> p c s", c=CT)
                for rnd in range(4):
                    for k in range(8):
                        tap = rnd * 8 + k
                        if tap < TAPS:
                            last = gp.tensor_tensor(slot[:, k].rearrange("p c (b t) -> p c b t", b=B), win[:, :, :, tap:tap + T_DEC],
                                                    wc[:, tap * CT:(tap + 1) * CT].unsqueeze(2).unsqueeze(3)
                                                    .to_broadcast([P, CT, B, T_DEC]), ALU.mult)
                        else:
                            last = gp.tensor_copy(slot[:, k], vec[:, R_BCONV:R_BCONV + CT].unsqueeze(2).to_broadcast([P, CT, NS]))
                    pc.link(last)
                    for half in (4, 2, 1):
                        if half == 1 and rnd == 0:
                            pc.link(gp.tensor_tensor(csum, slot[:, 0], slot[:, 1], ALU.add))
                        else:
                            pc.link(gp.tensor_tensor(flat[:, 0:half], flat[:, 0:half], flat[:, half:2 * half], ALU.add))
                    if rnd in (1, 2):
                        pc.link(gp.tensor_tensor(csum, csum, slot[:, 0], ALU.add))
                gp.tensor_tensor(cT[:, :, SEQ:T], csum, slot[:, 0], ALU.add).then_inc(V.sconv_ready, 1)
                pool.wait_ge(V.atok_copied, 2)
                pool.dma_start(conv_p[bass.ds(l, 1), 0].rearrange("a t c -> (a t) c"), atok[0:HIST, 0, :]).then_inc(V.atok_stored, 16)
                for b in range(B):
                    pool.dma_start(conv_s[bass.ds(l, 1), b, HIST - T_DEC:HIST, :].rearrange("a t c -> (a t) c"),
                                   atok[b * T_DEC:(b + 1) * T_DEC, 1, :]).then_inc(V.hist_stored, 16)
                pool.wait_ge(V.a_trans, 1)
                pool.wait_ge(V.sconv_ready, 1)
                pool.wait_ge(V.conv_ready, 1)
                for h in (2, 3):
                    pool.dma_start(state(h), dstate(ret_v, h)).then_inc(V.Sb_loaded, 16)
                pool.wait_ge(V.v_copied, 3)
                pool.wait_ge(V.sf_ready, 1)
                pool.dma_start(ret_p[bass.ds(l, 1), 0].rearrange("a h d e -> (a d) h e"),
                               sf.rearrange("p (h e) -> p h e", h=H)).then_inc(V.sf_stored, 16)
                pool.wait_ge(V.mod2_fold, 1)
                pool.wait_ge(V.o_done, H)
                for i, h in enumerate(STATE_ORDER):
                    if i >= 2:
                        pool.wait_ge(V.snew_done, i - 1)
                    gp.tensor_tensor(vmasks[i % 2][0:NS, :].rearrange("p (b e) -> p b e", b=B),
                                     vt[0:NS, 2, h * P:(h + 1) * P].unsqueeze(1).to_broadcast([NS, B, DH]),
                                     C("smask")[0:NS].unsqueeze(2).to_broadcast([NS, B, DH]), ALU.mult).then_inc(V.vmask_ready, 1)
                for i, h in enumerate(STATE_ORDER):
                    pool.wait_ge(V.snew_ready, i + 1)
                    pool.dma_start(dstate(rets_v, h), state(h)).then_inc(V.states_stored if i < 2 else V.Sa_stored, 16)
                pool.wait_ge(V.sf_stored, 16)
                with pool.If(l < L - 1):
                    pool.reg_add(next_layer, next_layer, 1)
                    nxt = pool.snap(pool.snap(next_layer) + 0, min_val=1, max_val=L - 1)
                    pool.dma_start(cbt[0:120, :, :], hist_v[bass.ds(nxt, 1)].rearrange("a p r c -> (a p) r c")).then_inc(cb_loaded, 16)
                pool.wait_ge(V.route_ready, 1)
                pool.wait_ge(V.y_copied, E + 2)
                pool.wait_ge(V.down_done, E + 2)
                for i in range(2):
                    pool.wait_ge(y_stored[i], 32 * (E // 2) + 16)
                pool.wait_ge(V.Sa_stored, 32)
                pool.wait_ge(V.gathered, E + 3)
                pool.wait_ge(V.xg_copied, E + 1)
                for t, (t0, m) in enumerate(TILES):
                    for k in range(2):
                        gp.indirect_dma_start(rows[t][0:m, k, :], None, ydram[:, :],
                                              bass.IndirectOffsetOnAxis(ap=rowi[0:m, k, t:t + 1], axis=0)) \
                            .then_inc(row_gathers[t], 16)
                for sgn in row_gathers:
                    pool.wait_ge(sgn, 32)
                pool.sem_inc(rows_read, 1)
                pool.wait_ge(V.x_end, KC)
                pool.wait_ge(layer_done, 3)
                pool.drain()
                pool.dma_reset(layer_sems)
                pool.sem_clear(layer_sems)
                pool.drain().then_inc(layer_open, 1)


_INS = ['x_prompt', 'x_sample', 'state_ret', 'state_conv', 'c_prompt', 'c_sample', 'w_mod', 'b_mod', 'g_mix_norm', 'w_in',
        'w_conv', 'b_conv', 'g_conv_ln', 'b_conv_ln', 'g_ret_gn', 'w_out', 'g_ffn_norm', 'w_router', 'b_router',
        'w_exp_gate', 'w_exp_up', 'w_exp_down', 'g_final']
_OUTS = [(1, SEQ, D), (B, T_DEC, D), (L, 1, H, DH, DH), (L, 1, HIST, D_CONV), (L, B, H, DH, DH), (L, B, HIST, D_CONV)]


def kernel(**inputs):
    import concourse.bacc as bacc
    from concourse.bass_utils import run_bass_kernel_spmd

    nc = bacc.Bacc("TRN2", target_bir_lowering=False, num_devices=1)
    arrays = {name: np.ascontiguousarray(inputs[name]) for name in _INS}
    arrays["consts"] = constants()
    args = [nc.dram_tensor(f"in_{n}", a.shape, mybir.dt.from_np(a.dtype), kind="ExternalInput").ap() for n, a in arrays.items()]
    args += [nc.dram_tensor(f"out_{i}", s, mybir.dt.float32, kind="ExternalOutput").ap() for i, s in enumerate(_OUTS)]
    hybrid_step_kernel(nc, *args)
    r = run_bass_kernel_spmd(nc, [{f"in_{n}": a for n, a in arrays.items()}], core_ids=[0])
    return tuple(r.results[0][f"out_{i}"] for i in range(len(_OUTS)))
```
